# Optimizing a Trainium2 kernel written in Bass

```python
import jax, jax.numpy as jnp
from jax import lax
import numpy as np

D_MODEL = 1024
BATCH = 1
SEQ = 256
DEPTH = 1

PLE_DIM = 256
FOX_HEADS = 8
FOX_HEAD_DIM = 64
Q_BLOCK = 128
RET_HEADS = 4
RET_KEY_DIM = 64
RET_VAL_DIM = 128
RET_CHUNK = 128
ROPE_BASE = 10000.0
N_BRANCHES = 2
BRANCH_WIDTH = 512
N_EXPERTS = 32
TOP_K = 4
EXPERT_FF = 1024
SWIGLU_LIMIT = 7.0
SWIGLU_ALPHA = 1.702
MOE_BLOCK = 128
EPS = 1e-6

FOX_W = FOX_HEADS * FOX_HEAD_DIM
RET_QK_W = RET_HEADS * RET_KEY_DIM
RET_V_W = RET_HEADS * RET_VAL_DIM
IN_SPLITS = list(np.cumsum([FOX_W, FOX_W, FOX_W, FOX_HEADS, RET_QK_W, RET_QK_W, RET_V_W]))
IN_WIDTH = 3 * FOX_W + FOX_HEADS + 2 * RET_QK_W + 2 * RET_V_W

kernel_name = "fox_retnet_gated_moe_ple_block"

def rms_norm(x, g):
    x32 = x.astype(jnp.float32)
    y = x32 * lax.rsqrt(jnp.mean(x32 * x32, axis=-1, keepdims=True) + EPS)
    return (y * g.astype(jnp.float32)).astype(x.dtype)

def rotary(x, pos):
    half = x.shape[-1] // 2
    inv = ROPE_BASE ** (-jnp.arange(half, dtype=jnp.float32) / half)
    ang = pos.astype(jnp.float32)[:, None] * inv[None, :]
    cos = jnp.cos(ang)[None, :, None, :]
    sin = jnp.sin(ang)[None, :, None, :]
    x32 = x.astype(jnp.float32)
    x1, x2 = x32[..., :half], x32[..., half:]
    return jnp.concatenate([x1 * cos - x2 * sin, x2 * cos + x1 * sin], axis=-1).astype(x.dtype)

def fox_attention(q, k, v, log_f):
    B, S, H, d = q.shape
    scale = d ** -0.5
    qh = q.transpose(0, 2, 1, 3)
    kh = k.transpose(0, 2, 1, 3)
    vh = v.transpose(0, 2, 1, 3)
    c = jnp.cumsum(log_f, axis=1).transpose(0, 2, 1)
    outs = []
    for blk in range(S // Q_BLOCK):
        q0, q1 = blk * Q_BLOCK, (blk + 1) * Q_BLOCK
        qb, kb, vb = qh[:, :, q0:q1], kh[:, :, :q1], vh[:, :, :q1]
        logits = (jnp.einsum('bhqd,bhkd->bhqk', qb, kb).astype(jnp.float32) * scale
                  + c[:, :, q0:q1, None] - c[:, :, None, :q1])
        qpos = jnp.arange(q0, q1)
        kpos = jnp.arange(q1)
        logits = jnp.where(kpos[None, :] <= qpos[:, None], logits, -jnp.inf)
        probs = jax.nn.softmax(logits, axis=-1).astype(vb.dtype)
        outs.append(jnp.einsum('bhqk,bhkd->bhqd', probs, vb))
    o = jnp.concatenate(outs, axis=2)
    return o.transpose(0, 2, 1, 3).reshape(B, S, H * d)

def retention(q, k, v):
    B, S, H, dk = q.shape
    dv = v.shape[-1]
    C = RET_CHUNK
    NC = S // C
    lg = jnp.log1p(-jnp.exp2(-5.0 - jnp.arange(H, dtype=jnp.float32)))
    i = jnp.arange(C, dtype=jnp.float32)
    diff = i[:, None] - i[None, :]
    inner_decay = jnp.where(diff >= 0, jnp.exp(jnp.maximum(diff, 0.0)[None] * lg[:, None, None]), 0.0)
    q_decay = jnp.exp((i + 1.0)[None, :] * lg[:, None])
    k_decay = jnp.exp((C - 1.0 - i)[None, :] * lg[:, None])
    chunk_decay = jnp.exp(C * lg)

    def to_chunks(t):
        return t.reshape(B, NC, C, H, t.shape[-1]).transpose(1, 0, 3, 2, 4)

    def step(state, inp):
        qi, ki, vi = inp
        qi32, ki32, vi32 = qi.astype(jnp.float32), ki.astype(jnp.float32), vi.astype(jnp.float32)
        scores = jnp.einsum('bhid,bhjd->bhij', qi32, ki32) * inner_decay[None]
        o_intra = jnp.einsum('bhij,bhjv->bhiv', scores, vi32)
        o_inter = jnp.einsum('bhid,bhdv->bhiv', qi32, state) * q_decay[None, :, :, None]
        new_state = (state * chunk_decay[None, :, None, None]
                     + jnp.einsum('bhjd,bhjv->bhdv', ki32 * k_decay[None, :, :, None], vi32))
        return new_state, o_intra + o_inter

    init = jnp.zeros((B, H, dk, dv), jnp.float32)
    _, oc = lax.scan(step, init, (to_chunks(q), to_chunks(k), to_chunks(v)))
    return oc.transpose(1, 0, 3, 2, 4).reshape(B, S, H, dv)

def mixer_block(h, mix_norm, w_in, b_forget, w_branch, w_merge_gate, b_merge_gate, w_out):
    B, S, D = h.shape
    xn = rms_norm(h, mix_norm)
    u = xn @ w_in
    fq, fk, fv, ff, rq, rk, rv, rg = jnp.split(u, IN_SPLITS, axis=-1)
    log_f = jax.nn.log_sigmoid((ff + b_forget).astype(jnp.float32))
    fox = fox_attention(fq.reshape(B, S, FOX_HEADS, FOX_HEAD_DIM),
                        fk.reshape(B, S, FOX_HEADS, FOX_HEAD_DIM),
                        fv.reshape(B, S, FOX_HEADS, FOX_HEAD_DIM), log_f)
    pos = jnp.arange(S)
    rq = rotary(rq.reshape(B, S, RET_HEADS, RET_KEY_DIM), pos)
    rk = rotary(rk.reshape(B, S, RET_HEADS, RET_KEY_DIM), pos) * (RET_KEY_DIM ** -0.5)
    ro = retention(rq, rk, rv.reshape(B, S, RET_HEADS, RET_VAL_DIM))
    ro = ro * lax.rsqrt(jnp.mean(ro * ro, axis=-1, keepdims=True) + EPS)
    ro = ro.reshape(B, S, RET_V_W).astype(h.dtype) * jax.nn.silu(rg)
    branches = jnp.stack([fox, ro], axis=2)
    proj = jnp.einsum('bsgc,gcd->bsgd', branches, w_branch)
    gates = jax.nn.sigmoid(xn @ w_merge_gate + b_merge_gate).reshape(B, S, N_BRANCHES, D)
    merged = jnp.sum(gates * proj, axis=2)
    return merged @ w_out

def moe_block(hn, w_router, b_router, w_gate_up, b_gate_up, w_down, b_down):
    B, S, D = hn.shape
    N = B * S
    A = N * TOP_K
    xf = hn.reshape(N, D)
    logits = (xf @ w_router + b_router).astype(jnp.float32)
    top_val, top_idx = lax.top_k(logits, TOP_K)
    top_w = jax.nn.softmax(top_val, axis=-1)
    flat_e = top_idx.reshape(A).astype(jnp.int32)
    flat_w = top_w.reshape(A)
    flat_tok = jnp.arange(A, dtype=jnp.int32) // TOP_K
    order = jnp.argsort(flat_e, stable=True)
    sorted_e, sorted_tok, sorted_w = flat_e[order], flat_tok[order], flat_w[order]
    counts = jnp.bincount(flat_e, length=N_EXPERTS)
    group_start = jnp.cumsum(counts) - counts
    padded = (counts + MOE_BLOCK - 1) // MOE_BLOCK * MOE_BLOCK
    pad_end = jnp.cumsum(padded)
    pad_start = pad_end - padded
    dest = pad_start[sorted_e] + jnp.arange(A, dtype=jnp.int32) - group_start[sorted_e]
    n_blocks = -(-(A + N_EXPERTS * (MOE_BLOCK - 1)) // MOE_BLOCK)
    P = n_blocks * MOE_BLOCK
    buf_tok = jnp.full((P,), N, jnp.int32).at[dest].set(sorted_tok)
    buf_w = jnp.zeros((P,), jnp.float32).at[dest].set(sorted_w)
    x_pad = jnp.concatenate([xf, jnp.zeros((1, D), xf.dtype)], axis=0)
    x_buf = x_pad[buf_tok].reshape(n_blocks, MOE_BLOCK, D)
    block_start = jnp.arange(n_blocks, dtype=jnp.int32) * MOE_BLOCK
    block_e = jnp.minimum(jnp.sum(block_start[:, None] >= pad_end[None, :], axis=1), N_EXPERTS - 1)

    def expert_block(args):
        xb, e = args
        gu = xb @ w_gate_up[e] + b_gate_up[e]
        glu = jnp.minimum(gu[:, ::2], SWIGLU_LIMIT)
        lin = jnp.clip(gu[:, 1::2], -SWIGLU_LIMIT, SWIGLU_LIMIT)
        act = glu * jax.nn.sigmoid(SWIGLU_ALPHA * glu) * (lin + 1.0)
        return act @ w_down[e] + b_down[e]

    y_buf = lax.map(expert_block, (x_buf, block_e)).reshape(P, D)
    y = y_buf * buf_w[:, None].astype(y_buf.dtype)
    out = jax.ops.segment_sum(y, buf_tok, num_segments=N + 1)[:N]
    return out.reshape(B, S, D)

def setup_inputs(seed: int = 0) -> dict:
    key = jax.random.key(seed)
    ks = jax.random.split(key, 20)
    f32 = jnp.float32
    L, D = DEPTH, D_MODEL

    def nrm(k, shape, fan_in):
        return jax.random.normal(k, shape, f32) * (fan_in ** -0.5)

    def gain(k, shape):
        return 1.0 + 0.01 * jax.random.normal(k, shape, f32)

    return {
        "x": jax.random.normal(ks[0], (BATCH, SEQ, D), f32),
        "p": jax.random.normal(ks[1], (L, BATCH, SEQ, PLE_DIM), f32),
        "mix_norm": gain(ks[2], (L, D)),
        "w_in": nrm(ks[3], (L, D, IN_WIDTH), D),
        "b_forget": jax.random.uniform(ks[4], (L, FOX_HEADS), f32, minval=1.0, maxval=5.0),
        "w_branch": nrm(ks[5], (L, N_BRANCHES, BRANCH_WIDTH, D), BRANCH_WIDTH),
        "w_merge_gate": nrm(ks[6], (L, D, N_BRANCHES * D), D),
        "b_merge_gate": 0.01 * jax.random.normal(ks[7], (L, N_BRANCHES * D), f32),
        "w_out": nrm(ks[8], (L, D, D), D),
        "ffn_norm": gain(ks[9], (L, D)),
        "w_router": nrm(ks[10], (L, D, N_EXPERTS), D),
        "b_router": 0.01 * jax.random.normal(ks[11], (L, N_EXPERTS), f32),
        "w_gate_up": nrm(ks[12], (L, N_EXPERTS, D, 2 * EXPERT_FF), D),
        "b_gate_up": 0.01 * jax.random.normal(ks[13], (L, N_EXPERTS, 2 * EXPERT_FF), f32),
        "w_down": nrm(ks[14], (L, N_EXPERTS, EXPERT_FF, D), EXPERT_FF),
        "b_down": 0.01 * jax.random.normal(ks[15], (L, N_EXPERTS, D), f32),
        "ple_norm": gain(ks[16], (L, D)),
        "w_ple_gate": nrm(ks[17], (L, D, D), D),
        "w_ple_proj": nrm(ks[18], (L, PLE_DIM, D), PLE_DIM),
        "final_norm": gain(ks[19], (D,)),
    }

def reference(x, p, mix_norm, w_in, b_forget, w_branch, w_merge_gate, b_merge_gate, w_out,
              ffn_norm, w_router, b_router, w_gate_up, b_gate_up, w_down, b_down,
              ple_norm, w_ple_gate, w_ple_proj, final_norm):
    h = x
    for i in range(DEPTH):
        h = h + mixer_block(h, mix_norm[i], w_in[i], b_forget[i], w_branch[i],
                            w_merge_gate[i], b_merge_gate[i], w_out[i])
        h = h + moe_block(rms_norm(h, ffn_norm[i]), w_router[i], b_router[i],
                          w_gate_up[i], b_gate_up[i], w_down[i], b_down[i])
        ple_gate = jax.nn.sigmoid(rms_norm(h, ple_norm[i]) @ w_ple_gate[i])
        h = h + ple_gate * (p[i] @ w_ple_proj[i])
    return rms_norm(h, final_norm)


_drawn_inputs = setup_inputs


def setup_inputs(seed=0):
    import zlib

    import numpy as np

    out = dict(_drawn_inputs(seed))
    spreads = {}
    factors = {'mix_norm': 3.016,
     'b_merge_gate': 8.0,
     'b_gate_up': 8.0,
     'b_down': 24.652,
     'ple_norm': 64.0,
     'final_norm': 32.417,
     'ffn_norm': 3.678,
     'b_router': 4.076}
    for name, (base, spread) in spreads.items():
        noise = np.random.default_rng([zlib.crc32(name.encode()), seed]).standard_normal(out[name].shape)
        drawn = base * np.exp(spread * noise) if base else spread * noise
        out[name] = __import__('jax').numpy.asarray(drawn.astype(out[name].dtype))
    for name, factor in factors.items():
        out[name] = (out[name] * factor).astype(out[name].dtype)
    return out
```

```python
import concourse.bass as bass
from concourse import mybir
from contextlib import ExitStack
import numpy as np

F32 = mybir.dt.float32
I32 = mybir.dt.int32
ALU = mybir.AluOpType
ACT = mybir.ActivationFunctionType
AX = mybir.AxisListType

P = 128
D = 1024
KT = D // P
T = 256
TT = T // P
FOX_HEADS, FOX_D = 8, 64
FOX_W = FOX_HEADS * FOX_D
RET_HEADS, RET_DK, RET_DV = 4, 64, 128
RET_QK_W = RET_HEADS * RET_DK
RET_V_W = RET_HEADS * RET_DV
BR_W = 512
E = 32
TOP_K = 4
FF = 1024
FT = FF // P
LIMIT, ALPHA = 7.0, 1.702
EPS = 1e-6
PLE = 256
SLOTS = 64
PAIRS = E // 2
ROUNDS = 2
MAX_JOBS = T * TOP_K // (SLOTS + 1)
C_FQ, C_FK, C_FV, C_FF = 0, FOX_W, 2 * FOX_W, 3 * FOX_W
C_RQ = C_FF + FOX_HEADS
C_RK = C_RQ + RET_QK_W
C_RV = C_RK + RET_QK_W
C_RG = C_RV + RET_V_W
CAUSAL_FILL = -1e30

MAIN_COLS = dict(ident=P, tri=2 * P, iota=P)
MIX_COLS = dict(cos=T, sin=T, rot=P, decay=RET_HEADS * 3 * P, mask=T, mean=P, la=1, lb=1,
                ra=FOX_HEADS, rb=FOX_HEADS)


def columns(spec):
    at, out = 0, {}
    for name, n in spec.items():
        out[name] = (at, at + n)
        at += n
    return out, at


MAIN_AT, MAIN_N = columns(MAIN_COLS)
MIX_AT, MIX_N = columns(MIX_COLS)


def tables():
    main = np.zeros((P, MAIN_N), np.float32)
    mix = np.zeros((P, MIX_N), np.float32)

    def put(table, at, name, value):
        a, b = at[name]
        table[:, a:b] = value

    i = np.arange(P)
    put(main, MAIN_AT, "ident", np.eye(P))
    put(main, MAIN_AT, "tri", np.concatenate([i[:, None] <= i[None, :], np.ones((P, P))], 1))
    put(main, MAIN_AT, "iota", i[None, :])
    half = RET_DK // 2
    inv = (np.float32(10000.0) ** (-np.arange(half, dtype=np.float32) / half)).astype(np.float32)
    ang = (inv[i % half][:, None] * np.arange(T, dtype=np.float32)[None, :]).astype(np.float32)
    put(mix, MIX_AT, "cos", np.cos(ang.astype(np.float64)))
    put(mix, MIX_AT, "sin", np.sin(ang.astype(np.float64)))
    rot = np.zeros((P, P))
    for m in range(P):
        if m % RET_DK < half:
            rot[m + half, m] = -1.0
        else:
            rot[m - half, m] = 1.0
    put(mix, MIX_AT, "rot", rot)
    lg = np.log1p(-np.exp2(-5.0 - np.arange(RET_HEADS)))
    key = i[:, None]
    for h in range(RET_HEADS):
        a = MIX_AT["decay"][0] + h * 3 * P
        gap = np.arange(T)[None, :] - key
        mix[:, a:a + T] = np.where(gap >= 0, np.exp(np.maximum(gap, 0) * lg[h]), 0)
        gap = i[None, :] - key
        mix[:, a + T:a + 3 * P] = np.where(gap >= 0, np.exp(np.maximum(gap, 0) * lg[h]), 0)
    mask = np.zeros((P, T))
    mask[:, P:] = np.where(i[None, :] <= i[:, None], 0.0, CAUSAL_FILL)
    put(mix, MIX_AT, "mask", mask)
    put(mix, MIX_AT, "mean", 1.0 / RET_DV)
    for h in range(FOX_HEADS):
        mix[h, MIX_AT["la"][0]] = 1.0
        mix[32 + h, MIX_AT["lb"][0]] = -1.0
        mix[32 + h, MIX_AT["ra"][0] + h] = 1.0
        mix[h, MIX_AT["rb"][0] + h] = 1.0
    return main, mix


UNITS = (
    [(f"xt{n}", "ad"[n % 2]) for n in range(4)]
    + [(f"bg{n}", "d") for n in range(4)] + [("bm", "d")]
    + [("q0", "a"), ("q1", "a"), ("k0", "d"), ("k1", "d")]
    + [("ff", "d"), ("v0", "d"), ("v1", "d")]
    + [("rq", "a"), ("rk", "a"), ("rv0", "a"), ("rv1", "a"), ("rg0", "d"), ("rg1", "d")]
    + [("rotq", "d"), ("rotk", "d"), ("cs", "d")]
    + [(f"rs{h}", "d") for h in range(4)]
    + [(f"fs{n}", "d") for n in range(6)]
    + [("ro0", "a"), ("ro1", "a")]
    + [(f"ga{n}", "a") for n in range(4)]
    + [("ms0", "d"), ("ms1", "d")]
    + [(f"pt{h}", "ad"[h % 2]) for h in range(8)]
    + [(f"gb{n}", "a") for n in range(4)]
    + [("fo0", "a"), ("fo1", "a")]
    + [(f"pr{n}", "d") for n in range(8)]
    + [(f"out{n}", "d") for n in range(4)]
    + [(f"ht{n}", "ad"[n % 2]) for n in range(4)]
    + [("rl", "d"), ("pos", "d"), ("wt", "d")]
)
NUMBER = {name: n for n, (name, _) in enumerate(UNITS)}
READER = dict(UNITS)
RANK = {}
for _eng in "ad":
    for _r, _name in enumerate([n for n, e in UNITS if e == _eng]):
        RANK[_name] = _r + 1

PROJ_BANK = (5, 6, 7, 4)
PE_AT = dict(gather=0, comb=2, gu=3, down=7, y=9, scatter=11)
PE_JOB_STEPS = 12
ACT_AT = dict(xg=0, exp=2, yT=6)
ACT_JOB_STEPS = 8
DVE_AT = dict(hot=0, comb=1, gu=2, y=10)
DVE_JOB_STEPS = 12
TAIL_T, TAIL_G = 5, 9


class Chain:

    def __init__(self, eng, sem):
        self.eng, self.sem, self.origin, self.steps = eng, sem, 0, 0

    def link(self, ins):
        self.steps += 1
        ins.then_inc(self.sem, 1)
        self.eng.wait_ge(self.sem, self.origin + self.steps)

    def enter(self, i, first, per):
        self.before = self.origin + self.steps
        self.per = per
        self.origin, self.steps = (i - first) * per + self.before, 0

    def leave(self, rounds):
        assert self.steps == self.per, (self.steps, self.per)
        self.origin, self.steps = self.before + rounds * self.per, 0


def build(nc, a, out, out_shape):
    ctx = ExitStack()
    with ctx:
        def sem(name):
            return ctx.enter_context(nc.semaphore(name))

        def sb(name, cols, dt=F32):
            return ctx.enter_context(nc.sbuf_tensor(name, [P, cols], dt))

        bank = [ctx.enter_context(nc.psum_tensor(f"bank{n}", [P, 512], F32)) for n in range(8)]

        slot = [sb(f"slot{n}", 8 * 1024) for n in range(4)]
        down_slot = sb("down_slot", 8 * 1024)
        h_t = sb("h", TT * D)
        xnT_t = sb("xnT", KT * T)
        gates_t = sb("gates", 16 * T)
        fr_t = sb("branches", 8 * T)
        cmain = sb("cmain", MAIN_N)
        bguT_t = sb("bguT", E * 2 * FT)
        small = sb("small", 740)
        jobs_i = sb("jobs_i", 16, I32)

        def wview(s):
            return s[:, :].rearrange("p (k n) -> p k n", k=KT)

        W = [wview(s) for s in slot]
        half_down = [down_slot[:, 4096 * n:4096 * (n + 1)].rearrange("p (k n) -> p k n", k=FT)
                     for n in range(2)]
        h = h_t[:, :].rearrange("p (t n) -> p t n", t=TT)
        xnT = xnT_t[:, :].rearrange("p (k n) -> p k n", k=KT)
        gates = gates_t[:, :].rearrange("p (k n) -> p k n", k=16)
        foxT = fr_t[:, 0:1024].rearrange("p (k n) -> p k n", k=4)
        roT = fr_t[:, 1024:2048].rearrange("p (k n) -> p k n", k=4)
        bguT = bguT_t[:, :].rearrange("p (e r i) -> p e r i", e=E, r=2)

        def main(name):
            return cmain[:, MAIN_AT[name][0]:MAIN_AT[name][1]]

        ident, tri, iota = main("ident"), main("tri"), main("iota")
        ones = tri[:, P:2 * P]

        taken = [0]

        def cut(n):
            taken[0] += n
            assert taken[0] <= small.shape[1], taken
            return small[:, taken[0] - n:taken[0]]

        lf = cut(2 * P).rearrange("p (t n) -> p t n", t=TT)
        wp = lf
        ffw = cut(KT * FOX_HEADS).rearrange("p (k n) -> p k n", k=KT)
        bfb = cut(FOX_HEADS)
        bmgT = cut(16)
        brb = cut(E)
        wrout = cut(KT * E).rearrange("p (k n) -> p k n", k=KT)
        zff = cut(16).rearrange("p (t n) -> p t n", t=TT)
        aff = cut(16).rearrange("p (t n) -> p t n", t=TT)
        ssq = cut(2)
        rstd = cut(2)
        newton = cut(2)
        epsb = cut(1)
        mx = cut(16)
        sums = cut(16)
        m8 = cut(16).rearrange("p (t n) -> p t n", t=TT)
        nmax = cut(2)
        ngt = cut(2)
        jobf = cut(16)

        def region(t, start):
            at = [start]

            def take(n):
                at[0] += n
                assert at[0] <= t.shape[1], at
                return t[:, at[0] - n:at[0]]
            return take

        s3 = region(slot[3], 0)
        cmix = s3(MIX_N)

        def mix(name):
            return cmix[:, MIX_AT[name][0]:MIX_AT[name][1]]

        early = region(slot[3], MIX_N)
        gain_mix = early(D)
        xn = early(TT * D).rearrange("p (t n) -> p t n", t=TT)
        brows = early(2 * FF)
        bmrows = early(P)
        vz = s3(TT * FOX_HEADS * P).rearrange("p (t h n) -> p t h n", t=TT, h=FOX_HEADS)
        rv = s3(TT * RET_V_W).rearrange("p (t n) -> p t n", t=TT)
        rqT = s3(2 * T).rearrange("p (k n) -> p k n", k=2)
        rkz = s3(RET_HEADS * T).rearrange("p (h n) -> p h n", h=RET_HEADS)
        L = s3(T)
        sd = region(down_slot, 0)
        qT = sd(4 * T).rearrange("p (k n) -> p k n", k=4)
        kz = sd(FOX_HEADS * T).rearrange("p (h n) -> p h n", h=FOX_HEADS)
        R = sd(FOX_HEADS * T).rearrange("p (h n) -> p h n", h=FOX_HEADS)
        probsT = sd(FOX_HEADS * 3 * P).rearrange("p (h n) -> p h n", h=FOX_HEADS)
        rr = probsT.rearrange("p h n -> p (h n)")[:, 0:1024].rearrange("p (k n) -> p k n", k=4)
        rsq = probsT.rearrange("p h n -> p (h n)")[:, 1024:2048].rearrange("p (k n) -> p k n", k=4)
        rseed = R[:, 0:4]
        rraw = gates_t[:, 0:1024].rearrange("p (w k n) -> p w k n", w=2, k=2)
        rtmp = gates_t[:, 1024:1536].rearrange("p (k n) -> p k n", k=2)
        rgsig = gates_t[:, 1536:2048].rearrange("p (k n) -> p k n", k=2)
        scT = gates_t[:, 2048:2048 + 1536].rearrange("p (h n) -> p h n", h=RET_HEADS)
        probs1 = gates_t[:, 2048:4096].rearrange("p (h n) -> p h n", h=FOX_HEADS)
        probs0 = fr_t[:, 0:1024].rearrange("p (h n) -> p h n", h=FOX_HEADS)

        gain_ffn = fr_t[:, 0:1024]
        bdown = fr_t[:, 1024:2048]
        hn = gates_t[:, 0:2048].rearrange("p (t n) -> p t n", t=TT)
        xg = gates_t[:, 2048:3072].rearrange("p (k s) -> p k s", k=KT)
        yT = gates_t[:, 3072:4096].rearrange("p (k s) -> p k s", k=KT)
        act = fr_t[:, 0:1024].rearrange("p (i s) -> p i s", i=FT)
        act2 = fr_t[:, 0:1024].rearrange("p (w i s) -> p w i s", w=2, i=FT)
        Y = fr_t[:, 1024:2048]
        mo = region(xnT_t, 0)
        hot = mo(2 * P).rearrange("p (t s) -> p t s", t=TT)
        comb = mo(2 * P).rearrange("p (t s) -> p t s", t=TT)
        combT = mo(T)
        gl = mo(512)
        ex = mo(256)
        posm = mo(2 * E).rearrange("p (t e) -> p t e", t=TT)
        wr = mo(2 * E).rearrange("p (t e) -> p t e", t=TT)
        posq = mo(TT * E * ROUNDS).rearrange("p (t e r) -> p t e r", t=TT, e=E)
        jf = mo(64)
        jscan = mo(64)
        jtmp = mo(64)
        lg = gl[:, 0:64].rearrange("p (t e) -> p t e", t=TT)
        gt = gl[:, 64:128].rearrange("p (t e) -> p t e", t=TT)
        eq = gl[:, 128:192].rearrange("p (t e) -> p t e", t=TT)
        cum = gl[:, 192:256].rearrange("p (t e) -> p t e", t=TT)
        sel = gl[:, 256:320].rearrange("p (t e) -> p t e", t=TT)
        ew = gl[:, 320:384].rearrange("p (t e) -> p t e", t=TT)

        tail = region(slot[1], 0)
        wpp = tail(2 * D).rearrange("p (k n) -> p k n", k=2)
        prow = tail(TT * PLE).rearrange("p (t n) -> p t n", t=TT)
        gain_ple = tail(D)
        gain_fin = tail(D)
        pT = tail(2 * T).rearrange("p (k n) -> p k n", k=2)
        hn3 = tail(TT * D).rearrange("p (t n) -> p t n", t=TT)
        sig = tail(D).rearrange("p (w n) -> p w n", w=2)
        hn3T = gates_t[:, 0:2048].rearrange("p (k n) -> p k n", k=KT)

        s_x, s_cmain, s_cmix, s_gain = sem("x_loaded"), sem("cmain_loaded"), sem("cmix_loaded"), sem("gain_loaded")
        s_ffw, s_bf, s_br = sem("ffw_loaded"), sem("b_forget_loaded"), sem("b_router_loaded")
        s_wrouter = sem("w_router_loaded")
        s_bias = sem("bias_rows_loaded")
        s_zero = sem("pool_zeroed")
        ld = {k: sem(f"loaded_{k}") for k in
              ("q", "k", "v", "rqk", "rvg", "gate0", "gate1", "branch", "out", "gain_ffn", "b_down")}
        unit_done = sem("unit_done")
        act_freed = sem("act_freed")
        dve_freed = sem("dve_freed")
        freed = {"a": act_freed, "d": dve_freed}
        dve_step, act_step = sem("dve_step"), sem("act_step")
        ssq_made = sem("sum_of_squares_made")
        xn_made = sem("xn_made")
        log1p_made = sem("log1p_made")
        zff_made = sem("forget_logits_made")
        lf_made = sem("log_forget_made")
        rgsig_made = sem("rg_sigmoid_made")
        rot_made = sem("rotary_made")
        max_made, probs_exp, probs_made = sem("row_max_made"), sem("probs_exp_made"), sem("probs_made")
        ro_made = sem("retention_made")
        rseed_made, s_eps = sem("retention_root_begun"), sem("eps_set")
        hn_made = sem("hn_made")
        sel_made, top_made, rexp_made, w_made = sem("selection_made"), sem("router_max_made"), sem("router_exp_made"), sem("routing_weights_made")
        wt_saved = sem("weights_T_saved")
        jobs_made = sem("jobs_made")
        acc_begun = sem("accumulators_begun")
        ld_gu = [sem(f"gate_up_loaded{n}") for n in range(4)]
        ld_dn = [sem(f"down_loaded{n}") for n in range(2)]
        gu_done = sem("gate_up_done")
        dn_done = sem("down_half_done")
        gather_done = sem("gather_done")
        ct_done = sem("comb_transposed")
        yt_done = sem("y_transposed")
        hot_made, comb_made = sem("one_hot_made"), sem("comb_made")
        clipped, act_made = sem("glu_clipped"), sem("act_made")
        ct_saved, y_saved = sem("combT_saved"), sem("y_saved")
        sig_done = sem("glu_sigmoid_made")
        xg_saved, yt_saved = sem("xg_saved"), sem("yT_saved")
        ld_job = sem("job_weights_loaded")
        job_pe, job_act, job_dve = sem("job_pe_step"), sem("job_act_step"), sem("job_dve_step")
        ld_tail = {k: sem(f"loaded_{k}") for k in ("ple_gate", "ple_proj", "p", "gain_ple", "gain_fin")}
        tail_done, tail_step = sem("tail_unit_done"), sem("dve_tail_step")
        pT_saved, h2_made, hn3_made, ht_act, ht_dve = sem("pT_saved"), sem("h2_made"), sem("hn3_made"), sem("hn3T_saved_by_act"), sem("hn3T_saved_by_dve")
        ple_sig, sig_made, ssq_tail = sem("ple_sigmoid_made"), sem("ple_gate_used"), sem("tail_squares_made")
        y_made, stored = sem("y_made"), sem("stored")

        gu_w = a["w_gate_up"][0].rearrange("e (k p) n -> e p k n", p=P)
        dn_w = a["w_down"][0].rearrange("e (k p) n -> e p k n", p=P)

        def rows(w):
            return w.rearrange("(k p) n -> p k n", p=P)

        w_in = rows(a["w_in"][0])
        w_mg = rows(a["w_merge_gate"][0])
        w_br = a["w_branch"][0].rearrange("g (c p) n -> p (g c) n", p=P)
        x_rows = a["x"][0].rearrange("(t p) n -> p t n", p=P)
        out_rows = out[0].rearrange("(t p) n -> p t n", p=P)
        tok = lambda t: slice(t * P, (t + 1) * P)

        def unit_ready(eng, name):
            eng.wait_ge(unit_done, NUMBER[name] + 1)

        def unit_saved(eng, name):
            eng.wait_ge(freed[READER[name]], RANK[name])

        def ubank(name):
            return bank[NUMBER[name] % 8]

        block = ctx.enter_context(nc.Block())

        @block.sync
        def _(sp):
            sp.dma_start(h, x_rows).then_inc(s_x, 16)
            sp.dma_start(cmain[:, :], a["t_main"]).then_inc(s_cmain, 16)
            sp.dma_start(W[0][:, :, 0:512], w_in[:, :, C_FQ:C_FK]).then_inc(ld["q"], 16)
            sp.dma_start(W[0][:, :, 512:1024], w_in[:, :, C_FK:C_FV]).then_inc(ld["k"], 16)
            sp.dma_start(W[1][:, :, 0:512], w_in[:, :, C_FV:C_FF]).then_inc(ld["v"], 16)
            sp.dma_start(W[1][:, :, 512:1024], w_in[:, :, C_RQ:C_RV]).then_inc(ld["rqk"], 16)
            sp.dma_start(W[2], w_in[:, :, C_RV:C_RG + RET_V_W]).then_inc(ld["rvg"], 16)
            unit_ready(sp, "k1")
            sp.dma_start(W[0], w_mg[:, :, 0:D]).then_inc(ld["gate0"], 16)
            unit_ready(sp, "rk")
            sp.dma_start(W[1], w_mg[:, :, D:2 * D]).then_inc(ld["gate1"], 16)
            unit_ready(sp, "rg1")
            sp.dma_start(W[2], w_br).then_inc(ld["branch"], 16)
            unit_ready(sp, "ga3")
            sp.dma_start(W[0], gu_w[0][:, :, 0:D]).then_inc(ld_gu[0], 16)
            unit_ready(sp, "gb3")
            sp.dma_start(W[1], gu_w[0][:, :, D:2 * D]).then_inc(ld_gu[1], 16)
            unit_ready(sp, "fo1")
            sp.wait_ge(ro_made, 2)
            sp.dma_start(W[3], rows(a["w_out"][0])).then_inc(ld["out"], 16)
            for n in range(2):
                sp.dma_start(half_down[n], dn_w[0][:, :, 512 * n:512 * (n + 1)]).then_inc(ld_dn[n], 16)
            unit_ready(sp, "pr7")
            sp.dma_start(gain_ffn, a["ffn_norm"].to_broadcast([P, D])).then_inc(ld["gain_ffn"], 16)
            sp.dma_start(W[2], gu_w[1][:, :, 0:D]).then_inc(ld_gu[2], 16)
            sp.wait_ge(s_zero, 7)
            sp.dma_start(bdown[0:E, :], a["b_down"][0]).then_inc(ld["b_down"], 16)
            unit_ready(sp, "out3")
            sp.dma_start(W[3], gu_w[1][:, :, D:2 * D]).then_inc(ld_gu[3], 16)

            def load_gate_up(n, p):
                sp.wait_ge(gu_done, 4 * p + (n + 1))
                sp.dma_start(W[n], gu_w[2 * p + (2 + n // 2)][:, :, D * (n % 2):D * (n % 2 + 1)]).then_inc(ld_gu[n], 16)

            def load_down(e, used):
                for n in range(2):
                    sp.wait_ge(dn_done, used + (n + 1))
                    sp.dma_start(half_down[n], dn_w[e][:, :, 512 * n:512 * (n + 1)]).then_inc(ld_dn[n], 16)

            with sp.Fori(0, PAIRS - 1) as p:
                load_gate_up(0, p)
                load_gate_up(1, p)
                load_gate_up(2, p)
                load_down(2 * p + 1, 4 * p)
                load_gate_up(3, p)
                load_down(2 * p + 2, 4 * p + 2)
            last = PAIRS - 1
            load_down(E - 1, 4 * last)
            sp.wait_ge(gu_done, 4 * last + 2)
            sp.dma_start(W[0], rows(a["w_ple_gate"][0])).then_inc(ld_tail["ple_gate"], 16)
            sp.dma_start(wpp, a["w_ple_proj"][0].rearrange("(k p) n -> p k n", p=P)).then_inc(ld_tail["ple_proj"], 16)
            sp.dma_start(prow, a["p"][0, 0].rearrange("(t p) n -> p t n", p=P)).then_inc(ld_tail["p"], 16)
            sp.dma_start(gain_ple, a["ple_norm"].to_broadcast([P, D])).then_inc(ld_tail["gain_ple"], 16)
            sp.dma_start(gain_fin, a["final_norm"].rearrange("(a n) -> a n", a=1).to_broadcast([P, D])).then_inc(ld_tail["gain_fin"], 16)
            sp.wait_ge(gu_done, 4 * PAIRS)
            sp.wait_ge(dn_done, 4 * PAIRS)
            sp.wait_ge(jobs_made, 1)
            n_jobs = sp.value_load(jobs_i[0:1, MAX_JOBS:MAX_JOBS + 1], min_val=0, max_val=MAX_JOBS)
            with sp.Fori(0, MAX_JOBS) as j:
                with sp.If(j < n_jobs):
                    q = sp.value_load(jobs_i[0:1, bass.ds(j, 1)], min_val=0, max_val=E * ROUNDS - 1)
                    e = sp.snap(q // 2)
                    sp.wait_ge(job_pe, j * PE_JOB_STEPS + 1)
                    for n in range(2):
                        sp.dma_start(W[2 + n], gu_w[e][:, :, D * n:D * (n + 1)]).then_inc(ld_job, 16)
                        sp.dma_start(half_down[n], dn_w[e][:, :, 512 * n:512 * (n + 1)]).then_inc(ld_job, 16)
            for t in range(TT):
                sp.wait_ge(y_made, t + 1)
                sp.dma_start(out_rows[:, t], hn3[:, t]).then_inc(stored, 16)
            sp.wait_ge(stored, 16 * TT)

        @block.gpsimd
        def _(pool):
            nc.gpsimd.memset(brows, 0.0).then_inc(s_zero, 1)
            nc.gpsimd.memset(bmrows, 0.0).then_inc(s_zero, 1)
            pool.wait_ge(s_zero, 2)
            pool.dma_start(brows[0:E, :], a["b_gate_up"][0]).then_inc(s_bias, 16)
            pool.dma_start(bmrows[0:16, :], a["b_merge_gate"].rearrange("a (r n) -> (a r) n", r=16)).then_inc(s_bias, 16)
            nc.gpsimd.memset(kz, 0.0).then_inc(s_zero, 1)
            nc.gpsimd.memset(small[:, 0:2 * P], 0.0).then_inc(s_zero, 1)
            unit_ready(pool, "bm")
            nc.gpsimd.memset(slot[3][:, MIX_N:MIX_N + TT * FOX_HEADS * P], 0.0).then_inc(s_zero, 1)
            nc.gpsimd.memset(rkz, 0.0).then_inc(s_zero, 1)
            unit_ready(pool, "pr7")
            nc.gpsimd.memset(bdown, 0.0).then_inc(s_zero, 1)

        @block.scalar
        def _(actE):
            chain = Chain(actE, act_step)
            link = chain.link

            def copy(o, i, scale=1.0):
                return nc.scalar.activation(o, i, ACT.Copy, scale=scale)

            actE.dma_start(gain_mix, a["mix_norm"].to_broadcast([P, D])).then_inc(s_gain, 16)
            actE.dma_start(cmix, a["t_mix"]).then_inc(s_cmix, 16)
            with nc.allow_non_contiguous_dma(reason="eight columns of w_in"):
                actE.dma_start(ffw, w_in[:, :, C_FF:C_RQ]).then_inc(s_ffw, 16)
            actE.dma_start(bfb, a["b_forget"].to_broadcast([P, FOX_HEADS])).then_inc(s_bf, 16)
            actE.dma_start(wrout, rows(a["w_router"][0])).then_inc(s_wrouter, 16)
            actE.dma_start(brb, a["b_router"].to_broadcast([P, E])).then_inc(s_br, 16)

            def squares(t, junk, done):
                link(nc.scalar.activation(junk, h[:, t], ACT.Square, accum_out=ssq[:, t:t + 1]))
                link(nc.scalar.activation(rstd[:, t:t + 1], ssq[:, t:t + 1], ACT.Ln, scale=1.0 / D, bias=epsb))
                nc.scalar.activation(rstd[:, t:t + 1], rstd[:, t:t + 1], ACT.Exp, scale=-0.5).then_inc(done, 1)

            actE.wait_ge(s_x, 16)
            actE.wait_ge(s_eps, 1)
            for t in range(TT):
                squares(t, xn[:, t], ssq_made)
            for n in (0, 2):
                unit_ready(actE, f"xt{n}")
                copy(xnT[:, 2 * n:2 * n + 2], ubank(f"xt{n}")[:, :].rearrange("p (k n) -> p k n", k=2)).then_inc(act_freed, 1)
            for n in range(2):
                unit_ready(actE, f"q{n}")
                copy(qT[:, 2 * n:2 * n + 2], ubank(f"q{n}")[:, :].rearrange("p (k n) -> p k n", k=2),
                     FOX_D ** -0.5).then_inc(act_freed, 1)
            actE.wait_ge(zff_made, 1)
            link(nc.scalar.activation(aff, aff, ACT.Exp))
            nc.scalar.activation(aff, aff, ACT.Ln, bias=1.0).then_inc(log1p_made, 1)
            for n, name in enumerate(("rq", "rk")):
                unit_ready(actE, name)
                copy(rraw[:, n], ubank(name)[:, :].rearrange("p (k n) -> p k n", k=2),
                     (1.0, RET_DK ** -0.5)[n]).then_inc(act_freed, 1)
            for t in range(TT):
                unit_ready(actE, f"rv{t}")
                copy(rv[:, t], ubank(f"rv{t}")[:, :]).then_inc(act_freed, 1)
            for n in range(2):
                unit_ready(actE, f"rg{n}")
                if n:
                    unit_saved(actE, "rg0")
                nc.scalar.activation(rgsig, ubank(f"rg{n}")[:, :].rearrange("p (k n) -> p k n", k=2),
                                     ACT.Sigmoid).then_inc(rgsig_made, 1)

            for b, pr in enumerate((probs0, probs1)):
                actE.wait_ge(max_made, b + 1)
                for hd in range(FOX_HEADS):
                    c = 8 * b + hd
                    last = nc.scalar.activation(pr[:, hd], pr[:, hd], ACT.Exp, bias=mx[:, c:c + 1],
                                                accum_out=sums[:, c:c + 1])
                last.then_inc(probs_exp, 1)
            for n in range(2):
                unit_ready(actE, f"ro{n}")
                v = ubank(f"ro{n}")[:, :].rearrange("p (k n) -> p k n", k=2)
                copy(rr[:, 2 * n:2 * n + 2], v)
                nc.scalar.activation(rsq[:, 2 * n:2 * n + 2], v, ACT.Square).then_inc(act_freed, 1)

            def gate(name, first):
                unit_ready(actE, name)
                for k in range(2):
                    last = nc.scalar.activation(gates[:, first + k], ubank(name)[:, k * T:(k + 1) * T],
                                                ACT.Sigmoid, bias=bmgT[:, first + k:first + k + 1])
                last.then_inc(act_freed, 1)

            actE.wait_ge(rot_made, 2)
            unit_saved(actE, "rg1")
            for n in range(4):
                gate(f"ga{n}", 2 * n)
            for n in range(2):
                unit_saved(actE, f"ms{n}")
                y = rseed[:, 2 * n:2 * n + 2]
                link(nc.scalar.activation(y, rsq[:, 2 * n:2 * n + 2], ACT.Ln))
                nc.scalar.activation(y, y, ACT.Exp, scale=-0.5).then_inc(rseed_made, 1)
            actE.wait_ge(ro_made, 2)
            for hd in range(0, FOX_HEADS, 2):
                unit_ready(actE, f"pt{hd}")
                copy(probsT[:, hd], ubank(f"pt{hd}")[:, 0:3 * P]).then_inc(act_freed, 1)
            for n in range(4):
                gate(f"gb{n}", 8 + 2 * n)
            for n in range(2):
                unit_ready(actE, f"fo{n}")
                copy(foxT[:, 2 * n:2 * n + 2], ubank(f"fo{n}")[:, :].rearrange("p (k n) -> p k n", k=2)).then_inc(act_freed, 1)

            unit_ready(actE, "out3")
            for t in range(TT):
                unit_saved(actE, f"out{2 * t + 1}")
                squares(t, hn[:, t], ssq_made)
            for n in (0, 2):
                unit_ready(actE, f"ht{n}")
                copy(xnT[:, 2 * n:2 * n + 2], ubank(f"ht{n}")[:, :].rearrange("p (k n) -> p k n", k=2)).then_inc(act_freed, 1)
            actE.wait_ge(top_made, 1)
            for t in range(TT):
                nc.scalar.activation(ew[:, t], lg[:, t], ACT.Exp, bias=nmax[:, t:t + 1]).then_inc(rexp_made, 1)

            def save_gathered(p):
                for n, b in enumerate((7, 4)):
                    actE.wait_ge(gather_done, 2 * p + (n + 1))
                    copy(xg[:, 4 * n:4 * n + 4], bank[b][:, :].rearrange("p (k s) -> p k s", k=4)).then_inc(xg_saved, 1)

            def pair(p, last):
                def exponentials(u):
                    actE.wait_ge(clipped, 4 * p + (u + 1))
                    nc.scalar.activation(ex, gl[:, 0:256], ACT.Sigmoid, scale=ALPHA).then_inc(sig_done, 1)

                def save_down(half):
                    actE.wait_ge(dn_done, 4 * p + (2 * half + 2))
                    copy(yT[:, :, SLOTS * half:SLOTS * (half + 1)],
                         bank[6][:, :].rearrange("p (k s) -> p k s", k=KT)).then_inc(yt_saved, 1)

                exponentials(0)
                exponentials(1)
                exponentials(2)
                save_down(0)
                exponentials(3)
                if not last:
                    save_gathered(p + 1)
                save_down(1)

            save_gathered(0)
            pair(0, False)
            with actE.Fori(1, PAIRS - 1) as p:
                pair(p, False)
            pair(PAIRS - 1, True)

            n_jobs = actE.value_load(jobs_i[0:1, MAX_JOBS:MAX_JOBS + 1], min_val=0, max_val=MAX_JOBS)
            with actE.Fori(0, MAX_JOBS) as j:
                with actE.If(j < n_jobs):
                    pe0, dve0 = j * PE_JOB_STEPS + 1, j * DVE_JOB_STEPS
                    for n, b in enumerate((7, 4)):
                        actE.wait_ge(job_pe, pe0 + PE_AT["gather"] + (n + 1))
                        copy(xg[:, 4 * n:4 * n + 4], bank[b][:, :].rearrange("p (k s) -> p k s", k=4)).then_inc(job_act, 1)
                    for u in range(4):
                        actE.wait_ge(job_dve, dve0 + DVE_AT["gu"] + (2 * u + 1))
                        nc.scalar.activation(ex, gl[:, 0:256], ACT.Sigmoid, scale=ALPHA).then_inc(job_act, 1)
                    for n in range(2):
                        actE.wait_ge(job_pe, pe0 + PE_AT["down"] + (n + 1))
                        copy(yT[:, 4 * n:4 * n + 4], bank[6 + n][:, :].rearrange("p (k s) -> p k s", k=4)).then_inc(job_act, 1)

            actE.wait_ge(tail_done, 1)
            copy(pT, bank[4][:, :].rearrange("p (k n) -> p k n", k=2)).then_inc(pT_saved, 1)
            for t in range(TT):
                actE.wait_ge(h2_made, 2 * (t + 1))
                squares(t, hn3[:, t], ssq_tail)
            for n in (0, 2):
                actE.wait_ge(tail_done, TAIL_T + n + 1)
                copy(hn3T[:, 2 * n:2 * n + 2], bank[n][:, :].rearrange("p (k n) -> p k n", k=2)).then_inc(ht_act, 1)
            for n in range(4):
                actE.wait_ge(tail_done, TAIL_G + n + 1)
                if n >= 2:
                    actE.wait_ge(sig_made, n - 1)
                nc.scalar.activation(sig[:, n % 2], bank[n][:, :], ACT.Sigmoid).then_inc(ple_sig, 1)
                if n % 2:
                    t = n // 2
                    actE.wait_ge(sig_made, n + 1)
                    squares(t, hn3[:, t], ssq_tail)

        @block.vector
        def _(dve):
            chain = Chain(dve, dve_step)
            link = chain.link
            v = nc.vector

            def inverse_rms(t):
                x, y, w = ssq[:, t:t + 1], rstd[:, t:t + 1], newton[:, t:t + 1]
                link(v.tensor_scalar(x, x, 1.0 / D, EPS, ALU.mult, ALU.add))
                link(v.scalar_tensor_tensor(out=w, in0=y, scalar=x, in1=y, op0=ALU.mult, op1=ALU.mult))
                link(v.tensor_scalar(w, w, -0.5, 1.5, ALU.mult, ALU.add))
                link(v.tensor_tensor(y, y, w, ALU.mult))

            def two(b):
                return b[:, :].rearrange("p (k n) -> p k n", k=2)

            v.memset(epsb, EPS).then_inc(s_eps, 1)
            dve.wait_ge(s_gain, 16)
            for t in range(TT):
                dve.wait_ge(ssq_made, t + 1)
                inverse_rms(t)
                v.scalar_tensor_tensor(out=xn[:, t], in0=h[:, t], scalar=rstd[:, t:t + 1], in1=gain_mix,
                                       op0=ALU.mult, op1=ALU.mult).then_inc(xn_made, 1)
            for n in (1, 3):
                unit_ready(dve, f"xt{n}")
                v.tensor_copy(xnT[:, 2 * n:2 * n + 2], two(ubank(f"xt{n}"))).then_inc(dve_freed, 1)
            for n in range(4):
                unit_ready(dve, f"bg{n}")
                v.tensor_copy(bguT[:, :, n // 2, 4 * (n % 2):4 * (n % 2) + 4].rearrange("p e i -> p i e"),
                              ubank(f"bg{n}")[:, :].rearrange("p (i e) -> p i e", i=4)[:, :, 0:E]).then_inc(dve_freed, 1)
            unit_ready(dve, "bm")
            v.tensor_copy(bmgT, ubank("bm")[:, 0:16]).then_inc(dve_freed, 1)
            dve.wait_ge(s_zero, 4)
            kz_p = kz.rearrange("p (t s) n -> p t s n", s=2)
            for n in range(2):
                unit_ready(dve, f"k{n}")
                for s in range(2):
                    last = v.tensor_copy(kz_p[64 * s:64 * s + 64, 2 * n:2 * n + 2, s],
                                         two(ubank(f"k{n}"))[64 * s:64 * s + 64])
                last.then_inc(dve_freed, 1)
            unit_ready(dve, "ff")
            dve.wait_ge(s_bf, 16)
            v.tensor_tensor(zff, ubank("ff")[:, 0:16].rearrange("p (t n) -> p t n", t=TT),
                            bfb.unsqueeze(1).to_broadcast([P, TT, FOX_HEADS]), ALU.add).then_inc(dve_freed, 1)
            unit_saved(dve, "ff")
            v.scalar_tensor_tensor(out=aff, in0=zff, scalar=-1.0, in1=zff,
                                   op0=ALU.mult, op1=ALU.min).then_inc(zff_made, 1)
            dve.wait_ge(s_zero, 6)
            for t in range(TT):
                unit_ready(dve, f"v{t}")
                src = ubank(f"v{t}")[:, :].rearrange("p (k s d) -> p k s d", s=2, d=FOX_D)
                dst = vz[:, t].rearrange("p (k s) n -> p k s n", s=2)
                for s in range(2):
                    last = v.tensor_copy(dst[:, :, s, FOX_D * s:FOX_D * (s + 1)], src[:, :, s])
                last.then_inc(dve_freed, 1)
            dve.wait_ge(log1p_made, 1)
            link(v.scalar_tensor_tensor(out=lf[:, :, 0:FOX_HEADS], in0=zff, scalar=0.0, in1=aff,
                                        op0=ALU.min, op1=ALU.subtract))
            v.tensor_copy(lf[:, :, 32:32 + FOX_HEADS], lf[:, :, 0:FOX_HEADS]).then_inc(lf_made, 1)
            for n in range(2):
                dve.wait_ge(rgsig_made, n + 1)
                v.tensor_tensor(roT[:, 2 * n:2 * n + 2], rgsig, two(ubank(f"rg{n}")), ALU.mult).then_inc(dve_freed, 1)
            dve.wait_ge(s_cmix, 16)
            sin2 = mix("sin").unsqueeze(1).to_broadcast([P, 2, T])
            cos2 = mix("cos").unsqueeze(1).to_broadcast([P, 2, T])
            rkz_p = rkz.rearrange("p (t s) n -> p t s n", s=2)
            for n, name in enumerate(("rotq", "rotk")):
                unit_ready(dve, name)
                v.tensor_tensor(rtmp, two(ubank(name)), sin2, ALU.mult).then_inc(dve_freed, 1)
                link(v.tensor_tensor(rraw[:, n], rraw[:, n], cos2, ALU.mult))
                if n == 0:
                    v.tensor_tensor(rqT, rraw[:, n], rtmp, ALU.add).then_inc(rot_made, 1)
                    dve.wait_ge(rot_made, 1)
                else:
                    for s in range(2):
                        hp = slice(64 * s, 64 * s + 64)
                        last = v.tensor_tensor(rkz_p[hp, :, s], rraw[hp, n], rtmp[hp], ALU.add)
                    last.then_inc(rot_made, 1)
            unit_ready(dve, "cs")
            cs = ubank("cs")[:, 0:T]
            v.tensor_scalar(L, cs, mix("la"), mix("lb"), ALU.mult, ALU.add)
            for hd in range(FOX_HEADS):
                last = v.tensor_scalar(R[:, hd], cs, mix("ra")[:, hd:hd + 1], mix("rb")[:, hd:hd + 1], ALU.mult, ALU.add)
            last.then_inc(dve_freed, 1)
            for hd in range(RET_HEADS):
                unit_ready(dve, f"rs{hd}")
                dec = mix("decay")[:, hd * 3 * P:(hd + 1) * 3 * P]
                v.tensor_tensor(scT[:, hd], ubank(f"rs{hd}")[:, 0:3 * P], dec, ALU.mult).then_inc(dve_freed, 1)
            m = mix("mask")
            for n in range(2):
                unit_ready(dve, f"fs{n}")
                v.tensor_tensor(probs0[:, 4 * n:4 * n + 4], ubank(f"fs{n}")[:, :].rearrange("p (k n) -> p k n", k=4),
                                m[:, P:2 * P].unsqueeze(1).to_broadcast([P, 4, P]), ALU.add).then_inc(dve_freed, 1)
            unit_saved(dve, "fs1")
            link(v.reduce_max(mx[:, 0:8], probs0, AX.X))
            v.tensor_scalar(mx[:, 0:8], mx[:, 0:8], -1.0, None, ALU.mult).then_inc(max_made, 1)
            unit_ready(dve, "ro1")
            for n in range(4):
                unit_ready(dve, f"fs{2 + n}")
                v.tensor_tensor(probs1[:, 2 * n:2 * n + 2], two(ubank(f"fs{2 + n}")),
                                m.unsqueeze(1).to_broadcast([P, 2, T]), ALU.add).then_inc(dve_freed, 1)
            unit_saved(dve, "fs5")
            link(v.reduce_max(mx[:, 8:16], probs1, AX.X))
            v.tensor_scalar(mx[:, 8:16], mx[:, 8:16], -1.0, None, ALU.mult).then_inc(max_made, 1)
            for b, pr in enumerate((probs0, probs1)):
                dve.wait_ge(probs_exp, b + 1)
                c = slice(8 * b, 8 * b + 8)
                link(v.reciprocal(sums[:, c], sums[:, c]))
                v.tensor_tensor(pr, pr, sums[:, c].unsqueeze(2).to_broadcast([P, FOX_HEADS, P * (b + 1)]),
                                ALU.mult).then_inc(probs_made, 1)
            for n in range(2):
                unit_ready(dve, f"ms{n}")
                s2 = rsq[:, 2 * n:2 * n + 2]
                v.tensor_scalar(s2, two(ubank(f"ms{n}")), EPS, None, ALU.add).then_inc(dve_freed, 1)
                dve.wait_ge(rseed_made, n + 1)
                y = rseed[:, 2 * n:2 * n + 2]
                link(v.tensor_tensor(s2, s2, y, ALU.mult))
                link(v.tensor_tensor(s2, s2, y, ALU.mult))
                link(v.tensor_scalar(s2, s2, -0.5, 1.5, ALU.mult, ALU.add))
                link(v.tensor_tensor(s2, s2, y, ALU.mult))
                link(v.tensor_tensor(s2, s2, rr[:, 2 * n:2 * n + 2], ALU.mult))
                v.tensor_tensor(roT[:, 2 * n:2 * n + 2], roT[:, 2 * n:2 * n + 2], s2, ALU.mult).then_inc(ro_made, 1)
            for hd in range(1, FOX_HEADS, 2):
                unit_ready(dve, f"pt{hd}")
                if hd == 1:
                    dve.wait_ge(ro_made, 2)
                v.tensor_copy(probsT[:, hd], ubank(f"pt{hd}")[:, 0:3 * P]).then_inc(dve_freed, 1)
            unit_saved(dve, "gb3")
            for n in range(4):
                unit_ready(dve, f"pr{n}")
                g = gates[:, 2 * n:2 * n + 2]
                v.tensor_tensor(g, g, two(ubank(f"pr{n}")), ALU.mult).then_inc(dve_freed, 1)
            for n in range(4):
                unit_ready(dve, f"pr{4 + n}")
                g, g1 = gates[:, 2 * n:2 * n + 2], gates[:, 8 + 2 * n:10 + 2 * n]
                link(v.tensor_tensor(g1, g1, two(ubank(f"pr{4 + n}")), ALU.mult))
                v.tensor_tensor(g, g, g1, ALU.add).then_inc(dve_freed, 1)
            for n in range(4):
                unit_ready(dve, f"out{n}")
                o = h[:, n // 2, 512 * (n % 2):512 * (n % 2 + 1)]
                v.tensor_tensor(o, o, ubank(f"out{n}")[:, :], ALU.add).then_inc(dve_freed, 1)
            dve.wait_ge(ld["gain_ffn"], 16)
            for t in range(TT):
                dve.wait_ge(ssq_made, TT + t + 1)
                inverse_rms(t)
                v.scalar_tensor_tensor(out=hn[:, t], in0=h[:, t], scalar=rstd[:, t:t + 1], in1=gain_ffn,
                                       op0=ALU.mult, op1=ALU.mult).then_inc(hn_made, 1)
            for n in (1, 3):
                unit_ready(dve, f"ht{n}")
                v.tensor_copy(xnT[:, 2 * n:2 * n + 2], two(ubank(f"ht{n}"))).then_inc(dve_freed, 1)
            unit_ready(dve, "rl")
            dve.wait_ge(s_br, 16)
            v.tensor_tensor(lg, ubank("rl")[:, 0:2 * E].rearrange("p (t e) -> p t e", t=TT),
                            brb.unsqueeze(1).to_broadcast([P, TT, E]), ALU.add).then_inc(dve_freed, 1)
            unit_saved(dve, "rl")
            for t in range(TT):
                link(v.max(m8[:, t], lg[:, t]))
            v.tensor_scalar(nmax.unsqueeze(2), m8[:, :, 0:1], -1.0, None, ALU.mult).then_inc(top_made, 1)
            thr = m8[:, :, TOP_K - 1:TOP_K].to_broadcast([P, TT, E])
            v.tensor_tensor(gt, lg, thr, ALU.is_gt)
            link(v.tensor_tensor(eq, lg, thr, ALU.is_equal))
            for t in range(TT):
                v.tensor_tensor_scan(cum[:, t], ones[:, 0:E], eq[:, t], 0.0, ALU.mult, ALU.add)
            link(v.reduce_sum(ngt, gt, AX.X))
            link(v.tensor_scalar(ngt, ngt, -1.0, float(TOP_K), ALU.mult, ALU.add))
            link(v.tensor_tensor(cum, cum, ngt.unsqueeze(2).to_broadcast([P, TT, E]), ALU.is_le))
            link(v.tensor_tensor(eq, eq, cum, ALU.mult))
            v.tensor_tensor(sel, gt, eq, ALU.add).then_inc(sel_made, 1)
            dve.wait_ge(sel_made, 1)
            dve.wait_ge(rexp_made, 2)
            link(v.tensor_tensor(ew, ew, sel, ALU.mult))
            link(v.reduce_sum(ngt, ew, AX.X))
            link(v.reciprocal(ngt, ngt))
            link(v.memset(small[:, 0:2 * P], 0.0))
            link(v.tensor_tensor(wr, ew, ngt.unsqueeze(2).to_broadcast([P, TT, E]), ALU.mult))
            v.tensor_copy(wp[:, :, 0:E], wr).then_inc(w_made, 1)
            unit_ready(dve, "pos")
            pos = ubank("pos")
            link(v.tensor_tensor(posm, pos[:, 0:2 * E].rearrange("p (t e) -> p t e", t=TT), sel, ALU.mult))
            link(v.tensor_scalar(posm, posm, -1.0, None, ALU.add))
            for r in range(ROUNDS):
                first = float(SLOTS + 2 * SLOTS * r)
                v.tensor_scalar(posq[:, :, :, r], posm, -first, None, ALU.add)
                last = v.tensor_scalar(jf.rearrange("p (e r) -> p e r", r=ROUNDS)[:, :, r], pos[:, 2 * E:3 * E],
                                       first, None, ALU.is_gt)
            last.then_inc(dve_freed, 1)
            unit_ready(dve, "wt")
            v.tensor_copy(combT, ubank("wt")[:, 0:T]).then_inc(dve_freed, 1)

            def one_hot(o, position, weight=None):
                for t in range(TT):
                    if weight is None:
                        last = v.tensor_scalar(o[t], iota[:, 0:o[t].shape[-1]], position(t), None, ALU.is_equal)
                    else:
                        last = v.tensor_scalar(o[t], iota[:, 0:o[t].shape[-1]], position(t), weight(t),
                                               ALU.is_equal, ALU.mult)
                return last

            def col(table, t, e):
                return table[:, t, bass.ds(e, 1)] if not isinstance(e, int) else table[:, t, e:e + 1]

            def pair_hot(p):
                for half in range(2):
                    s = slice(SLOTS * half, SLOTS * (half + 1))
                    last = one_hot([hot[:, t, s] for t in range(TT)], lambda t: col(posm, t, 2 * p + half))
                last.then_inc(hot_made, 1)

            def swiglu(u, psum, e, tiles, dst, freed_sem, done_sem, exp_wait):
                i0 = u * tiles if tiles == 2 else (u % 2) * tiles
                width = 256 // tiles
                b = bguT[:, e, :, i0:i0 + tiles] if isinstance(e, int) else bguT[:, bass.ds(e, 1), :, i0:i0 + tiles].squeeze(1)
                link(v.tensor_tensor(gl.rearrange("p (r i s) -> p r i s", r=2, i=tiles),
                                     psum[:, :].rearrange("p (r i s) -> p r i s", r=2, i=tiles),
                                     b.unsqueeze(3).to_broadcast([P, 2, tiles, width]), ALU.add))
                v.tensor_scalar(gl[:, 0:256], gl[:, 0:256], LIMIT, None, ALU.min).then_inc(freed_sem, 1)
                link(v.tensor_scalar(gl[:, 256:512], gl[:, 256:512], LIMIT, -LIMIT, ALU.min, ALU.max))
                link(v.scalar_tensor_tensor(out=gl[:, 256:512], in0=gl[:, 256:512], scalar=1.0,
                                            in1=gl[:, 0:256], op0=ALU.add, op1=ALU.mult))
                exp_wait()
                v.tensor_tensor(dst, gl[:, 256:512].rearrange("p (i s) -> p i s", i=tiles),
                                ex.rearrange("p (i s) -> p i s", i=tiles), ALU.mult).then_inc(done_sem, 1)

            def save_y(p):
                for n in range(2):
                    dve.wait_ge(yt_done, 2 * p + (n + 1))
                    v.tensor_copy(Y[:, 512 * n:512 * (n + 1)], bank[6 + n][:, :]).then_inc(y_saved, 1)

            def pair(p, first, last):
                if not first:
                    dve.wait_ge(ct_done, p)
                for half in range(2):
                    s = slice(SLOTS * half, SLOTS * (half + 1))
                    ins = one_hot([comb[:, t, s] for t in range(TT)], lambda t: col(posm, t, 2 * p + half),
                                  lambda t: col(wr, t, 2 * p + half))
                ins.then_inc(comb_made, 1)
                if not last:
                    dve.wait_ge(gather_done, 2 * p + 2)
                    pair_hot(p + 1)

                def activate(u):
                    dve.wait_ge(gu_done, 4 * p + (u + 1))
                    if not (first and u == 0):
                        dve.wait_ge(act_made, 4 * p + u)
                    swiglu(u, bank[4 + u % 2], 2 * p + u // 2, 4,
                           act2[:, u // 2, 4 * (u % 2):4 * (u % 2) + 4], clipped, act_made,
                           lambda: dve.wait_ge(sig_done, 4 * p + (u + 1)))

                activate(0)
                if not first:
                    save_y(p - 1)
                activate(1)
                activate(2)
                activate(3)
                dve.wait_ge(ct_done, p + 1)
                v.tensor_copy(combT, bank[5][:, 0:T]).then_inc(ct_saved, 1)

            dve.wait_ge(acc_begun, 1)
            pair_hot(0)
            link(v.tensor_tensor_scan(jscan, ones[:, 0:64], jf, 0.0, ALU.mult, ALU.add))
            link(v.tensor_copy(jobf[:, MAX_JOBS:MAX_JOBS + 1], jscan[:, 63:64]))
            link(v.tensor_tensor(jscan, jscan, jf, ALU.mult))
            for j in range(MAX_JOBS):
                link(v.tensor_scalar(jtmp, jscan, float(j + 1), None, ALU.is_equal))
                link(v.tensor_tensor(jtmp, jtmp, iota[:, 0:64], ALU.mult))
                link(v.reduce_sum(jobf[:, j:j + 1], jtmp, AX.X))
            v.tensor_copy(jobs_i[:, :], jobf).then_inc(jobs_made, 1)

            pair(0, True, False)
            with dve.Fori(1, PAIRS - 1) as p:
                chain.enter(p, 1, 4 * 3)
                pair(p, False, False)
                chain.leave(PAIRS - 2)
            pair(PAIRS - 1, False, True)
            save_y(PAIRS - 1)

            dve.wait_ge(jobs_made, 1)
            n_jobs = dve.value_load(jobs_i[0:1, MAX_JOBS:MAX_JOBS + 1], min_val=0, max_val=MAX_JOBS)
            with dve.Fori(0, MAX_JOBS) as j:
                with dve.If(j < n_jobs):
                    chain.enter(j, 0, 4 * 3)
                    q = dve.value_load(jobs_i[0:1, bass.ds(j, 1)], min_val=0, max_val=E * ROUNDS - 1)
                    e = dve.snap(q // 2)
                    pe0, act0, dve0 = j * PE_JOB_STEPS + 1, j * ACT_JOB_STEPS, j * DVE_JOB_STEPS
                    dve.wait_ge(job_pe, pe0)
                    posf = posq.rearrange("p t e r -> p t (e r)")
                    one_hot([hot[:, t] for t in range(TT)], lambda t: col(posf, t, q))
                    one_hot([comb[:, t] for t in range(TT)], lambda t: col(posf, t, q),
                            lambda t: col(wr, t, e)).then_inc(job_dve, 1)
                    dve.wait_ge(job_pe, pe0 + PE_AT["comb"] + 1)
                    v.tensor_copy(combT, bank[5][:, 0:T]).then_inc(job_dve, 1)
                    for u in range(4):
                        dve.wait_ge(job_pe, pe0 + PE_AT["gu"] + (u + 1))
                        dve.wait_ge(job_dve, dve0 + DVE_AT["gu"] + 2 * u)
                        swiglu(u, bank[4 + u % 2], e, 2, act[:, 2 * u:2 * u + 2], job_dve, job_dve,
                               lambda: dve.wait_ge(job_act, act0 + ACT_AT["exp"] + (u + 1)))
                    for n in range(2):
                        dve.wait_ge(job_pe, pe0 + PE_AT["y"] + (n + 1))
                        v.tensor_copy(Y[:, 512 * n:512 * (n + 1)], bank[4 + n][:, :]).then_inc(job_dve, 1)
                    chain.leave(MAX_JOBS)
            chain = Chain(dve, tail_step)
            link = chain.link

            dve.wait_ge(tail_done, 1)
            for n in range(4):
                o = h[:, n // 2, 512 * (n % 2):512 * (n % 2 + 1)]
                v.tensor_tensor(o, o, bank[n][:, :], ALU.add).then_inc(h2_made, 1)
            dve.wait_ge(ld_tail["gain_ple"], 16)
            for t in range(TT):
                dve.wait_ge(ssq_tail, t + 1)
                inverse_rms(t)
                v.scalar_tensor_tensor(out=hn3[:, t], in0=h[:, t], scalar=rstd[:, t:t + 1], in1=gain_ple,
                                       op0=ALU.mult, op1=ALU.mult).then_inc(hn3_made, 1)
            for n in (1, 3):
                dve.wait_ge(tail_done, TAIL_T + n + 1)
                v.tensor_copy(hn3T[:, 2 * n:2 * n + 2], two(bank[n])).then_inc(ht_dve, 1)
            for n in range(4):
                t = n // 2
                s = sig[:, n % 2]
                dve.wait_ge(ple_sig, n + 1)
                link(v.tensor_tensor(s, s, bank[PROJ_BANK[n]][:, :], ALU.mult))
                o = h[:, t, 512 * (n % 2):512 * (n % 2 + 1)]
                v.tensor_tensor(o, o, s, ALU.add).then_inc(sig_made, 1)
                if n % 2:
                    dve.wait_ge(ld_tail["gain_fin"], 16)
                    dve.wait_ge(ssq_tail, TT + t + 1)
                    inverse_rms(t)
                    v.scalar_tensor_tensor(out=hn3[:, t], in0=h[:, t], scalar=rstd[:, t:t + 1], in1=gain_fin,
                                           op0=ALU.mult, op1=ALU.mult).then_inc(y_made, 1)

        @block.tensor
        def _(pe):
            mm = nc.tensor.matmul

            def begin(name):
                n = NUMBER[name]
                if n >= 8:
                    unit_saved(pe, UNITS[n - 8][0])
                return bank[n % 8]

            def transposes(name, pieces):
                b = begin(name)
                for n, piece in enumerate(pieces):
                    last = nc.tensor.transpose(b[:, n * P:(n + 1) * P], piece, ident)
                last.then_inc(unit_done, 1)

            def to_T(name, w, cols, src=None, tiles=KT):
                b = begin(name)
                src = xnT if src is None else src
                for n, c in enumerate(cols):
                    for k in range(tiles):
                        last = mm(b[:, n * T:(n + 1) * T], w[:, k, c:c + P], src[:, k], start=(k == 0), stop=(k == tiles - 1))
                last.then_inc(unit_done, 1)

            def to_tokens(name, w, t, c, src=None):
                b = begin(name)
                src = xnT if src is None else src
                for k in range(KT):
                    last = mm(b[:, :], src[:, k, tok(t)], w[:, k, c:c + 512], start=(k == 0), stop=(k == KT - 1))
                last.then_inc(unit_done, 1)

            pe.wait_ge(s_cmain, 16)
            pe.wait_ge(xn_made, 2)
            for n in range(4):
                transposes(f"xt{n}", [xn[:, t, k * P:(k + 1) * P] for k in (2 * n, 2 * n + 1) for t in range(TT)])
            pe.wait_ge(s_bias, 32)
            for n in range(4):
                transposes(f"bg{n}", [brows[:, 2 * P * i + n // 2:2 * P * (i + 1):2]
                                      for i in range(4 * (n % 2), 4 * (n % 2) + 4)])
            transposes("bm", [bmrows])
            for n in range(4):
                unit_saved(pe, f"xt{n}")
            pe.wait_ge(ld["q"], 16)
            for n in range(2):
                to_T(f"q{n}", W[0], (2 * P * n, 2 * P * n + P))
            pe.wait_ge(ld["k"], 16)
            for n in range(2):
                to_T(f"k{n}", W[0], (512 + 2 * P * n, 512 + 2 * P * n + P))
            b = begin("ff")
            pe.wait_ge(s_ffw, 16)
            for t in range(TT):
                for k in range(KT):
                    last = mm(b[:, 8 * t:8 * t + 8], xnT[:, k, tok(t)], ffw[:, k], start=(k == 0), stop=(k == KT - 1))
            last.then_inc(unit_done, 1)
            pe.wait_ge(ld["v"], 16)
            for t in range(TT):
                to_tokens(f"v{t}", W[1], t, 0)
            pe.wait_ge(ld["rqk"], 16)
            to_T("rq", W[1], (512, 512 + P))
            to_T("rk", W[1], (512 + 2 * P, 512 + 3 * P))
            pe.wait_ge(ld["rvg"], 16)
            for t in range(TT):
                to_tokens(f"rv{t}", W[2], t, 0)
            for n in range(2):
                to_T(f"rg{n}", W[2], (512 + 2 * P * n, 512 + 2 * P * n + P))
            pe.wait_ge(s_cmix, 16)
            for n, name in enumerate(("rotq", "rotk")):
                b = begin(name)
                unit_saved(pe, ("rq", "rk")[n])
                mm(b[:, :], mix("rot"), rraw[:, n].rearrange("p k n -> p (k n)"), start=True, stop=True).then_inc(unit_done, 1)
            b = begin("cs")
            pe.wait_ge(lf_made, 1)
            mm(b[:, 0:T], lf[:, 0], tri, start=True, stop=False)
            mm(b[:, P:T], lf[:, 1], tri[:, 0:P], start=False, stop=True).then_inc(unit_done, 1)
            pe.wait_ge(rot_made, 2)
            for hd in range(RET_HEADS):
                b = begin(f"rs{hd}")
                mm(b[:, 0:T], rkz[:, hd, 0:P], rqT[:, hd // 2], start=True, stop=True)
                mm(b[:, T:3 * P], rkz[:, hd, P:T], rqT[:, hd // 2, P:T], start=True, stop=True).then_inc(unit_done, 1)
            unit_saved(pe, "cs")
            unit_saved(pe, "q1")
            for n in range(6):
                b = begin(f"fs{n}")
                t, heads, width = (0, range(4 * n, 4 * n + 4), P) if n < 2 else (1, range(2 * n - 4, 2 * n - 2), T)
                for i, hd in enumerate(heads):
                    o = b[:, i * width:(i + 1) * width]
                    mm(o, qT[:, hd // 2, tok(t)], kz[:, hd, 0:width], start=True, stop=False)
                    last = mm(o, L[:, tok(t)], R[:, hd, 0:width], start=False, stop=True)
                last.then_inc(unit_done, 1)
            unit_saved(pe, "rs3")
            unit_saved(pe, "rv1")
            for n in range(2):
                b = begin(f"ro{n}")
                for i in range(2):
                    hd = 2 * n + i
                    c = slice(hd * RET_DV, (hd + 1) * RET_DV)
                    mm(b[:, i * T:(i + 1) * T], rv[:, 0, c], scT[:, hd, 0:T], start=True, stop=False)
                    last = mm(b[:, i * T + P:(i + 1) * T], rv[:, 1, c], scT[:, hd, T:3 * P], start=False, stop=True)
                last.then_inc(unit_done, 1)
            pe.wait_ge(ld["gate0"], 16)
            for n in range(4):
                to_T(f"ga{n}", W[0], (2 * P * n, 2 * P * n + P))
            for n in range(2):
                b = begin(f"ms{n}")
                unit_saved(pe, f"ro{n}")
                mm(b[:, :], mix("mean"), rsq[:, 2 * n:2 * n + 2].rearrange("p k n -> p (k n)"), start=True, stop=True).then_inc(unit_done, 1)
            pe.wait_ge(probs_made, 2)
            for hd in range(FOX_HEADS):
                transposes(f"pt{hd}", [probs0[:, hd], probs1[:, hd, 0:P], probs1[:, hd, P:T]])
            pe.wait_ge(ld["gate1"], 16)
            for n in range(4):
                to_T(f"gb{n}", W[1], (2 * P * n, 2 * P * n + P))
            unit_saved(pe, "pt6")
            unit_saved(pe, "pt7")
            for n in range(2):
                b = begin(f"fo{n}")
                for i in range(2):
                    for s in range(2):
                        hd = 2 * (2 * n + i) + s
                        mm(b[:, i * T:(i + 1) * T], vz[:, 0, hd], probsT[:, hd, 0:T], start=(s == 0), stop=False)
                        last = mm(b[:, i * T + P:(i + 1) * T], vz[:, 1, hd], probsT[:, hd, T:3 * P], start=False, stop=(s == 1))
                last.then_inc(unit_done, 1)
            pe.wait_ge(ld["branch"], 16)
            unit_saved(pe, "fo1")
            for n in range(4):
                to_T(f"pr{n}", W[2], (2 * P * n, 2 * P * n + P), foxT, 4)
            pe.wait_ge(ro_made, 2)
            for n in range(4):
                to_T(f"pr{4 + n}", W[2][:, 4:8], (2 * P * n, 2 * P * n + P), roT, 4)
            pe.wait_ge(ld["out"], 16)
            unit_saved(pe, "pr7")
            for n in range(4):
                to_tokens(f"out{n}", W[3], n // 2, 512 * (n % 2), gates)
            pe.wait_ge(hn_made, 2)
            for n in range(4):
                transposes(f"ht{n}", [hn[:, t, k * P:(k + 1) * P] for k in (2 * n, 2 * n + 1) for t in range(TT)])
            for n in range(4):
                unit_saved(pe, f"ht{n}")
            b = begin("rl")
            pe.wait_ge(s_wrouter, 16)
            for t in range(TT):
                for k in range(KT):
                    last = mm(b[:, E * t:E * (t + 1)], xnT[:, k, tok(t)], wrout[:, k], start=(k == 0), stop=(k == KT - 1))
            last.then_inc(unit_done, 1)
            b = begin("pos")
            pe.wait_ge(sel_made, 1)
            mm(b[:, 0:E], tri[:, 0:P], sel[:, 0], start=True, stop=True)
            mm(b[:, E:2 * E], ones, sel[:, 0], start=True, stop=False)
            mm(b[:, E:2 * E], tri[:, 0:P], sel[:, 1], start=False, stop=True)
            mm(b[:, 2 * E:3 * E], ones, sel[:, 0], start=True, stop=False)
            mm(b[:, 2 * E:3 * E], ones, sel[:, 1], start=False, stop=True).then_inc(unit_done, 1)
            pe.wait_ge(w_made, 1)
            transposes("wt", [wp[:, t] for t in range(TT)])
            for n in range(len(UNITS) - 8, len(UNITS)):
                unit_saved(pe, UNITS[n][0])
            pe.wait_ge(ld["b_down"], 16)
            for n in range(4):
                last = mm(bank[n][:, :], combT[:, tok(n // 2)], bdown[:, 512 * (n % 2):512 * (n % 2 + 1)],
                          start=True, stop=False, skip_group_check=True)
            last.then_inc(acc_begun, 1)

            def gather(done, banks, wait_second=None):
                for n in range(2):
                    if n and wait_second:
                        wait_second()
                    for i in range(4):
                        k = 4 * n + i
                        for t in range(TT):
                            last = mm(bank[banks[n]][:, i * P:(i + 1) * P], hn[:, t, k * P:(k + 1) * P], hot[:, t],
                                      start=(t == 0), stop=(t == TT - 1))
                    last.then_inc(done, 1)

            def gate_up(b, w, tiles, first, rhs, width, done):
                for r in range(2):
                    for i in range(tiles):
                        c = 2 * P * (first + i) + r
                        o = (r * tiles + i) * width
                        for k in range(KT):
                            last = mm(b[:, o:o + width], w[:, k, c:c + 2 * P - 1:2], rhs[:, k],
                                      start=(k == 0), stop=(k == KT - 1))
                last.then_inc(done, 1)

            def comb_transpose(done):
                for t in range(TT):
                    last = nc.tensor.transpose(bank[5][:, tok(t)], comb[:, t], ident)
                last.then_inc(done, 1)

            def y_transpose(banks, done):
                for n in range(2):
                    for i in range(4):
                        last = nc.tensor.transpose(bank[banks[n]][:, i * P:(i + 1) * P], yT[:, 4 * n + i], ident)
                    last.then_inc(done, 1)

            def scatter():
                for n in range(4):
                    last = mm(bank[n][:, :], combT[:, tok(n // 2)], Y[:, 512 * (n % 2):512 * (n % 2 + 1)],
                              start=False, stop=False, skip_group_check=True)
                return last

            def finish_pair(p):
                pe.wait_ge(y_saved, 2 * p + 2)
                pe.wait_ge(ct_saved, p + 1)
                return scatter()

            def pair(p, first, last):
                def units(u):
                    pe.wait_ge(ld_gu[u], 16 * p + 16)
                    half = u // 2
                    gate_up(bank[4 + u % 2], W[u], 4, 0, xg[:, :, SLOTS * half:SLOTS * (half + 1)], SLOTS, gu_done)

                def down(half):
                    for n in range(2):
                        pe.wait_ge(ld_dn[n], 32 * p + 16 * (half + 1))
                        for i in range(4):
                            o = (4 * n + i) * SLOTS
                            for k in range(FT):
                                ins = mm(bank[6][:, o:o + SLOTS], half_down[n][:, k, i * P:(i + 1) * P],
                                         act2[:, half, k], start=(k == 0), stop=(k == FT - 1))
                        ins.then_inc(dn_done, 1)

                pe.wait_ge(xg_saved, 2 * p + 2)
                units(0)
                if not first:
                    pe.wait_ge(yt_saved, 2 * p)
                    y_transpose((6, 7), yt_done)
                    pe.wait_ge(ct_saved, p)
                units(1)
                if not first:
                    finish_pair(p - 1)
                pe.wait_ge(act_made, 4 * p + 1)
                units(2)
                pe.wait_ge(act_made, 4 * p + 2)
                down(0)
                units(3)
                if not last:
                    pe.wait_ge(hot_made, p + 2)
                    gather(gather_done, (7, 4), lambda: pe.wait_ge(act_made, 4 * p + 3))
                pe.wait_ge(yt_saved, 2 * p + 1)
                pe.wait_ge(act_made, 4 * p + 4)
                down(1)
                pe.wait_ge(comb_made, p + 1)
                comb_transpose(ct_done)

            pe.wait_ge(hot_made, 1)
            gather(gather_done, (7, 4))
            pair(0, True, False)
            with pe.Fori(1, PAIRS - 1) as p:
                pair(p, False, False)
            pair(PAIRS - 1, False, True)
            pe.wait_ge(yt_saved, 2 * PAIRS)
            y_transpose((6, 7), yt_done)
            finish_pair(PAIRS - 1).then_inc(job_pe, 1)

            pe.wait_ge(jobs_made, 1)
            n_jobs = pe.value_load(jobs_i[0:1, MAX_JOBS:MAX_JOBS + 1], min_val=0, max_val=MAX_JOBS)
            with pe.Fori(0, MAX_JOBS) as j:
                with pe.If(j < n_jobs):
                    act0, dve0 = j * ACT_JOB_STEPS, j * DVE_JOB_STEPS
                    pe.wait_ge(job_dve, dve0 + 1)
                    gather(job_pe, (7, 4))
                    comb_transpose(job_pe)
                    pe.wait_ge(ld_job, j * 64 + 64)
                    pe.wait_ge(job_act, act0 + ACT_AT["xg"] + 2)
                    pe.wait_ge(job_dve, dve0 + DVE_AT["comb"] + 1)
                    for u in range(4):
                        if u >= 2:
                            pe.wait_ge(job_dve, dve0 + DVE_AT["gu"] + 2 * (u - 1))
                        gate_up(bank[4 + u % 2], W[2 + u // 2], 2, 2 * (u % 2), xg, P, job_pe)
                    pe.wait_ge(job_dve, dve0 + DVE_AT["gu"] + 8)
                    for n in range(2):
                        for i in range(4):
                            for k in range(FT):
                                ins = mm(bank[6 + n][:, i * P:(i + 1) * P], half_down[n][:, k, i * P:(i + 1) * P],
                                         act[:, k], start=(k == 0), stop=(k == FT - 1))
                        ins.then_inc(job_pe, 1)
                    pe.wait_ge(job_act, act0 + ACT_JOB_STEPS)
                    y_transpose((4, 5), job_pe)
                    pe.wait_ge(job_dve, dve0 + DVE_JOB_STEPS)
                    scatter().then_inc(job_pe, 1)

            pe.wait_ge(ld_tail["p"], 16)
            for k in range(2):
                for t in range(TT):
                    last = nc.tensor.transpose(bank[4][:, k * T + t * P:k * T + (t + 1) * P], prow[:, t, k * P:(k + 1) * P], ident)
            last.then_inc(tail_done, 1)
            pe.wait_ge(pT_saved, 1)
            pe.wait_ge(ld_tail["ple_proj"], 16)
            for n in range(4):
                for k in range(2):
                    last = mm(bank[PROJ_BANK[n]][:, :], pT[:, k, tok(n // 2)], wpp[:, k, 512 * (n % 2):512 * (n % 2 + 1)],
                              start=(k == 0), stop=(k == 1))
                last.then_inc(tail_done, 1)
            pe.wait_ge(h2_made, 4)
            pe.wait_ge(hn3_made, 2)
            for n in range(4):
                for i in range(4):
                    k, t = 2 * n + i // 2, i % 2
                    last = nc.tensor.transpose(bank[n][:, i * P:(i + 1) * P], hn3[:, t, k * P:(k + 1) * P], ident)
                last.then_inc(tail_done, 1)
            pe.wait_ge(ht_act, 2)
            pe.wait_ge(ht_dve, 2)
            pe.wait_ge(ld_tail["ple_gate"], 16)
            for n in range(4):
                for k in range(KT):
                    last = mm(bank[n][:, :], hn3T[:, k, tok(n // 2)], W[0][:, k, 512 * (n % 2):512 * (n % 2 + 1)],
                              start=(k == 0), stop=(k == KT - 1))
                last.then_inc(tail_done, 1)


_INS = ["x", "p", "mix_norm", "w_in", "b_forget", "w_branch", "w_merge_gate", "b_merge_gate", "w_out",
        "ffn_norm", "w_router", "b_router", "w_gate_up", "b_gate_up", "w_down", "b_down",
        "ple_norm", "w_ple_gate", "w_ple_proj", "final_norm"]


def kernel(**inputs):
    import concourse.bacc as _bacc
    from concourse.bass_utils import run_bass_kernel_spmd as _run

    nc = _bacc.Bacc("TRN2", target_bir_lowering=False, num_devices=1)
    data = {name: np.ascontiguousarray(inputs[name]) for name in _INS}
    data["t_main"], data["t_mix"] = tables()
    arrays, args = {}, {}
    for name, x in data.items():
        arrays[f"in_{name}"] = x
        args[name] = nc.dram_tensor(f"in_{name}", x.shape, mybir.dt.from_np(x.dtype), kind="ExternalInput").ap()
    shape = (1, T, D)
    out = nc.dram_tensor("out_0", shape, F32, kind="ExternalOutput").ap()
    build(nc, args, out, shape)
    r = _run(nc, [arrays], core_ids=[0])
    return r.results[0]["out_0"]
```

```python
import concourse.bass as bass
from concourse import mybir
from contextlib import ExitStack
import numpy as np

F32 = mybir.dt.float32
I32 = mybir.dt.int32
ALU = mybir.AluOpType
ACT = mybir.ActivationFunctionType
AX = mybir.AxisListType

P = 128
D = 1024
KT = D // P
T = 256
TT = T // P
FOX_HEADS, FOX_D = 8, 64
FOX_W = FOX_HEADS * FOX_D
RET_HEADS, RET_DK, RET_DV = 4, 64, 128
RET_QK_W = RET_HEADS * RET_DK
RET_V_W = RET_HEADS * RET_DV
BR_W = 512
E = 32
TOP_K = 4
FF = 1024
FT = FF // P
LIMIT, ALPHA = 7.0, 1.702
EPS = 1e-6
PLE = 256
CHUNK = 512
GU = 2 * FF // CHUNK
DN = D // CHUNK
SLOTS = 64
PAIRS = E // 2
ROUNDS = 2
MAX_JOBS = T * TOP_K // (SLOTS + 1)
C_FQ, C_FK, C_FV, C_FF = 0, FOX_W, 2 * FOX_W, 3 * FOX_W
C_RQ = C_FF + FOX_HEADS
C_RK = C_RQ + RET_QK_W
C_RV = C_RK + RET_QK_W
C_RG = C_RV + RET_V_W
CAUSAL_FILL = -1e30
ROOT_MAGIC = float(0x5f3759df)

MAIN_COLS = dict(ident=P, tri=2 * P, iota=P)
MIX_COLS = dict(cos=T, sin=T, rot=P, decay=RET_HEADS * 3 * P, mask=T, mean=P, la=1, lb=1,
                ra=FOX_HEADS, rb=FOX_HEADS)


def columns(spec):
    at, out = 0, {}
    for name, n in spec.items():
        out[name] = (at, at + n)
        at += n
    return out, at


MAIN_AT, MAIN_N = columns(MAIN_COLS)
MIX_AT, MIX_N = columns(MIX_COLS)


def tables():
    main = np.zeros((P, MAIN_N), np.float32)
    mix = np.zeros((P, MIX_N), np.float32)

    def put(table, at, name, value):
        a, b = at[name]
        table[:, a:b] = value

    i = np.arange(P)
    put(main, MAIN_AT, "ident", np.eye(P))
    put(main, MAIN_AT, "tri", np.concatenate([i[:, None] <= i[None, :], np.ones((P, P))], 1))
    put(main, MAIN_AT, "iota", i[None, :])
    half = RET_DK // 2
    inv = (np.float32(10000.0) ** (-np.arange(half, dtype=np.float32) / half)).astype(np.float32)
    ang = (inv[i % half][:, None] * np.arange(T, dtype=np.float32)[None, :]).astype(np.float32)
    put(mix, MIX_AT, "cos", np.cos(ang.astype(np.float64)))
    put(mix, MIX_AT, "sin", np.sin(ang.astype(np.float64)))
    rot = np.zeros((P, P))
    for m in range(P):
        if m % RET_DK < half:
            rot[m + half, m] = -1.0
        else:
            rot[m - half, m] = 1.0
    put(mix, MIX_AT, "rot", rot)
    lg = np.log1p(-np.exp2(-5.0 - np.arange(RET_HEADS)))
    key = i[:, None]
    for h in range(RET_HEADS):
        a = MIX_AT["decay"][0] + h * 3 * P
        gap = np.arange(T)[None, :] - key
        mix[:, a:a + T] = np.where(gap >= 0, np.exp(np.maximum(gap, 0) * lg[h]), 0)
        gap = i[None, :] - key
        mix[:, a + T:a + 3 * P] = np.where(gap >= 0, np.exp(np.maximum(gap, 0) * lg[h]), 0)
    mask = np.zeros((P, T))
    mask[:, P:] = np.where(i[None, :] <= i[:, None], 0.0, CAUSAL_FILL)
    put(mix, MIX_AT, "mask", mask)
    put(mix, MIX_AT, "mean", 1.0 / RET_DV)
    for h in range(FOX_HEADS):
        mix[h, MIX_AT["la"][0]] = 1.0
        mix[32 + h, MIX_AT["lb"][0]] = -1.0
        mix[32 + h, MIX_AT["ra"][0] + h] = 1.0
        mix[h, MIX_AT["rb"][0] + h] = 1.0
    return main, mix


UNITS = (
    [(f"xt{n}", "ad"[n % 2]) for n in range(4)]
    + [("bm", "d")]
    + [("q0", "a"), ("q1", "a"), ("k0", "d"), ("k1", "d")]
    + [("ff", "d"), ("v0", "d"), ("v1", "d")]
    + [("rq", "a"), ("rk", "a"), ("rv0", "a"), ("rotq", "d"), ("rotk", "d"), ("rv1", "a")]
    + [("rg0", "d"), ("rg1", "d"), ("cs", "d")]
    + [(f"rs{h}", "d") for h in range(4)]
    + [(f"fs{n}", "d") for n in range(6)]
    + [("ro0", "a"), ("ro1", "a")]
    + [(f"ga{n}", "a") for n in range(4)]
    + [(f"pt{h}", "ad"[h % 2]) for h in range(8)]
    + [("ms0", "d"), ("ms1", "d")]
    + [(f"gb{n}", "a") for n in range(4)]
    + [("fo0", "a"), ("fo1", "a")]
    + [(f"pr{n}", "d") for n in range(8)]
    + [(f"out{n}", "d") for n in range(4)]
    + [(f"ht{n}", "ad"[n % 2]) for n in range(4)]
    + [("rl", "d"), ("pos", "d"), ("wt", "d")]
)
NUMBER = {name: n for n, (name, _) in enumerate(UNITS)}
READER = dict(UNITS)
RANK = {}
for _eng in "ad":
    for _r, _name in enumerate([n for n, e in UNITS if e == _eng]):
        RANK[_name] = _r + 1

PROJ_BANK = (5, 6, 7, 4)
PE_AT = dict(gather=0, comb=2, gu=3, actT=7, down=9, scatter=11)
PE_JOB_STEPS = 12
ACT_AT = dict(xg=0, sigmoid=2, actT=6)
ACT_JOB_STEPS = 8
DVE_AT = dict(hot=0, comb=1, gu=2, y=10)
DVE_JOB_STEPS = 12
TAIL_T, TAIL_G = 5, 9


class Chain:

    def __init__(self, eng, sem):
        self.eng, self.sem, self.origin, self.steps = eng, sem, 0, 0

    def link(self, ins):
        self.steps += 1
        ins.then_inc(self.sem, 1)
        self.eng.wait_ge(self.sem, self.origin + self.steps)

    def enter(self, i, first, per):
        self.before = self.origin + self.steps
        self.per = per
        self.origin, self.steps = (i - first) * per + self.before, 0

    def leave(self, rounds):
        assert self.steps == self.per, (self.steps, self.per)
        self.origin, self.steps = self.before + rounds * self.per, 0


def build(nc, a, out, out_shape):
    ctx = ExitStack()
    with ctx:
        def sem(name):
            return ctx.enter_context(nc.semaphore(name))

        def sb(name, cols, dt=F32):
            return ctx.enter_context(nc.sbuf_tensor(name, [P, cols], dt))

        bank = [ctx.enter_context(nc.psum_tensor(f"bank{n}", [P, 512], F32)) for n in range(8)]

        slot = [sb(f"slot{n}", 8 * 1024) for n in range(4)]
        down_slot = sb("down_slot", 8 * 1024)
        h_t = sb("h", TT * D)
        xnT_t = sb("xnT", KT * T)
        gates_t = sb("gates", 16 * T)
        fr_t = sb("branches", 8 * T)
        cmain = sb("cmain", MAIN_N)
        bgu = sb("b_gate_up", CHUNK)
        small = sb("small", 740)
        jobs_i = sb("jobs_i", 16, I32)

        def wview(s):
            return s[:, :].rearrange("p (k n) -> p k n", k=KT)

        W = [wview(s) for s in slot]

        def halves(s):
            return [s[:, 4096 * n:4096 * (n + 1)].rearrange("p (k n) -> p k n", k=KT) for n in range(2)]

        gu_slot = [halves(s) for s in slot]
        dn_slot = halves(down_slot)
        h = h_t[:, :].rearrange("p (t n) -> p t n", t=TT)
        xnT = xnT_t[:, :].rearrange("p (k n) -> p k n", k=KT)
        gates = gates_t[:, :].rearrange("p (k n) -> p k n", k=16)
        foxT = fr_t[:, 0:1024].rearrange("p (k n) -> p k n", k=4)
        roT = fr_t[:, 1024:2048].rearrange("p (k n) -> p k n", k=4)

        def main(name):
            return cmain[:, MAIN_AT[name][0]:MAIN_AT[name][1]]

        ident, tri, iota = main("ident"), main("tri"), main("iota")
        ones = tri[:, P:2 * P]

        taken = [0]

        def cut(n):
            taken[0] += n
            assert taken[0] <= small.shape[1], taken
            return small[:, taken[0] - n:taken[0]]

        lf = cut(2 * P).rearrange("p (t n) -> p t n", t=TT)
        wp = lf
        ffw = cut(KT * FOX_HEADS).rearrange("p (k n) -> p k n", k=KT)
        bfb = cut(FOX_HEADS)
        bmgT = cut(16)
        brb = cut(E)
        wrout = cut(KT * E).rearrange("p (k n) -> p k n", k=KT)
        zff = cut(16).rearrange("p (t n) -> p t n", t=TT)
        aff = cut(16).rearrange("p (t n) -> p t n", t=TT)
        ssq = cut(2)
        rstd = cut(2)
        newton = cut(2)
        mx = cut(16)
        sums = cut(16)
        m8 = cut(16).rearrange("p (t n) -> p t n", t=TT)
        nmax = cut(2)
        ngt = cut(2)
        jobf = cut(16)

        def region(t, start):
            at = [start]

            def take(n):
                at[0] += n
                assert at[0] <= t.shape[1], at
                return t[:, at[0] - n:at[0]]
            return take

        s3 = region(slot[3], 0)
        cmix = s3(MIX_N)

        def mix(name):
            return cmix[:, MIX_AT[name][0]:MIX_AT[name][1]]

        early = region(slot[3], MIX_N)
        gain_mix = early(D)
        xn = early(TT * D).rearrange("p (t n) -> p t n", t=TT)
        bmrows = early(P)
        vz = s3(TT * FOX_HEADS * P).rearrange("p (t h n) -> p t h n", t=TT, h=FOX_HEADS)
        rv = s3(TT * RET_V_W).rearrange("p (t n) -> p t n", t=TT)
        rqT = s3(2 * T).rearrange("p (k n) -> p k n", k=2)
        rkz = s3(RET_HEADS * T).rearrange("p (h n) -> p h n", h=RET_HEADS)
        L = s3(T)
        sd = region(down_slot, 0)
        qT = sd(4 * T).rearrange("p (k n) -> p k n", k=4)
        kz = sd(FOX_HEADS * T).rearrange("p (h n) -> p h n", h=FOX_HEADS)
        R = sd(FOX_HEADS * T).rearrange("p (h n) -> p h n", h=FOX_HEADS)
        probsT = sd(FOX_HEADS * 3 * P).rearrange("p (h n) -> p h n", h=FOX_HEADS)
        rr, rsq = kz[:, 0:4], kz[:, 4:8]
        rseed = R[:, 0:4]
        rraw = gates_t[:, 0:1024].rearrange("p (w k n) -> p w k n", w=2, k=2)
        rtmp = gates_t[:, 1024:1536].rearrange("p (k n) -> p k n", k=2)
        rgsig = gates_t[:, 1536:2048].rearrange("p (k n) -> p k n", k=2)
        scT = gates_t[:, 2048:2048 + 1536].rearrange("p (h n) -> p h n", h=RET_HEADS)
        probs1 = gates_t[:, 2048:4096].rearrange("p (h n) -> p h n", h=FOX_HEADS)
        probs0 = fr_t[:, 0:1024].rearrange("p (h n) -> p h n", h=FOX_HEADS)

        gain_ffn = fr_t[:, 0:1024]
        bdown = fr_t[:, 1024:2048]
        hn = gates_t[:, 0:2048].rearrange("p (t n) -> p t n", t=TT)
        xg = gates_t[:, 2048:3072].rearrange("p (k s) -> p k s", k=KT)
        actT = gates_t[:, 3072:4096].rearrange("p (k s) -> p k s", k=FT)
        act = fr_t[:, 0:1024]
        Y = fr_t[:, 1024:2048]
        mo = region(xnT_t, 0)
        hot = mo(2 * P).rearrange("p (t s) -> p t s", t=TT)
        comb = mo(2 * P).rearrange("p (t s) -> p t s", t=TT)
        combT = small[:, 0:T]
        gl = mo(512)
        ex = mo(256)
        posm = mo(2 * E).rearrange("p (t e) -> p t e", t=TT)
        wr = mo(2 * E).rearrange("p (t e) -> p t e", t=TT)
        posq = mo(TT * E * ROUNDS).rearrange("p (t e r) -> p t e r", t=TT, e=E)
        ind = mo(GU * P).rearrange("p (n s) -> p n s", n=GU)
        jobrow = wrout.rearrange("p k n -> p (k n)")
        jf, jscan, jtmp = jobrow[:, 0:64], jobrow[:, 64:128], jobrow[:, 128:192]
        lg = gl[:, 0:64].rearrange("p (t e) -> p t e", t=TT)
        gt = gl[:, 64:128].rearrange("p (t e) -> p t e", t=TT)
        eq = gl[:, 128:192].rearrange("p (t e) -> p t e", t=TT)
        cum = gl[:, 192:256].rearrange("p (t e) -> p t e", t=TT)
        sel = gl[:, 256:320].rearrange("p (t e) -> p t e", t=TT)
        ew = gl[:, 320:384].rearrange("p (t e) -> p t e", t=TT)

        tail = region(slot[1], 0)
        wpp = tail(2 * D).rearrange("p (k n) -> p k n", k=2)
        prow = tail(TT * PLE).rearrange("p (t n) -> p t n", t=TT)
        gain_ple = tail(D)
        gain_fin = tail(D)
        pT = tail(2 * T).rearrange("p (k n) -> p k n", k=2)
        hn3 = tail(TT * D).rearrange("p (t n) -> p t n", t=TT)
        sig = tail(D).rearrange("p (w n) -> p w n", w=2)
        hn3T = gates_t[:, 0:2048].rearrange("p (k n) -> p k n", k=KT)

        s_x, s_cmain, s_cmix, s_gain = sem("x_loaded"), sem("cmain_loaded"), sem("cmix_loaded"), sem("gain_loaded")
        s_ffw, s_bf, s_br = sem("ffw_loaded"), sem("b_forget_loaded"), sem("b_router_loaded")
        s_wrouter = sem("w_router_loaded")
        s_bias = sem("bias_rows_loaded")
        s_bgu = sem("b_gate_up_loaded")
        s_zero = sem("pool_zeroed")
        ld = {k: sem(f"loaded_{k}") for k in
              ("q", "k", "v", "rqk", "rvg", "gate0", "gate1", "branch", "out", "gain_ffn", "b_down")}
        unit_done = sem("unit_done")
        act_freed = sem("act_freed")
        dve_freed = sem("dve_freed")
        freed = {"a": act_freed, "d": dve_freed}
        dve_step, act_step = sem("dve_step"), sem("act_step")
        ssq_made = sem("sum_of_squares_made")
        xn_made = sem("xn_made")
        log1p_made = sem("log1p_made")
        zff_made = sem("forget_logits_made")
        lf_made = sem("log_forget_made")
        rgsig_made = sem("rg_sigmoid_made")
        rot_made = sem("rotary_made")
        max_made, probs_exp, probs_made = sem("row_max_made"), sem("probs_exp_made"), sem("probs_made")
        ro_made = sem("retention_made")
        rseed_made = sem("retention_root_begun")
        hn_made = sem("hn_made")
        sel_made, top_made, rexp_made, w_made = sem("selection_made"), sem("router_max_made"), sem("router_exp_made"), sem("routing_weights_made")
        wt_saved = sem("weights_T_saved")
        jobs_made = sem("jobs_made")
        acc_begun = sem("accumulators_begun")
        ld_gu = [sem(f"gate_up_loaded{n}") for n in range(GU)]
        ld_dn = sem("down_loaded")
        gu_done = sem("gate_up_done")
        dn_done = sem("down_done")
        gather_done = sem("gather_done")
        ct_done = sem("comb_transposed")
        at_done = sem("act_transposed")
        hot_made, comb_made, ind_made = sem("one_hot_made"), sem("comb_made"), sem("bias_picker_made")
        clipped, act_made = sem("glu_clipped"), sem("act_made")
        ct_saved, y_saved = sem("combT_saved"), sem("y_saved")
        sig_done = sem("glu_sigmoid_made")
        xg_saved, at_saved = sem("xg_saved"), sem("actT_saved")
        ld_job = sem("job_weights_loaded")
        job_pe, job_act, job_dve = sem("job_pe_step"), sem("job_act_step"), sem("job_dve_step")
        ld_tail = {k: sem(f"loaded_{k}") for k in ("ple_gate", "ple_proj", "p", "gain_ple", "gain_fin")}
        tail_done, tail_step = sem("tail_unit_done"), sem("dve_tail_step")
        pT_saved, h2_made, hn3_made, ht_act, ht_dve = sem("pT_saved"), sem("h2_made"), sem("hn3_made"), sem("hn3T_saved_by_act"), sem("hn3T_saved_by_dve")
        ple_sig, sig_made, ssq_tail = sem("ple_sigmoid_made"), sem("ple_gate_used"), sem("tail_squares_made")
        y_made, stored = sem("y_made"), sem("stored")

        gu_w = a["w_gate_up"][0].rearrange("e (k p) n -> e p k n", p=P)
        dn_w = a["w_down"][0].rearrange("e (k p) n -> e p k n", p=P)

        def rows(w):
            return w.rearrange("(k p) n -> p k n", p=P)

        w_in = rows(a["w_in"][0])
        w_mg = rows(a["w_merge_gate"][0])
        w_br = a["w_branch"][0].rearrange("g (c p) n -> p (g c) n", p=P)
        x_rows = a["x"][0].rearrange("(t p) n -> p t n", p=P)
        out_rows = out[0].rearrange("(t p) n -> p t n", p=P)
        tok = lambda t: slice(t * P, (t + 1) * P)

        def unit_ready(eng, name):
            eng.wait_ge(unit_done, NUMBER[name] + 1)

        def unit_saved(eng, name):
            eng.wait_ge(freed[READER[name]], RANK[name])

        def ubank(name):
            return bank[(NUMBER[name] + 4) % 8]

        block = ctx.enter_context(nc.Block())

        @block.sync
        def _(sp):
            sp.dma_start(h, x_rows).then_inc(s_x, 16)
            sp.dma_start(cmain[:, :], a["t_main"]).then_inc(s_cmain, 16)
            sp.dma_start(W[0][:, :, 0:512], w_in[:, :, C_FQ:C_FK]).then_inc(ld["q"], 16)
            sp.dma_start(W[0][:, :, 512:1024], w_in[:, :, C_FK:C_FV]).then_inc(ld["k"], 16)
            sp.dma_start(W[1][:, :, 0:512], w_in[:, :, C_FV:C_FF]).then_inc(ld["v"], 16)
            sp.dma_start(W[1][:, :, 512:1024], w_in[:, :, C_RQ:C_RV]).then_inc(ld["rqk"], 16)
            sp.dma_start(W[2], w_in[:, :, C_RV:C_RG + RET_V_W]).then_inc(ld["rvg"], 16)
            unit_ready(sp, "k1")
            sp.dma_start(W[0], w_mg[:, :, 0:D]).then_inc(ld["gate0"], 16)
            unit_ready(sp, "rk")
            sp.dma_start(W[1], w_mg[:, :, D:2 * D]).then_inc(ld["gate1"], 16)
            unit_ready(sp, "rg1")
            sp.dma_start(W[2], w_br).then_inc(ld["branch"], 16)
            def load_gate_up(n, a0):
                for half in range(2):
                    sp.dma_start(gu_slot[n][half], gu_w[a0 + half][:, :, CHUNK * n:CHUNK * (n + 1)]).then_inc(ld_gu[n], 16)

            def load_down(n, a0):
                for half in range(2):
                    sp.dma_start(dn_slot[half], dn_w[a0 + half][:, :, CHUNK * n:CHUNK * (n + 1)]).then_inc(ld_dn, 16)

            unit_ready(sp, "ga3")
            load_gate_up(0, 0)
            unit_ready(sp, "gb3")
            load_gate_up(1, 0)
            unit_ready(sp, "fo1")
            sp.wait_ge(ro_made, 2)
            sp.dma_start(W[3], rows(a["w_out"][0])).then_inc(ld["out"], 16)
            load_down(0, 0)
            unit_ready(sp, "pr7")
            sp.dma_start(gain_ffn, a["ffn_norm"].to_broadcast([P, D])).then_inc(ld["gain_ffn"], 16)
            load_gate_up(2, 0)
            sp.wait_ge(s_zero, 6)
            sp.dma_start(bdown[0:E, :], a["b_down"][0]).then_inc(ld["b_down"], 16)
            unit_ready(sp, "out3")
            load_gate_up(3, 0)

            def next_gate_up(n, p):
                sp.wait_ge(gu_done, GU * p + (n + 1))
                load_gate_up(n, 2 * p + 2)

            def rest_of_down(p):
                sp.wait_ge(dn_done, DN * p + 1)
                load_down(1, 2 * p)

            def next_down(p):
                sp.wait_ge(dn_done, DN * p + 2)
                load_down(0, 2 * p + 2)

            next_gate_up(0, 0)
            next_gate_up(1, 0)
            next_gate_up(2, 0)
            rest_of_down(0)
            next_gate_up(3, 0)
            next_down(0)
            with sp.Fori(1, PAIRS - 1) as p:
                next_gate_up(0, p)
                next_gate_up(1, p)
                rest_of_down(p)
                next_gate_up(2, p)
                next_gate_up(3, p)
                next_down(p)
            last = PAIRS - 1
            sp.wait_ge(gu_done, GU * last + 1)
            sp.dma_start(W[0], rows(a["w_ple_gate"][0])).then_inc(ld_tail["ple_gate"], 16)
            rest_of_down(last)
            sp.wait_ge(gu_done, GU * last + 2)
            sp.dma_start(prow, a["p"][0, 0].rearrange("(t p) n -> p t n", p=P)).then_inc(ld_tail["p"], 16)
            sp.dma_start(wpp, a["w_ple_proj"][0].rearrange("(k p) n -> p k n", p=P)).then_inc(ld_tail["ple_proj"], 16)
            sp.dma_start(gain_ple, a["ple_norm"].to_broadcast([P, D])).then_inc(ld_tail["gain_ple"], 16)
            sp.dma_start(gain_fin, a["final_norm"].rearrange("(a n) -> a n", a=1).to_broadcast([P, D])).then_inc(ld_tail["gain_fin"], 16)
            sp.wait_ge(gu_done, GU * PAIRS)
            sp.wait_ge(dn_done, DN * PAIRS)
            sp.wait_ge(jobs_made, 1)
            n_jobs = sp.value_load(jobs_i[0:1, MAX_JOBS:MAX_JOBS + 1], min_val=0, max_val=MAX_JOBS)
            with sp.Fori(0, MAX_JOBS) as j:
                with sp.If(j < n_jobs):
                    q = sp.value_load(jobs_i[0:1, bass.ds(j, 1)], min_val=0, max_val=E * ROUNDS - 1)
                    e = sp.snap(q // 2)
                    sp.wait_ge(job_pe, j * PE_JOB_STEPS + 1)
                    for n in range(GU):
                        sp.dma_start(gu_slot[2 + n // 2][n % 2], gu_w[e][:, :, CHUNK * n:CHUNK * (n + 1)]).then_inc(ld_job, 16)
                    for n in range(DN):
                        sp.dma_start(dn_slot[n], dn_w[e][:, :, CHUNK * n:CHUNK * (n + 1)]).then_inc(ld_job, 16)
            for t in range(TT):
                sp.wait_ge(y_made, t + 1)
                sp.dma_start(out_rows[:, t], hn3[:, t]).then_inc(stored, 16)
            sp.wait_ge(stored, 16 * TT)

        @block.gpsimd
        def _(pool):
            nc.gpsimd.memset(bmrows, 0.0).then_inc(s_zero, 1)
            pool.wait_ge(s_zero, 1)
            pool.dma_start(bmrows[0:16, :], a["b_merge_gate"].rearrange("a (r n) -> (a r) n", r=16)).then_inc(s_bias, 16)
            nc.gpsimd.memset(kz, 0.0).then_inc(s_zero, 1)
            nc.gpsimd.memset(small[:, 0:2 * P], 0.0).then_inc(s_zero, 1)
            unit_ready(pool, "bm")
            nc.gpsimd.memset(slot[3][:, MIX_N:MIX_N + TT * FOX_HEADS * P], 0.0).then_inc(s_zero, 1)
            nc.gpsimd.memset(rkz, 0.0).then_inc(s_zero, 1)
            unit_ready(pool, "pr7")
            nc.gpsimd.memset(bdown, 0.0).then_inc(s_zero, 1)

        @block.scalar
        def _(actE):
            chain = Chain(actE, act_step)
            link = chain.link

            def copy(o, i, scale=1.0):
                return nc.scalar.activation(o, i, ACT.Copy, scale=scale)

            actE.dma_start(gain_mix, a["mix_norm"].to_broadcast([P, D])).then_inc(s_gain, 16)
            actE.dma_start(cmix, a["t_mix"]).then_inc(s_cmix, 16)
            with nc.allow_non_contiguous_dma(reason="eight columns of w_in"):
                actE.dma_start(ffw, w_in[:, :, C_FF:C_RQ]).then_inc(s_ffw, 16)
            actE.dma_start(bfb, a["b_forget"].to_broadcast([P, FOX_HEADS])).then_inc(s_bf, 16)
            actE.dma_start(wrout, rows(a["w_router"][0])).then_inc(s_wrouter, 16)
            for n in range(GU):
                actE.dma_start(bgu[E * n:E * (n + 1), :], a["b_gate_up"][0][:, CHUNK * n:CHUNK * (n + 1)]).then_inc(s_bgu, 16)
            actE.dma_start(brb, a["b_router"].to_broadcast([P, E])).then_inc(s_br, 16)

            def squares(t, junk, done):
                nc.scalar.activation(junk, h[:, t], ACT.Square, accum_out=ssq[:, t:t + 1]).then_inc(done, 1)

            actE.wait_ge(s_x, 16)
            for t in range(TT):
                squares(t, xn[:, t], ssq_made)
            for n in (0, 2):
                unit_ready(actE, f"xt{n}")
                copy(xnT[:, 2 * n:2 * n + 2], ubank(f"xt{n}")[:, :].rearrange("p (k n) -> p k n", k=2)).then_inc(act_freed, 1)
            for n in range(2):
                unit_ready(actE, f"q{n}")
                copy(qT[:, 2 * n:2 * n + 2], ubank(f"q{n}")[:, :].rearrange("p (k n) -> p k n", k=2),
                     FOX_D ** -0.5).then_inc(act_freed, 1)
            actE.wait_ge(zff_made, 1)
            link(nc.scalar.activation(aff, aff, ACT.Exp))
            nc.scalar.activation(aff, aff, ACT.Ln, bias=1.0).then_inc(log1p_made, 1)
            for n, name in enumerate(("rq", "rk")):
                unit_ready(actE, name)
                copy(rraw[:, n], ubank(name)[:, :].rearrange("p (k n) -> p k n", k=2),
                     (1.0, RET_DK ** -0.5)[n]).then_inc(act_freed, 1)
            for t in range(TT):
                unit_ready(actE, f"rv{t}")
                copy(rv[:, t], ubank(f"rv{t}")[:, :]).then_inc(act_freed, 1)
            for n in range(2):
                unit_ready(actE, f"rg{n}")
                if n:
                    unit_saved(actE, "rg0")
                nc.scalar.activation(rgsig, ubank(f"rg{n}")[:, :].rearrange("p (k n) -> p k n", k=2),
                                     ACT.Sigmoid).then_inc(rgsig_made, 1)

            for b, pr in enumerate((probs0, probs1)):
                actE.wait_ge(max_made, b + 1)
                for hd in range(FOX_HEADS):
                    c = 8 * b + hd
                    last = nc.scalar.activation(pr[:, hd], pr[:, hd], ACT.Exp, bias=mx[:, c:c + 1],
                                                accum_out=sums[:, c:c + 1])
                last.then_inc(probs_exp, 1)
            for n in range(2):
                unit_ready(actE, f"ro{n}")
                v = ubank(f"ro{n}")[:, :].rearrange("p (k n) -> p k n", k=2)
                copy(rr[:, 2 * n:2 * n + 2], v)
                nc.scalar.activation(rsq[:, 2 * n:2 * n + 2], v, ACT.Square).then_inc(act_freed, 1)

            def gate(name, first):
                unit_ready(actE, name)
                for k in range(2):
                    last = nc.scalar.activation(gates[:, first + k], ubank(name)[:, k * T:(k + 1) * T],
                                                ACT.Sigmoid, bias=bmgT[:, first + k:first + k + 1])
                last.then_inc(act_freed, 1)

            actE.wait_ge(rot_made, 2)
            unit_saved(actE, "rg1")
            for n in range(4):
                gate(f"ga{n}", 2 * n)
            for hd in range(0, FOX_HEADS, 2):
                unit_ready(actE, f"pt{hd}")
                copy(probsT[:, hd], ubank(f"pt{hd}")[:, 0:3 * P]).then_inc(act_freed, 1)
            for n in range(2):
                unit_saved(actE, f"ms{n}")
                y = rseed[:, 2 * n:2 * n + 2]
                link(nc.scalar.activation(y, rsq[:, 2 * n:2 * n + 2], ACT.Ln))
                nc.scalar.activation(y, y, ACT.Exp, scale=-0.5).then_inc(rseed_made, 1)
            for n in range(4):
                gate(f"gb{n}", 8 + 2 * n)
            for n in range(2):
                unit_ready(actE, f"fo{n}")
                copy(foxT[:, 2 * n:2 * n + 2], ubank(f"fo{n}")[:, :].rearrange("p (k n) -> p k n", k=2)).then_inc(act_freed, 1)

            unit_ready(actE, "out3")
            for t in range(TT):
                unit_saved(actE, f"out{2 * t + 1}")
                squares(t, hn[:, t], ssq_made)
            for n in (0, 2):
                unit_ready(actE, f"ht{n}")
                copy(xnT[:, 2 * n:2 * n + 2], ubank(f"ht{n}")[:, :].rearrange("p (k n) -> p k n", k=2)).then_inc(act_freed, 1)
            actE.wait_ge(top_made, 1)
            for t in range(TT):
                nc.scalar.activation(ew[:, t], lg[:, t], ACT.Exp, bias=nmax[:, t:t + 1]).then_inc(rexp_made, 1)

            def save_gathered(p):
                for n, b in enumerate((7, 4)):
                    actE.wait_ge(gather_done, 2 * p + (n + 1))
                    copy(xg[:, 4 * n:4 * n + 4], bank[b][:, :].rearrange("p (k s) -> p k s", k=4)).then_inc(xg_saved, 1)

            def pair(p, last):
                def sigmoid(n):
                    actE.wait_ge(clipped, GU * p + (n + 1))
                    nc.scalar.activation(ex, gl[:, 0:256], ACT.Sigmoid, scale=ALPHA).then_inc(sig_done, 1)

                def save_activations(n):
                    actE.wait_ge(at_done, 2 * p + (n + 1))
                    copy(actT[:, 4 * n:4 * n + 4], bank[6][:, :].rearrange("p (k s) -> p k s", k=4)).then_inc(at_saved, 1)

                sigmoid(0)
                sigmoid(1)
                sigmoid(2)
                save_activations(0)
                sigmoid(3)
                save_activations(1)
                if not last:
                    save_gathered(p + 1)

            save_gathered(0)
            pair(0, False)
            with actE.Fori(1, PAIRS - 1) as p:
                pair(p, False)
            pair(PAIRS - 1, True)

            n_jobs = actE.value_load(jobs_i[0:1, MAX_JOBS:MAX_JOBS + 1], min_val=0, max_val=MAX_JOBS)
            with actE.Fori(0, MAX_JOBS) as j:
                with actE.If(j < n_jobs):
                    pe0, dve0 = j * PE_JOB_STEPS + 1, j * DVE_JOB_STEPS
                    for n, b in enumerate((7, 4)):
                        actE.wait_ge(job_pe, pe0 + PE_AT["gather"] + (n + 1))
                        copy(xg[:, 4 * n:4 * n + 4], bank[b][:, :].rearrange("p (k s) -> p k s", k=4)).then_inc(job_act, 1)
                    for n in range(GU):
                        actE.wait_ge(job_dve, dve0 + DVE_AT["gu"] + (2 * n + 1))
                        nc.scalar.activation(ex, gl[:, 0:256], ACT.Sigmoid, scale=ALPHA).then_inc(job_act, 1)
                    for n in range(2):
                        actE.wait_ge(job_pe, pe0 + PE_AT["actT"] + (n + 1))
                        copy(actT[:, 4 * n:4 * n + 4], bank[6 + n][:, :].rearrange("p (k s) -> p k s", k=4)).then_inc(job_act, 1)

            actE.wait_ge(tail_done, 1)
            copy(pT, bank[4][:, :].rearrange("p (k n) -> p k n", k=2)).then_inc(pT_saved, 1)
            for t in range(TT):
                actE.wait_ge(h2_made, 2 * (t + 1))
                squares(t, hn3[:, t], ssq_tail)
            for n in (0, 2):
                actE.wait_ge(tail_done, TAIL_T + n + 1)
                copy(hn3T[:, 2 * n:2 * n + 2], bank[n][:, :].rearrange("p (k n) -> p k n", k=2)).then_inc(ht_act, 1)
            for n in range(4):
                actE.wait_ge(tail_done, TAIL_G + n + 1)
                if n >= 2:
                    actE.wait_ge(sig_made, n - 1)
                nc.scalar.activation(sig[:, n % 2], bank[n][:, :], ACT.Sigmoid).then_inc(ple_sig, 1)
                if n % 2:
                    t = n // 2
                    actE.wait_ge(sig_made, n + 1)
                    squares(t, hn3[:, t], ssq_tail)

        @block.vector
        def _(dve):
            chain = Chain(dve, dve_step)
            link = chain.link
            v = nc.vector

            def inverse_rms(c):
                x, y, w = ssq[:, c], rstd[:, c], newton[:, c]
                link(v.tensor_scalar(x, x, 1.0 / D, EPS, ALU.mult, ALU.add))
                link(v.tensor_scalar(y.bitcast(I32), x.bitcast(I32), -0.5, ROOT_MAGIC, ALU.mult, ALU.add))
                for _ in range(3):
                    link(v.tensor_tensor(w, y, y, ALU.mult))
                    link(v.scalar_tensor_tensor(out=w, in0=w, scalar=-0.5, in1=x, op0=ALU.mult, op1=ALU.mult))
                    link(v.scalar_tensor_tensor(out=y, in0=w, scalar=1.5, in1=y, op0=ALU.add, op1=ALU.mult))

            def two(b):
                return b[:, :].rearrange("p (k n) -> p k n", k=2)

            dve.wait_ge(ssq_made, TT)
            inverse_rms(slice(0, TT))
            dve.wait_ge(s_gain, 16)
            for t in range(TT):
                v.scalar_tensor_tensor(out=xn[:, t], in0=h[:, t], scalar=rstd[:, t:t + 1], in1=gain_mix,
                                       op0=ALU.mult, op1=ALU.mult).then_inc(xn_made, 1)
            for n in (1, 3):
                unit_ready(dve, f"xt{n}")
                v.tensor_copy(xnT[:, 2 * n:2 * n + 2], two(ubank(f"xt{n}"))).then_inc(dve_freed, 1)
            unit_ready(dve, "bm")
            v.tensor_copy(bmgT, ubank("bm")[:, 0:16]).then_inc(dve_freed, 1)
            dve.wait_ge(s_zero, 3)
            kz_p = kz.rearrange("p (t s) n -> p t s n", s=2)
            for n in range(2):
                unit_ready(dve, f"k{n}")
                for s in range(2):
                    last = v.tensor_copy(kz_p[64 * s:64 * s + 64, 2 * n:2 * n + 2, s],
                                         two(ubank(f"k{n}"))[64 * s:64 * s + 64])
                last.then_inc(dve_freed, 1)
            unit_ready(dve, "ff")
            dve.wait_ge(s_bf, 16)
            v.tensor_tensor(zff, ubank("ff")[:, 0:16].rearrange("p (t n) -> p t n", t=TT),
                            bfb.unsqueeze(1).to_broadcast([P, TT, FOX_HEADS]), ALU.add).then_inc(dve_freed, 1)
            unit_saved(dve, "ff")
            v.scalar_tensor_tensor(out=aff, in0=zff, scalar=-1.0, in1=zff,
                                   op0=ALU.mult, op1=ALU.min).then_inc(zff_made, 1)
            dve.wait_ge(s_zero, 5)
            for t in range(TT):
                unit_ready(dve, f"v{t}")
                src = ubank(f"v{t}")[:, :].rearrange("p (k s d) -> p k s d", s=2, d=FOX_D)
                dst = vz[:, t].rearrange("p (k s) n -> p k s n", s=2)
                for s in range(2):
                    last = v.tensor_copy(dst[:, :, s, FOX_D * s:FOX_D * (s + 1)], src[:, :, s])
                last.then_inc(dve_freed, 1)
            dve.wait_ge(log1p_made, 1)
            link(v.scalar_tensor_tensor(out=lf[:, :, 0:FOX_HEADS], in0=zff, scalar=0.0, in1=aff,
                                        op0=ALU.min, op1=ALU.subtract))
            v.tensor_copy(lf[:, :, 32:32 + FOX_HEADS], lf[:, :, 0:FOX_HEADS]).then_inc(lf_made, 1)
            dve.wait_ge(s_cmix, 16)
            sin2 = mix("sin").unsqueeze(1).to_broadcast([P, 2, T])
            cos2 = mix("cos").unsqueeze(1).to_broadcast([P, 2, T])
            rkz_p = rkz.rearrange("p (t s) n -> p t s n", s=2)
            for n, name in enumerate(("rotq", "rotk")):
                unit_ready(dve, name)
                v.tensor_tensor(rtmp, two(ubank(name)), sin2, ALU.mult).then_inc(dve_freed, 1)
                link(v.tensor_tensor(rraw[:, n], rraw[:, n], cos2, ALU.mult))
                if n == 0:
                    v.tensor_tensor(rqT, rraw[:, n], rtmp, ALU.add).then_inc(rot_made, 1)
                    dve.wait_ge(rot_made, 1)
                else:
                    for s in range(2):
                        hp = slice(64 * s, 64 * s + 64)
                        last = v.tensor_tensor(rkz_p[hp, :, s], rraw[hp, n], rtmp[hp], ALU.add)
                    last.then_inc(rot_made, 1)
            for n in range(2):
                dve.wait_ge(rgsig_made, n + 1)
                v.tensor_tensor(roT[:, 2 * n:2 * n + 2], rgsig, two(ubank(f"rg{n}")), ALU.mult).then_inc(dve_freed, 1)
            unit_ready(dve, "cs")
            cs = ubank("cs")[:, 0:T]
            v.tensor_scalar(L, cs, mix("la"), mix("lb"), ALU.mult, ALU.add)
            for hd in range(FOX_HEADS):
                last = v.tensor_scalar(R[:, hd], cs, mix("ra")[:, hd:hd + 1], mix("rb")[:, hd:hd + 1], ALU.mult, ALU.add)
            last.then_inc(dve_freed, 1)
            for hd in range(RET_HEADS):
                unit_ready(dve, f"rs{hd}")
                dec = mix("decay")[:, hd * 3 * P:(hd + 1) * 3 * P]
                v.tensor_tensor(scT[:, hd], ubank(f"rs{hd}")[:, 0:3 * P], dec, ALU.mult).then_inc(dve_freed, 1)
            m = mix("mask")
            for n in range(2):
                unit_ready(dve, f"fs{n}")
                v.tensor_tensor(probs0[:, 4 * n:4 * n + 4], ubank(f"fs{n}")[:, :].rearrange("p (k n) -> p k n", k=4),
                                m[:, P:2 * P].unsqueeze(1).to_broadcast([P, 4, P]), ALU.add).then_inc(dve_freed, 1)
            unit_saved(dve, "fs1")
            link(v.reduce_max(mx[:, 0:8], probs0, AX.X))
            v.tensor_scalar(mx[:, 0:8], mx[:, 0:8], -1.0, None, ALU.mult).then_inc(max_made, 1)
            unit_ready(dve, "ro1")
            for n in range(4):
                unit_ready(dve, f"fs{2 + n}")
                v.tensor_tensor(probs1[:, 2 * n:2 * n + 2], two(ubank(f"fs{2 + n}")),
                                m.unsqueeze(1).to_broadcast([P, 2, T]), ALU.add).then_inc(dve_freed, 1)
            unit_saved(dve, "fs5")
            link(v.reduce_max(mx[:, 8:16], probs1, AX.X))
            v.tensor_scalar(mx[:, 8:16], mx[:, 8:16], -1.0, None, ALU.mult).then_inc(max_made, 1)
            for b, pr in enumerate((probs0, probs1)):
                dve.wait_ge(probs_exp, b + 1)
                c = slice(8 * b, 8 * b + 8)
                link(v.reciprocal(sums[:, c], sums[:, c]))
                v.tensor_tensor(pr, pr, sums[:, c].unsqueeze(2).to_broadcast([P, FOX_HEADS, P * (b + 1)]),
                                ALU.mult).then_inc(probs_made, 1)
            for hd in range(1, FOX_HEADS, 2):
                unit_ready(dve, f"pt{hd}")
                v.tensor_copy(probsT[:, hd], ubank(f"pt{hd}")[:, 0:3 * P]).then_inc(dve_freed, 1)
            for n in range(2):
                unit_ready(dve, f"ms{n}")
                s2 = rsq[:, 2 * n:2 * n + 2]
                v.tensor_scalar(s2, two(ubank(f"ms{n}")), EPS, None, ALU.add).then_inc(dve_freed, 1)
                dve.wait_ge(rseed_made, n + 1)
                y = rseed[:, 2 * n:2 * n + 2]
                link(v.tensor_tensor(s2, s2, y, ALU.mult))
                link(v.tensor_tensor(s2, s2, y, ALU.mult))
                link(v.tensor_scalar(s2, s2, -0.5, 1.5, ALU.mult, ALU.add))
                link(v.tensor_tensor(s2, s2, y, ALU.mult))
                link(v.tensor_tensor(s2, s2, rr[:, 2 * n:2 * n + 2], ALU.mult))
                v.tensor_tensor(roT[:, 2 * n:2 * n + 2], roT[:, 2 * n:2 * n + 2], s2, ALU.mult).then_inc(ro_made, 1)
            unit_saved(dve, "gb3")
            for n in range(4):
                unit_ready(dve, f"pr{n}")
                g = gates[:, 2 * n:2 * n + 2]
                v.tensor_tensor(g, g, two(ubank(f"pr{n}")), ALU.mult).then_inc(dve_freed, 1)
            for n in range(4):
                unit_ready(dve, f"pr{4 + n}")
                g, g1 = gates[:, 2 * n:2 * n + 2], gates[:, 8 + 2 * n:10 + 2 * n]
                link(v.tensor_tensor(g1, g1, two(ubank(f"pr{4 + n}")), ALU.mult))
                v.tensor_tensor(g, g, g1, ALU.add).then_inc(dve_freed, 1)
            for n in range(4):
                unit_ready(dve, f"out{n}")
                o = h[:, n // 2, 512 * (n % 2):512 * (n % 2 + 1)]
                v.tensor_tensor(o, o, ubank(f"out{n}")[:, :], ALU.add).then_inc(dve_freed, 1)
            dve.wait_ge(ssq_made, 2 * TT)
            inverse_rms(slice(0, TT))
            dve.wait_ge(ld["gain_ffn"], 16)
            for t in range(TT):
                v.scalar_tensor_tensor(out=hn[:, t], in0=h[:, t], scalar=rstd[:, t:t + 1], in1=gain_ffn,
                                       op0=ALU.mult, op1=ALU.mult).then_inc(hn_made, 1)
            for n in (1, 3):
                unit_ready(dve, f"ht{n}")
                v.tensor_copy(xnT[:, 2 * n:2 * n + 2], two(ubank(f"ht{n}"))).then_inc(dve_freed, 1)
            unit_ready(dve, "rl")
            dve.wait_ge(s_br, 16)
            v.tensor_tensor(lg, ubank("rl")[:, 0:2 * E].rearrange("p (t e) -> p t e", t=TT),
                            brb.unsqueeze(1).to_broadcast([P, TT, E]), ALU.add).then_inc(dve_freed, 1)
            unit_saved(dve, "rl")
            for t in range(TT):
                link(v.max(m8[:, t], lg[:, t]))
            v.tensor_scalar(nmax.unsqueeze(2), m8[:, :, 0:1], -1.0, None, ALU.mult).then_inc(top_made, 1)
            thr = m8[:, :, TOP_K - 1:TOP_K].to_broadcast([P, TT, E])
            v.tensor_tensor(gt, lg, thr, ALU.is_gt)
            link(v.tensor_tensor(eq, lg, thr, ALU.is_equal))
            for t in range(TT):
                v.tensor_tensor_scan(cum[:, t], ones[:, 0:E], eq[:, t], 0.0, ALU.mult, ALU.add)
            link(v.reduce_sum(ngt, gt, AX.X))
            link(v.tensor_scalar(ngt, ngt, -1.0, float(TOP_K), ALU.mult, ALU.add))
            link(v.tensor_tensor(cum, cum, ngt.unsqueeze(2).to_broadcast([P, TT, E]), ALU.is_le))
            link(v.tensor_tensor(eq, eq, cum, ALU.mult))
            v.tensor_tensor(sel, gt, eq, ALU.add).then_inc(sel_made, 1)

            def one_hot(o, position, weight=None):
                for t in range(TT):
                    if weight is None:
                        last = v.tensor_scalar(o[t], iota[:, 0:o[t].shape[-1]], position(t), None, ALU.is_equal)
                    else:
                        last = v.tensor_scalar(o[t], iota[:, 0:o[t].shape[-1]], position(t), weight(t),
                                               ALU.is_equal, ALU.mult)
                return last

            def col(table, t, e):
                return table[:, t, bass.ds(e, 1)] if not isinstance(e, int) else table[:, t, e:e + 1]

            def pair_hot(p):
                for half in range(2):
                    s = slice(SLOTS * half, SLOTS * (half + 1))
                    last = one_hot([hot[:, t, s] for t in range(TT)], lambda t: col(posm, t, 2 * p + half))
                last.then_inc(hot_made, 1)

            def swiglu(psum, dst, clip_sem, done_sem, wait_sigmoid):
                glu, lin = gl[:, 0:256], gl[:, 256:512]
                v.tensor_scalar(glu, psum[:, 0:CHUNK:2], LIMIT, None, ALU.min).then_inc(clip_sem, 1)
                link(v.tensor_scalar(lin, psum[:, 1:CHUNK:2], LIMIT, -LIMIT, ALU.min, ALU.max))
                link(v.scalar_tensor_tensor(out=lin, in0=lin, scalar=1.0, in1=glu, op0=ALU.add, op1=ALU.mult))
                wait_sigmoid()
                v.tensor_tensor(dst, lin, ex, ALU.mult).then_inc(done_sem, 1)

            ident_n = ident.rearrange("p (n e) -> p n e", n=GU)

            def pair_picker(p):
                src = ident_n[:, :, bass.ds(2 * p, 2)] if not isinstance(p, int) else ident_n[:, :, 2 * p:2 * p + 2]
                v.tensor_copy(ind.rearrange("p n (w s) -> p n w s", w=2),
                              src.unsqueeze(3).to_broadcast([P, GU, 2, SLOTS])).then_inc(ind_made, 1)

            def pair(p, first, last):
                if not first:
                    dve.wait_ge(ct_done, p)
                for half in range(2):
                    s = slice(SLOTS * half, SLOTS * (half + 1))
                    ins = one_hot([comb[:, t, s] for t in range(TT)], lambda t: col(posm, t, 2 * p + half),
                                  lambda t: col(wr, t, 2 * p + half))
                ins.then_inc(comb_made, 1)
                if not last:
                    dve.wait_ge(gather_done, 2 * p + 2)
                    pair_hot(p + 1)
                for n in range(GU):
                    dve.wait_ge(gu_done, GU * p + (n + 1))
                    if not (first and n == 0):
                        dve.wait_ge(act_made, GU * p + n)
                    swiglu(bank[4 + n % 2], act[:, 256 * n:256 * (n + 1)], clipped, act_made,
                           lambda: dve.wait_ge(sig_done, GU * p + (n + 1)))
                if not last:
                    pair_picker(p + 1)
                if first:
                    dve.wait_ge(acc_begun, 1)
                save_down(p, 0)
                dve.wait_ge(ct_done, p + 1)
                v.tensor_copy(combT, bank[7][:, 0:T]).then_inc(ct_saved, 1)
                if first:
                    make_jobs()
                save_down(p, 1)

            def save_down(p, n):
                dve.wait_ge(dn_done, DN * p + (n + 1))
                v.tensor_copy(Y[:, CHUNK * n:CHUNK * (n + 1)], bank[5 + n][:, :]).then_inc(y_saved, 1)

            def make_jobs():
                link(v.tensor_tensor_scan(jscan, ones[:, 0:64], jf, 0.0, ALU.mult, ALU.add))
                link(v.tensor_copy(jobf[:, MAX_JOBS:MAX_JOBS + 1], jscan[:, 63:64]))
                link(v.tensor_tensor(jscan, jscan, jf, ALU.mult))
                for j in range(MAX_JOBS):
                    link(v.tensor_scalar(jtmp, jscan, float(j + 1), None, ALU.is_equal))
                    link(v.tensor_tensor(jtmp, jtmp, iota[:, 0:64], ALU.mult))
                    link(v.reduce_sum(jobf[:, j:j + 1], jtmp, AX.X))
                v.tensor_copy(jobs_i[:, :], jobf).then_inc(jobs_made, 1)

            unit_ready(dve, "pos")
            pos = ubank("pos")
            link(v.tensor_tensor(posm, pos[:, 0:2 * E].rearrange("p (t e) -> p t e", t=TT), sel, ALU.mult))
            link(v.tensor_scalar(posm, posm, -1.0, None, ALU.add))
            pair_hot(0)
            for r in range(ROUNDS):
                first = float(SLOTS + 2 * SLOTS * r)
                v.tensor_scalar(posq[:, :, :, r], posm, -first, None, ALU.add)
                last = v.tensor_scalar(jf.rearrange("p (e r) -> p e r", r=ROUNDS)[:, :, r], pos[:, 2 * E:3 * E],
                                       first, None, ALU.is_gt)
            last.then_inc(dve_freed, 1)
            dve.wait_ge(rexp_made, 2)
            link(v.tensor_tensor(ew, ew, sel, ALU.mult))
            link(v.reduce_sum(ngt, ew, AX.X))
            link(v.reciprocal(ngt, ngt))
            link(v.memset(small[:, 0:2 * P], 0.0))
            link(v.tensor_tensor(wr, ew, ngt.unsqueeze(2).to_broadcast([P, TT, E]), ALU.mult))
            v.tensor_copy(wp[:, :, 0:E], wr).then_inc(w_made, 1)
            pair_picker(0)
            unit_ready(dve, "wt")
            v.tensor_copy(combT, ubank("wt")[:, 0:T]).then_inc(dve_freed, 1)

            pair(0, True, False)
            with dve.Fori(1, PAIRS - 1) as p:
                chain.enter(p, 1, 2 * GU)
                pair(p, False, False)
                chain.leave(PAIRS - 2)
            pair(PAIRS - 1, False, True)

            dve.wait_ge(jobs_made, 1)
            n_jobs = dve.value_load(jobs_i[0:1, MAX_JOBS:MAX_JOBS + 1], min_val=0, max_val=MAX_JOBS)
            with dve.Fori(0, MAX_JOBS) as j:
                with dve.If(j < n_jobs):
                    chain.enter(j, 0, 2 * GU)
                    q = dve.value_load(jobs_i[0:1, bass.ds(j, 1)], min_val=0, max_val=E * ROUNDS - 1)
                    e = dve.snap(q // 2)
                    pe0, act0, dve0 = j * PE_JOB_STEPS + 1, j * ACT_JOB_STEPS, j * DVE_JOB_STEPS
                    dve.wait_ge(job_pe, pe0)
                    posf = posq.rearrange("p t e r -> p t (e r)")
                    one_hot([hot[:, t] for t in range(TT)], lambda t: col(posf, t, q))
                    one_hot([comb[:, t] for t in range(TT)], lambda t: col(posf, t, q),
                            lambda t: col(wr, t, e))
                    v.tensor_copy(ind, ident_n[:, :, bass.ds(e, 1)].to_broadcast([P, GU, P])).then_inc(job_dve, 1)
                    dve.wait_ge(job_pe, pe0 + PE_AT["comb"] + 1)
                    v.tensor_copy(combT, bank[5][:, 0:T]).then_inc(job_dve, 1)
                    for n in range(GU):
                        dve.wait_ge(job_pe, pe0 + PE_AT["gu"] + (n + 1))
                        dve.wait_ge(job_dve, dve0 + DVE_AT["gu"] + 2 * n)
                        swiglu(bank[4 + n % 2], act[:, 256 * n:256 * (n + 1)], job_dve, job_dve,
                               lambda: dve.wait_ge(job_act, act0 + ACT_AT["sigmoid"] + (n + 1)))
                    for n in range(DN):
                        dve.wait_ge(job_pe, pe0 + PE_AT["down"] + (n + 1))
                        v.tensor_copy(Y[:, CHUNK * n:CHUNK * (n + 1)], bank[4 + n][:, :]).then_inc(job_dve, 1)
                    chain.leave(MAX_JOBS)
            chain = Chain(dve, tail_step)
            link = chain.link

            dve.wait_ge(tail_done, 1)
            for n in range(4):
                o = h[:, n // 2, 512 * (n % 2):512 * (n % 2 + 1)]
                v.tensor_tensor(o, o, bank[n][:, :], ALU.add).then_inc(h2_made, 1)
            dve.wait_ge(ssq_tail, TT)
            inverse_rms(slice(0, TT))
            dve.wait_ge(ld_tail["gain_ple"], 16)
            for t in range(TT):
                v.scalar_tensor_tensor(out=hn3[:, t], in0=h[:, t], scalar=rstd[:, t:t + 1], in1=gain_ple,
                                       op0=ALU.mult, op1=ALU.mult).then_inc(hn3_made, 1)
            for n in (1, 3):
                dve.wait_ge(tail_done, TAIL_T + n + 1)
                v.tensor_copy(hn3T[:, 2 * n:2 * n + 2], two(bank[n])).then_inc(ht_dve, 1)
            for n in range(4):
                t = n // 2
                s = sig[:, n % 2]
                dve.wait_ge(ple_sig, n + 1)
                link(v.tensor_tensor(s, s, bank[PROJ_BANK[n]][:, :], ALU.mult))
                o = h[:, t, 512 * (n % 2):512 * (n % 2 + 1)]
                v.tensor_tensor(o, o, s, ALU.add).then_inc(sig_made, 1)
                if n % 2:
                    dve.wait_ge(ld_tail["gain_fin"], 16)
                    dve.wait_ge(ssq_tail, TT + t + 1)
                    inverse_rms(slice(t, t + 1))
                    v.scalar_tensor_tensor(out=hn3[:, t], in0=h[:, t], scalar=rstd[:, t:t + 1], in1=gain_fin,
                                           op0=ALU.mult, op1=ALU.mult).then_inc(y_made, 1)

        @block.tensor
        def _(pe):
            mm = nc.tensor.matmul

            def begin(name):
                n = NUMBER[name]
                if n >= 8:
                    unit_saved(pe, UNITS[n - 8][0])
                return ubank(name)

            def transposes(name, pieces):
                b = begin(name)
                for n, piece in enumerate(pieces):
                    last = nc.tensor.transpose(b[:, n * P:(n + 1) * P], piece, ident)
                last.then_inc(unit_done, 1)

            def to_T(name, w, cols, src=None, tiles=KT):
                b = begin(name)
                src = xnT if src is None else src
                for n, c in enumerate(cols):
                    for k in range(tiles):
                        last = mm(b[:, n * T:(n + 1) * T], w[:, k, c:c + P], src[:, k], start=(k == 0), stop=(k == tiles - 1))
                last.then_inc(unit_done, 1)

            def to_tokens(name, w, t, c, src=None):
                b = begin(name)
                src = xnT if src is None else src
                for k in range(KT):
                    last = mm(b[:, :], src[:, k, tok(t)], w[:, k, c:c + 512], start=(k == 0), stop=(k == KT - 1))
                last.then_inc(unit_done, 1)

            pe.wait_ge(s_cmain, 16)
            pe.wait_ge(xn_made, 2)
            for n in range(4):
                transposes(f"xt{n}", [xn[:, t, k * P:(k + 1) * P] for k in (2 * n, 2 * n + 1) for t in range(TT)])
            pe.wait_ge(s_bias, 16)
            transposes("bm", [bmrows])
            for n in range(4):
                unit_saved(pe, f"xt{n}")
            pe.wait_ge(ld["q"], 16)
            for n in range(2):
                to_T(f"q{n}", W[0], (2 * P * n, 2 * P * n + P))
            pe.wait_ge(ld["k"], 16)
            for n in range(2):
                to_T(f"k{n}", W[0], (512 + 2 * P * n, 512 + 2 * P * n + P))
            b = begin("ff")
            pe.wait_ge(s_ffw, 16)
            for t in range(TT):
                for k in range(KT):
                    last = mm(b[:, 8 * t:8 * t + 8], xnT[:, k, tok(t)], ffw[:, k], start=(k == 0), stop=(k == KT - 1))
            last.then_inc(unit_done, 1)
            pe.wait_ge(ld["v"], 16)
            for t in range(TT):
                to_tokens(f"v{t}", W[1], t, 0)
            pe.wait_ge(ld["rqk"], 16)
            to_T("rq", W[1], (512, 512 + P))
            to_T("rk", W[1], (512 + 2 * P, 512 + 3 * P))
            pe.wait_ge(ld["rvg"], 16)
            to_tokens("rv0", W[2], 0, 0)
            pe.wait_ge(s_cmix, 16)
            for n, name in enumerate(("rotq", "rotk")):
                b = begin(name)
                unit_saved(pe, ("rq", "rk")[n])
                mm(b[:, :], mix("rot"), rraw[:, n].rearrange("p k n -> p (k n)"), start=True, stop=True).then_inc(unit_done, 1)
            to_tokens("rv1", W[2], 1, 0)
            for n in range(2):
                to_T(f"rg{n}", W[2], (512 + 2 * P * n, 512 + 2 * P * n + P))
            b = begin("cs")
            pe.wait_ge(lf_made, 1)
            mm(b[:, 0:T], lf[:, 0], tri, start=True, stop=False)
            mm(b[:, P:T], lf[:, 1], tri[:, 0:P], start=False, stop=True).then_inc(unit_done, 1)
            pe.wait_ge(rot_made, 2)
            for hd in range(RET_HEADS):
                b = begin(f"rs{hd}")
                mm(b[:, 0:T], rkz[:, hd, 0:P], rqT[:, hd // 2], start=True, stop=True)
                mm(b[:, T:3 * P], rkz[:, hd, P:T], rqT[:, hd // 2, P:T], start=True, stop=True).then_inc(unit_done, 1)
            unit_saved(pe, "cs")
            unit_saved(pe, "q1")
            for n in range(6):
                b = begin(f"fs{n}")
                t, heads, width = (0, range(4 * n, 4 * n + 4), P) if n < 2 else (1, range(2 * n - 4, 2 * n - 2), T)
                for i, hd in enumerate(heads):
                    o = b[:, i * width:(i + 1) * width]
                    mm(o, qT[:, hd // 2, tok(t)], kz[:, hd, 0:width], start=True, stop=False)
                    last = mm(o, L[:, tok(t)], R[:, hd, 0:width], start=False, stop=True)
                last.then_inc(unit_done, 1)
            unit_saved(pe, "rs3")
            unit_saved(pe, "rv1")
            for n in range(2):
                b = begin(f"ro{n}")
                for i in range(2):
                    hd = 2 * n + i
                    c = slice(hd * RET_DV, (hd + 1) * RET_DV)
                    mm(b[:, i * T:(i + 1) * T], rv[:, 0, c], scT[:, hd, 0:T], start=True, stop=False)
                    last = mm(b[:, i * T + P:(i + 1) * T], rv[:, 1, c], scT[:, hd, T:3 * P], start=False, stop=True)
                last.then_inc(unit_done, 1)
            pe.wait_ge(ld["gate0"], 16)
            for n in range(4):
                to_T(f"ga{n}", W[0], (2 * P * n, 2 * P * n + P))
            pe.wait_ge(probs_made, 2)
            for hd in range(FOX_HEADS):
                transposes(f"pt{hd}", [probs0[:, hd], probs1[:, hd, 0:P], probs1[:, hd, P:T]])
            for n in range(2):
                b = begin(f"ms{n}")
                unit_saved(pe, f"ro{n}")
                mm(b[:, :], mix("mean"), rsq[:, 2 * n:2 * n + 2].rearrange("p k n -> p (k n)"), start=True, stop=True).then_inc(unit_done, 1)
            pe.wait_ge(ld["gate1"], 16)
            for n in range(4):
                to_T(f"gb{n}", W[1], (2 * P * n, 2 * P * n + P))
            unit_saved(pe, "pt6")
            unit_saved(pe, "pt7")
            for n in range(2):
                b = begin(f"fo{n}")
                for i in range(2):
                    for s in range(2):
                        hd = 2 * (2 * n + i) + s
                        mm(b[:, i * T:(i + 1) * T], vz[:, 0, hd], probsT[:, hd, 0:T], start=(s == 0), stop=False)
                        last = mm(b[:, i * T + P:(i + 1) * T], vz[:, 1, hd], probsT[:, hd, T:3 * P], start=False, stop=(s == 1))
                last.then_inc(unit_done, 1)
            pe.wait_ge(ld["branch"], 16)
            unit_saved(pe, "fo1")
            for n in range(4):
                to_T(f"pr{n}", W[2], (2 * P * n, 2 * P * n + P), foxT, 4)
            pe.wait_ge(ro_made, 2)
            for n in range(4):
                to_T(f"pr{4 + n}", W[2][:, 4:8], (2 * P * n, 2 * P * n + P), roT, 4)
            pe.wait_ge(ld["out"], 16)
            unit_saved(pe, "pr7")
            for n in range(4):
                to_tokens(f"out{n}", W[3], n // 2, 512 * (n % 2), gates)
            pe.wait_ge(hn_made, 2)
            for n in range(4):
                transposes(f"ht{n}", [hn[:, t, k * P:(k + 1) * P] for k in (2 * n, 2 * n + 1) for t in range(TT)])
            for n in range(4):
                unit_saved(pe, f"ht{n}")
            b = begin("rl")
            pe.wait_ge(s_wrouter, 16)
            for t in range(TT):
                for k in range(KT):
                    last = mm(b[:, E * t:E * (t + 1)], xnT[:, k, tok(t)], wrout[:, k], start=(k == 0), stop=(k == KT - 1))
            last.then_inc(unit_done, 1)
            b = begin("pos")
            pe.wait_ge(sel_made, 1)
            mm(b[:, 0:E], tri[:, 0:P], sel[:, 0], start=True, stop=True)
            mm(b[:, E:2 * E], ones, sel[:, 0], start=True, stop=False)
            mm(b[:, E:2 * E], tri[:, 0:P], sel[:, 1], start=False, stop=True)
            mm(b[:, 2 * E:3 * E], ones, sel[:, 0], start=True, stop=False)
            mm(b[:, 2 * E:3 * E], ones, sel[:, 1], start=False, stop=True).then_inc(unit_done, 1)
            def gather(done, banks):
                for n in range(2):
                    for i in range(4):
                        k = 4 * n + i
                        for t in range(TT):
                            last = mm(bank[banks[n]][:, i * P:(i + 1) * P], hn[:, t, k * P:(k + 1) * P], hot[:, t],
                                      start=(t == 0), stop=(t == TT - 1))
                    last.then_inc(done, 1)

            def gate_up(b, n, w, stationary, cols, done):
                for k in range(KT):
                    for half, c in enumerate(cols):
                        mm(b[c, :], stationary[:, k, c], w[half][:, k], start=(k == 0), stop=False, skip_group_check=True)
                for c in cols:
                    last = mm(b[c, :], ind[:, n, c], bgu[:, :], start=False, stop=True, skip_group_check=True)
                last.then_inc(done, 1)

            def down(b, w, cols, done):
                for k in range(FT):
                    for half, c in enumerate(cols):
                        last = mm(b[c, :], actT[:, k, c], w[half][:, k], start=(k == 0), stop=(k == FT - 1), skip_group_check=True)
                last.then_inc(done, 1)

            def comb_transpose(b, done):
                for t in range(TT):
                    last = nc.tensor.transpose(b[:, tok(t)], comb[:, t], ident)
                last.then_inc(done, 1)

            def act_transpose(b, n, done):
                for i in range(4):
                    k = 4 * n + i
                    last = nc.tensor.transpose(b[:, i * P:(i + 1) * P], act[:, k * P:(k + 1) * P], ident)
                last.then_inc(done, 1)

            def scatter():
                for n in range(4):
                    last = mm(bank[n][:, :], combT[:, tok(n // 2)], Y[:, 512 * (n % 2):512 * (n % 2 + 1)],
                              start=False, stop=False, skip_group_check=True)
                return last

            def finish_pair(p):
                pe.wait_ge(y_saved, 2 * p + 2)
                pe.wait_ge(ct_saved, p + 1)
                return scatter()

            AB = [slice(SLOTS * half, SLOTS * (half + 1)) for half in range(2)]

            def pair(p, first, last):
                def gate_up_chunk(n):
                    pe.wait_ge(ld_gu[n], 32 * p + 32)
                    gate_up(bank[4 + n % 2], n, gu_slot[n], xg, AB, gu_done)

                def down_chunk(n):
                    pe.wait_ge(ld_dn, 64 * p + 32 * (n + 1))
                    down(bank[5 + n], dn_slot, AB, dn_done)

                pe.wait_ge(xg_saved, 2 * p + 2)
                pe.wait_ge(ind_made, p + 1)
                gate_up_chunk(0)
                if first:
                    begin_output()
                else:
                    pe.wait_ge(y_saved, 2 * p)
                gate_up_chunk(1)
                pe.wait_ge(act_made, GU * p + 1)
                gate_up_chunk(2)
                pe.wait_ge(act_made, GU * p + 2)
                act_transpose(bank[6], 0, at_done)
                gate_up_chunk(3)
                if not first:
                    finish_pair(p - 1)
                pe.wait_ge(at_saved, 2 * p + 1)
                pe.wait_ge(act_made, GU * p + 4)
                act_transpose(bank[6], 1, at_done)
                pe.wait_ge(at_saved, 2 * p + 2)
                down_chunk(0)
                if not last:
                    pe.wait_ge(hot_made, p + 2)
                    gather(gather_done, (7, 4))
                    pe.wait_ge(xg_saved, 2 * p + 3)
                pe.wait_ge(comb_made, p + 1)
                comb_transpose(bank[7], ct_done)
                down_chunk(1)

            def begin_output():
                for n in range(len(UNITS) - 8, len(UNITS)):
                    unit_saved(pe, UNITS[n][0])
                pe.wait_ge(ld["b_down"], 16)
                for n in range(4):
                    last = mm(bank[n][:, :], combT[:, tok(n // 2)], bdown[:, 512 * (n % 2):512 * (n % 2 + 1)],
                              start=True, stop=False, skip_group_check=True)
                last.then_inc(acc_begun, 1)

            pe.wait_ge(s_bgu, 16 * GU)
            pe.wait_ge(hot_made, 1)
            unit_saved(pe, "out3")
            unit_saved(pe, "ht2")
            gather(gather_done, (7, 4))
            pe.wait_ge(w_made, 1)
            transposes("wt", [wp[:, t] for t in range(TT)])
            pair(0, True, False)
            with pe.Fori(1, PAIRS - 1) as p:
                pair(p, False, False)
            pair(PAIRS - 1, False, True)
            finish_pair(PAIRS - 1).then_inc(job_pe, 1)

            pe.wait_ge(jobs_made, 1)
            n_jobs = pe.value_load(jobs_i[0:1, MAX_JOBS:MAX_JOBS + 1], min_val=0, max_val=MAX_JOBS)
            with pe.Fori(0, MAX_JOBS) as j:
                with pe.If(j < n_jobs):
                    act0, dve0 = j * ACT_JOB_STEPS, j * DVE_JOB_STEPS
                    pe.wait_ge(job_dve, dve0 + 1)
                    gather(job_pe, (7, 4))
                    comb_transpose(bank[5], job_pe)
                    pe.wait_ge(ld_job, j * (16 * (GU + DN)) + 16 * (GU + DN))
                    pe.wait_ge(job_act, act0 + ACT_AT["xg"] + 2)
                    pe.wait_ge(job_dve, dve0 + DVE_AT["comb"] + 1)
                    for n in range(GU):
                        if n >= 2:
                            pe.wait_ge(job_dve, dve0 + DVE_AT["gu"] + 2 * (n - 1))
                        gate_up(bank[4 + n % 2], n, [gu_slot[2 + n // 2][n % 2]], xg, [slice(0, P)], job_pe)
                    pe.wait_ge(job_dve, dve0 + DVE_AT["gu"] + 2 * GU)
                    for n in range(2):
                        act_transpose(bank[6 + n], n, job_pe)
                    pe.wait_ge(job_act, act0 + ACT_JOB_STEPS)
                    for n in range(DN):
                        down(bank[4 + n], [dn_slot[n]], [slice(0, P)], job_pe)
                    pe.wait_ge(job_dve, dve0 + DVE_JOB_STEPS)
                    scatter().then_inc(job_pe, 1)

            pe.wait_ge(ld_tail["p"], 16)
            for k in range(2):
                for t in range(TT):
                    last = nc.tensor.transpose(bank[4][:, k * T + t * P:k * T + (t + 1) * P], prow[:, t, k * P:(k + 1) * P], ident)
            last.then_inc(tail_done, 1)
            pe.wait_ge(pT_saved, 1)
            pe.wait_ge(ld_tail["ple_proj"], 16)
            for n in range(4):
                for k in range(2):
                    last = mm(bank[PROJ_BANK[n]][:, :], pT[:, k, tok(n // 2)], wpp[:, k, 512 * (n % 2):512 * (n % 2 + 1)],
                              start=(k == 0), stop=(k == 1))
                last.then_inc(tail_done, 1)
            pe.wait_ge(h2_made, 4)
            pe.wait_ge(hn3_made, 2)
            for n in range(4):
                for i in range(4):
                    k, t = 2 * n + i // 2, i % 2
                    last = nc.tensor.transpose(bank[n][:, i * P:(i + 1) * P], hn3[:, t, k * P:(k + 1) * P], ident)
                last.then_inc(tail_done, 1)
            pe.wait_ge(ht_act, 2)
            pe.wait_ge(ht_dve, 2)
            pe.wait_ge(ld_tail["ple_gate"], 16)
            for n in range(4):
                for k in range(KT):
                    last = mm(bank[n][:, :], hn3T[:, k, tok(n // 2)], W[0][:, k, 512 * (n % 2):512 * (n % 2 + 1)],
                              start=(k == 0), stop=(k == KT - 1))
                last.then_inc(tail_done, 1)


_INS = ["x", "p", "mix_norm", "w_in", "b_forget", "w_branch", "w_merge_gate", "b_merge_gate", "w_out",
        "ffn_norm", "w_router", "b_router", "w_gate_up", "b_gate_up", "w_down", "b_down",
        "ple_norm", "w_ple_gate", "w_ple_proj", "final_norm"]


def kernel(**inputs):
    import concourse.bacc as _bacc
    from concourse.bass_utils import run_bass_kernel_spmd as _run

    nc = _bacc.Bacc("TRN2", target_bir_lowering=False, num_devices=1)
    data = {name: np.ascontiguousarray(inputs[name]) for name in _INS}
    data["t_main"], data["t_mix"] = tables()
    arrays, args = {}, {}
    for name, x in data.items():
        arrays[f"in_{name}"] = x
        args[name] = nc.dram_tensor(f"in_{name}", x.shape, mybir.dt.from_np(x.dtype), kind="ExternalInput").ap()
    shape = (1, T, D)
    out = nc.dram_tensor("out_0", shape, F32, kind="ExternalOutput").ap()
    build(nc, args, out, shape)
    r = _run(nc, [arrays], core_ids=[0])
    return r.results[0]["out_0"]
```

```python
import concourse.bass as bass
from concourse import mybir
from contextlib import ExitStack
import numpy as np

F32 = mybir.dt.float32
I32 = mybir.dt.int32
ALU = mybir.AluOpType
ACT = mybir.ActivationFunctionType
AX = mybir.AxisListType

P = 128
D = 1024
KT = D // P
T = 256
TT = T // P
FOX_HEADS, FOX_D = 8, 64
FOX_W = FOX_HEADS * FOX_D
RET_HEADS, RET_DK, RET_DV = 4, 64, 128
RET_QK_W = RET_HEADS * RET_DK
RET_V_W = RET_HEADS * RET_DV
E = 32
TOP_K = 4
FF = 1024
FT = FF // P
LIMIT, ALPHA = 7.0, 1.702
EPS = 1e-6
PLE = 256
CHUNK = 512
GU = 2 * FF // CHUNK
DN = D // CHUNK
SPLIT = 2
STEPS = 4
SLOTS = 64
PAIRS = E // 2
ROUNDS = 2
MAX_JOBS = T * TOP_K // (SLOTS + 1)
C_FQ, C_FK, C_FV, C_FF = 0, FOX_W, 2 * FOX_W, 3 * FOX_W
C_RQ = C_FF + FOX_HEADS
C_RK = C_RQ + RET_QK_W
C_RV = C_RK + RET_QK_W
C_RG = C_RV + RET_V_W
CAUSAL_FILL = -1e30
ROOT_MAGIC = float(0x5f3759df)

MAIN_COLS = dict(ident=P, tri=2 * P, iota=P)
MIX_COLS = dict(cos=T, sin=T, rot=P, decay=RET_HEADS * 3 * P, mask=T, mean=P, la=1, lb=1,
                ra=FOX_HEADS, rb=FOX_HEADS)


def columns(spec):
    at, out = 0, {}
    for name, n in spec.items():
        out[name] = (at, at + n)
        at += n
    return out, at


MAIN_AT, MAIN_N = columns(MAIN_COLS)
MIX_AT, MIX_N = columns(MIX_COLS)


def tables():
    main = np.zeros((P, MAIN_N), np.float32)
    mix = np.zeros((P, MIX_N), np.float32)

    def put(table, at, name, value):
        a, b = at[name]
        table[:, a:b] = value

    i = np.arange(P)
    put(main, MAIN_AT, "ident", np.eye(P))
    put(main, MAIN_AT, "tri", np.concatenate([i[:, None] <= i[None, :], np.ones((P, P))], 1))
    put(main, MAIN_AT, "iota", i[None, :])
    half = RET_DK // 2
    inv = (np.float32(10000.0) ** (-np.arange(half, dtype=np.float32) / half)).astype(np.float32)
    ang = (inv[i % half][:, None] * np.arange(T, dtype=np.float32)[None, :]).astype(np.float32)
    put(mix, MIX_AT, "cos", np.cos(ang.astype(np.float64)))
    put(mix, MIX_AT, "sin", np.sin(ang.astype(np.float64)))
    rot = np.zeros((P, P))
    for m in range(P):
        if m % RET_DK < half:
            rot[m + half, m] = -1.0
        else:
            rot[m - half, m] = 1.0
    put(mix, MIX_AT, "rot", rot)
    lg = np.log1p(-np.exp2(-5.0 - np.arange(RET_HEADS)))
    key = i[:, None]
    for h in range(RET_HEADS):
        a = MIX_AT["decay"][0] + h * 3 * P
        gap = np.arange(T)[None, :] - key
        mix[:, a:a + T] = np.where(gap >= 0, np.exp(np.maximum(gap, 0) * lg[h]), 0)
        gap = i[None, :] - key
        mix[:, a + T:a + 3 * P] = np.where(gap >= 0, np.exp(np.maximum(gap, 0) * lg[h]), 0)
    mask = np.zeros((P, T))
    mask[:, P:] = np.where(i[None, :] <= i[:, None], 0.0, CAUSAL_FILL)
    put(mix, MIX_AT, "mask", mask)
    put(mix, MIX_AT, "mean", 1.0 / RET_DV)
    for h in range(FOX_HEADS):
        mix[h, MIX_AT["la"][0]] = 1.0
        mix[32 + h, MIX_AT["lb"][0]] = -1.0
        mix[32 + h, MIX_AT["ra"][0] + h] = 1.0
        mix[h, MIX_AT["rb"][0] + h] = 1.0
    return main, mix


UNITS = (
    [(f"xt{n}", "d") for n in range(4)]
    + [("bm", "d")]
    + [("q0", "a"), ("q1", "a"), ("k0", "d"), ("k1", "d")]
    + [("ff", "d"), ("v0", "d"), ("v1", "d")]
    + [("rq", "a"), ("rk", "a"), ("rv0", "a"), ("rotq", "d"), ("rotk", "d"), ("rv1", "a")]
    + [("cs", "d"), ("rg0", "d"), ("rg1", "d")]
    + [(f"rs{h}", "d") for h in range(4)]
    + [(f"fs{n}", "d") for n in range(6)]
    + [("ro0", "a"), ("ro1", "a")]
    + [(f"ga{n}", "a") for n in range(4)]
    + [(f"pt{h}", "ad"[h % 2]) for h in range(8)]
    + [("ms0", "d"), ("ms1", "d")]
    + [(f"gb{n}", "a") for n in range(4)]
    + [("fo0", "a"), ("fo1", "a")]
    + [(f"pr{n}", "d") for n in range(8)]
    + [("out0", "d"), ("out1", "d"), ("out2", "d")]
    + [("ht0", "a"), ("ht1", "d"), ("ht2", "a")]
    + [("out3", "d"), ("ht3", "a")]
    + [("rl", "d"), ("pos", "d"), ("wt", "d")]
)
NUMBER = {name: n for n, (name, _) in enumerate(UNITS)}
READER = dict(UNITS)
RANK = {}
for _eng in "ad":
    for _r, _name in enumerate([n for n, e in UNITS if e == _eng]):
        RANK[_name] = _r + 1

PROJ_BANK = (5, 6, 7, 4)
PE_AT = dict(gather=0, comb=2, gu=3, actT=7, down=9, scatter=11)
PE_JOB_STEPS = 12
ACT_AT = dict(xg=0, sigmoid=2, actT=6)
ACT_JOB_STEPS = 8
DVE_AT = dict(hot=0, comb=1, gu=2, y=10)
DVE_JOB_STEPS = 12


class Chain:

    def __init__(self, eng, sem):
        self.eng, self.sem, self.origin, self.steps = eng, sem, 0, 0

    def link(self, ins):
        self.steps += 1
        ins.then_inc(self.sem, 1)
        self.eng.wait_ge(self.sem, self.origin + self.steps)

    def enter(self, i, first, per):
        self.before = self.origin + self.steps
        self.per = per
        self.origin, self.steps = (i - first) * per + self.before, 0

    def leave(self, rounds):
        assert self.steps == self.per, (self.steps, self.per)
        self.origin, self.steps = self.before + rounds * self.per, 0


def build(nc, a, out):
    ctx = ExitStack()
    with ctx:
        def sem(name):
            return ctx.enter_context(nc.semaphore(name))

        def sb(name, cols, dt=F32):
            return ctx.enter_context(nc.sbuf_tensor(name, [P, cols], dt))

        bank = [ctx.enter_context(nc.psum_tensor(f"bank{n}", [P, 512], F32)) for n in range(8)]

        slot = [sb(f"slot{n}", 8 * 1024) for n in range(4)]
        down_slot = sb("down_slot", 8 * 1024)
        h_t = sb("h", TT * D)
        xnT_t = sb("xnT", KT * T)
        gates_t = sb("gates", 16 * T)
        fr_t = sb("branches", 8 * T)
        cmain = sb("cmain", MAIN_N)
        bgu = sb("b_gate_up", CHUNK)
        small = sb("small", 744)
        jobs_i = sb("jobs_i", 16, I32)

        def wview(s):
            return s[:, :].rearrange("p (k n) -> p k n", k=KT)

        W = [wview(s) for s in slot]

        def halves(s):
            return [s[:, 4096 * n:4096 * (n + 1)].rearrange("p (k n) -> p k n", k=KT) for n in range(2)]

        gu_slot = [halves(s) for s in slot]
        dn_slot = halves(down_slot)
        h = h_t[:, :].rearrange("p (t n) -> p t n", t=TT)
        xnT = xnT_t[:, :].rearrange("p (k n) -> p k n", k=KT)
        gates = gates_t[:, :].rearrange("p (k n) -> p k n", k=16)
        foxT = fr_t[:, 0:1024].rearrange("p (k n) -> p k n", k=4)
        roT = fr_t[:, 1024:2048].rearrange("p (k n) -> p k n", k=4)

        def main(name):
            return cmain[:, MAIN_AT[name][0]:MAIN_AT[name][1]]

        ident, tri, iota = main("ident"), main("tri"), main("iota")
        ones = tri[:, P:2 * P]

        taken = [0]

        def cut(n):
            taken[0] += n
            assert taken[0] <= small.shape[1], taken
            return small[:, taken[0] - n:taken[0]]

        lf = cut(2 * P).rearrange("p (t n) -> p t n", t=TT)
        wp = lf
        ffw = cut(KT * FOX_HEADS).rearrange("p (k n) -> p k n", k=KT)
        bfb = cut(FOX_HEADS)
        bmgT = cut(16)
        brb = cut(E)
        wrout = cut(KT * E).rearrange("p (k n) -> p k n", k=KT)
        zff = cut(16).rearrange("p (t n) -> p t n", t=TT)
        aff = cut(16).rearrange("p (t n) -> p t n", t=TT)
        ssq = cut(2)
        ssq_half = cut(4)
        rstd = cut(2)
        newton = cut(2)
        mx = cut(16)
        sums = cut(16)
        m8 = cut(16).rearrange("p (t n) -> p t n", t=TT)
        nmax = cut(2)
        ngt = cut(2)
        jobf = cut(16)

        def region(t, start):
            at = [start]

            def take(n):
                at[0] += n
                assert at[0] <= t.shape[1], at
                return t[:, at[0] - n:at[0]]
            return take

        s3 = region(slot[3], 0)
        cmix = s3(MIX_N)

        def mix(name):
            return cmix[:, MIX_AT[name][0]:MIX_AT[name][1]]

        early = region(slot[3], MIX_N)
        gain_mix = early(D)
        xgain = early(TT * D).rearrange("p (t n) -> p t n", t=TT)
        diag = early(TT * P).rearrange("p (t n) -> p t n", t=TT)
        rT = early(T)
        bmrows = early(P)
        fv = s3(TT * FOX_W).rearrange("p (t n) -> p t n", t=TT)
        rv = s3(TT * RET_V_W).rearrange("p (t n) -> p t n", t=TT)
        rqT = s3(2 * T).rearrange("p (k n) -> p k n", k=2)
        rkz = s3(RET_HEADS * T).rearrange("p (h n) -> p h n", h=RET_HEADS)
        L = s3(T)
        sd = region(down_slot, 0)
        qT = sd(4 * T).rearrange("p (k n) -> p k n", k=4)
        kz = sd(FOX_HEADS * T).rearrange("p (h n) -> p h n", h=FOX_HEADS)
        R = sd(FOX_HEADS * T).rearrange("p (h n) -> p h n", h=FOX_HEADS)
        probsT = sd(FOX_HEADS * 3 * P).rearrange("p (h n) -> p h n", h=FOX_HEADS)
        junk = probsT.rearrange("p h n -> p (h n)")[:, 0:TT * D].rearrange("p (t n) -> p t n", t=TT)
        rr, rsq = kz[:, 0:4], kz[:, 4:8]
        rseed = R[:, 0:4]
        rraw = gates_t[:, 0:1024].rearrange("p (w k n) -> p w k n", w=2, k=2)
        rtmp = gates_t[:, 1024:1536].rearrange("p (k n) -> p k n", k=2)
        rgsig = gates_t[:, 1536:2048].rearrange("p (k n) -> p k n", k=2)
        scT = gates_t[:, 2048:2048 + 1536].rearrange("p (h n) -> p h n", h=RET_HEADS)
        probs1 = gates_t[:, 2048:4096].rearrange("p (h n) -> p h n", h=FOX_HEADS)
        probs0 = fr_t[:, 0:1024].rearrange("p (h n) -> p h n", h=FOX_HEADS)

        gain_ffn = fr_t[:, 0:1024]
        bdown = fr_t[:, 1024:2048]
        hn = gates_t[:, 2048:4096].rearrange("p (t n) -> p t n", t=TT)
        xg = gates_t[:, 0:1024].rearrange("p (k s) -> p k s", k=KT)
        actT = gates_t[:, 1024:2048].rearrange("p (k s) -> p k s", k=FT)
        act = fr_t[:, 0:1024]
        Y = fr_t[:, 1024:2048]
        mo = region(xnT_t, 0)
        hot = mo(2 * P).rearrange("p (t s) -> p t s", t=TT)
        comb = mo(2 * P).rearrange("p (t s) -> p t s", t=TT)
        combT = small[:, 0:T]
        gl = mo(512)
        ex = mo(256)
        posm = mo(2 * E).rearrange("p (t e) -> p t e", t=TT)
        wr = mo(2 * E).rearrange("p (t e) -> p t e", t=TT)
        posq = mo(TT * E * ROUNDS).rearrange("p (t e r) -> p t e r", t=TT, e=E)
        ind = mo(GU * P).rearrange("p (n s) -> p n s", n=GU)
        jobrow = wrout.rearrange("p k n -> p (k n)")
        jf, jscan, jtmp = jobrow[:, 0:64], jobrow[:, 64:128], jobrow[:, 128:192]
        lg = gl[:, 0:64].rearrange("p (t e) -> p t e", t=TT)
        gt = gl[:, 64:128].rearrange("p (t e) -> p t e", t=TT)
        eq = gl[:, 128:192].rearrange("p (t e) -> p t e", t=TT)
        cum = gl[:, 192:256].rearrange("p (t e) -> p t e", t=TT)
        sel = gl[:, 256:320].rearrange("p (t e) -> p t e", t=TT)
        ew = gl[:, 320:384].rearrange("p (t e) -> p t e", t=TT)

        tail = region(slot[1], 0)
        wpp = tail(2 * D).rearrange("p (k n) -> p k n", k=2)
        prow = tail(TT * PLE).rearrange("p (t n) -> p t n", t=TT)
        gain_ple = tail(D)
        gain_fin = tail(D)
        pT = tail(2 * T).rearrange("p (k n) -> p k n", k=2)
        hn3 = tail(TT * D).rearrange("p (t n) -> p t n", t=TT)
        sig = tail(D).rearrange("p (w n) -> p w n", w=2)
        hn3T = gates_t[:, 0:2048].rearrange("p (k n) -> p k n", k=KT)

        s_x = [sem(f"x_loaded{t}") for t in range(TT)]
        s_cmain, s_cmix, s_gain = sem("cmain_loaded"), sem("cmix_loaded"), sem("gain_loaded")
        s_ffw, s_bf, s_br = sem("ffw_loaded"), sem("b_forget_loaded"), sem("b_router_loaded")
        s_wrouter = sem("w_router_loaded")
        s_bias = sem("bias_rows_loaded")
        s_bgu = sem("b_gate_up_loaded")
        s_zero = sem("pool_zeroed")
        ld = {k: sem(f"loaded_{k}") for k in
              ("q0", "q1", "k", "v", "rqk", "rvg", "gate0", "gate1", "branch", "out", "gain_ffn", "b_down")}
        unit_done = sem("unit_done")
        act_freed = sem("act_freed")
        dve_freed = sem("dve_freed")
        freed = {"a": act_freed, "d": dve_freed}
        dve_step, act_step = sem("dve_step"), sem("act_step")
        ssq_made = sem("sum_of_squares_made")
        xgain_made, diag_made = sem("x_times_gain_made"), sem("diagonal_made")
        log1p_made = sem("log1p_made")
        zff_made = sem("forget_logits_made")
        lf_made = sem("log_forget_made")
        rgsig_made = sem("rg_sigmoid_made")
        rot_made = sem("rotary_made")
        max_made, probs_exp, probs_made = sem("row_max_made"), sem("probs_exp_made"), sem("probs_made")
        ro_made = sem("retention_made")
        rseed_made = sem("retention_root_begun")
        hn_made = sem("hn_made")
        sel_made, top_made, rexp_made, w_made = sem("selection_made"), sem("router_max_made"), sem("router_exp_made"), sem("routing_weights_made")
        jobs_made = sem("jobs_made")
        acc_begun = sem("accumulators_begun")
        ld_gu = [sem(f"gate_up_loaded{n}") for n in range(GU)]
        ld_dn = sem("down_loaded")
        ld_last_dn = sem("last_down_loaded")
        gu_done = sem("gate_up_done")
        dn_done = sem("down_done")
        gather_done = sem("gather_done")
        ct_done = sem("comb_transposed")
        at_done = sem("act_transposed")
        hot_made, comb_made, ind_made = sem("one_hot_made"), sem("comb_made"), sem("bias_picker_made")
        clipped, act_made = sem("glu_clipped"), sem("act_made")
        ct_saved, y_saved = sem("combT_saved"), sem("y_saved")
        sig_done = sem("glu_sigmoid_made")
        xg_saved, at_saved = sem("xg_saved"), sem("actT_saved")
        ld_job = sem("job_weights_loaded")
        job_pe, job_act, job_dve = sem("job_pe_step"), sem("job_act_step"), sem("job_dve_step")
        ld_tail = {k: sem(f"loaded_{k}") for k in ("ple_gate0", "ple_gate1", "ple_proj", "p", "gain_ple", "gain_fin")}
        p_transposed, proj_done, hT_done, gate_done = sem("p_transposed"), sem("ple_projection_done"), sem("hn3_transposed"), sem("ple_gate_done")
        tail_step, rstd_made, rstd_fin = sem("dve_tail_step"), sem("ple_rstd_made"), sem("final_rstd_made")
        pT_saved, h2_made, hn3_made, ht_act, ht_dve = sem("pT_saved"), sem("h2_made"), sem("hn3_made"), sem("hn3T_saved_by_act"), sem("hn3T_saved_by_dve")
        ple_sig, sig_made, ssq_tail = sem("ple_sigmoid_made"), sem("ple_gate_used"), sem("tail_squares_made")
        y_dve, y_act, stored = sem("y_made_by_dve"), sem("y_made_by_act"), sem("stored")

        gu_w = a["w_gate_up"][0].rearrange("e (k p) n -> e p k n", p=P)
        dn_w = a["w_down"][0].rearrange("e (k p) n -> e p k n", p=P)

        def rows(w):
            return w.rearrange("(k p) n -> p k n", p=P)

        w_in = rows(a["w_in"][0])
        w_mg = rows(a["w_merge_gate"][0])
        w_br = a["w_branch"][0].rearrange("g (c p) n -> p (g c) n", p=P)
        x_rows = a["x"][0].rearrange("(t p) n -> p t n", p=P)
        out_rows = out[0].rearrange("(t p) n -> p t n", p=P)
        tok = lambda t: slice(t * P, (t + 1) * P)

        def unit_ready(eng, name):
            eng.wait_ge(unit_done, NUMBER[name] + 1)

        def unit_saved(eng, name):
            eng.wait_ge(freed[READER[name]], RANK[name])

        def ubank(name):
            return bank[(NUMBER[name] + 4) % 8]

        block = ctx.enter_context(nc.Block())

        @block.sync
        def _(sp):
            for t in range(TT):
                sp.dma_start(h[:, t], x_rows[:, t]).then_inc(s_x[t], 16)
            sp.dma_start(cmain[:, :], a["t_main"]).then_inc(s_cmain, 16)
            for n in range(2):
                sp.dma_start(W[0][:, :, 256 * n:256 * (n + 1)], w_in[:, :, C_FQ + 256 * n:C_FQ + 256 * (n + 1)]).then_inc(ld[f"q{n}"], 16)
            sp.dma_start(W[0][:, :, 512:1024], w_in[:, :, C_FK:C_FV]).then_inc(ld["k"], 16)
            with nc.allow_non_contiguous_dma(reason="eight columns of w_in"):
                sp.dma_start(ffw, w_in[:, :, C_FF:C_RQ]).then_inc(s_ffw, 16)
            sp.dma_start(bfb, a["b_forget"].to_broadcast([P, FOX_HEADS])).then_inc(s_bf, 16)
            sp.dma_start(W[1][:, :, 0:512], w_in[:, :, C_FV:C_FF]).then_inc(ld["v"], 16)
            sp.dma_start(W[1][:, :, 512:1024], w_in[:, :, C_RQ:C_RV]).then_inc(ld["rqk"], 16)
            sp.dma_start(cmix, a["t_mix"]).then_inc(s_cmix, 16)
            sp.dma_start(W[2], w_in[:, :, C_RV:C_RG + RET_V_W]).then_inc(ld["rvg"], 16)
            sp.dma_start(wrout, rows(a["w_router"][0])).then_inc(s_wrouter, 16)
            for n in range(GU):
                sp.dma_start(bgu[E * n:E * (n + 1), :], a["b_gate_up"][0][:, CHUNK * n:CHUNK * (n + 1)]).then_inc(s_bgu, 16)
            sp.dma_start(brb, a["b_router"].to_broadcast([P, E])).then_inc(s_br, 16)
            unit_ready(sp, "k1")
            sp.dma_start(W[0], w_mg[:, :, 0:D]).then_inc(ld["gate0"], 16)
            unit_ready(sp, "rk")
            sp.dma_start(W[1], w_mg[:, :, D:2 * D]).then_inc(ld["gate1"], 16)
            unit_ready(sp, "rg1")
            sp.dma_start(W[2], w_br).then_inc(ld["branch"], 16)

            def load_gate_up(n, a0):
                if n == SPLIT:
                    load_quarters(a0, range(4))
                    return
                for half in range(2):
                    sp.dma_start(gu_slot[n][half], gu_w[a0 + half][:, :, CHUNK * n:CHUNK * (n + 1)]).then_inc(ld_gu[n], 16)

            def load_quarters(a0, quarters):
                n = SPLIT
                for q in quarters:
                    half, k = q // 2, slice(KT // 2 * (q % 2), KT // 2 * (q % 2 + 1))
                    sp.dma_start(gu_slot[n][half][:, k], gu_w[a0 + half][:, k, CHUNK * n:CHUNK * (n + 1)]).then_inc(ld_gu[n], 16)

            def load_down(n, a0, to=dn_slot, done=ld_dn):
                for half in range(2):
                    sp.dma_start(to[half], dn_w[a0 + half][:, :, CHUNK * n:CHUNK * (n + 1)]).then_inc(done, 16)

            unit_ready(sp, "ga3")
            load_gate_up(0, 0)
            unit_ready(sp, "gb3")
            load_gate_up(1, 0)
            unit_ready(sp, "fo1")
            sp.wait_ge(ro_made, 2)
            sp.dma_start(W[3], rows(a["w_out"][0])).then_inc(ld["out"], 16)
            load_down(0, 0)
            unit_ready(sp, "pr7")
            sp.dma_start(gain_ffn, a["ffn_norm"].to_broadcast([P, D])).then_inc(ld["gain_ffn"], 16)
            load_gate_up(2, 0)
            sp.wait_ge(s_zero, 5)
            sp.dma_start(bdown[0:E, :], a["b_down"][0]).then_inc(ld["b_down"], 16)
            unit_ready(sp, "out3")
            load_gate_up(3, 0)

            def next_gate_up(n, p):
                sp.wait_ge(gu_done, GU * p + (n + 1))
                load_gate_up(n, 2 * p + 2)

            def rest_of_down(p):
                sp.wait_ge(dn_done, DN * p + 1)
                load_down(1, 2 * p)

            def next_down(p):
                sp.wait_ge(dn_done, DN * p + 2)
                load_down(0, 2 * p + 2)

            with sp.Fori(0, PAIRS - 1 - STEPS) as p:
                next_gate_up(0, p)
                next_gate_up(1, p)
                next_gate_up(2, p)
                rest_of_down(p)
                next_gate_up(3, p)
                next_down(p)
            last = PAIRS - 1
            for step in range(STEPS):
                p = last - STEPS + step
                before = range(STEPS - 1 - step)
                next_gate_up(0, p)
                next_gate_up(1, p)
                if before:
                    sp.wait_ge(gu_done, GU * p + (SPLIT + 1))
                    load_quarters(2 * p + 2, before)
                rest_of_down(p)
                sp.wait_ge(gu_done, GU * p + (SPLIT + 1))
                load_quarters(2 * p + 2, range(len(before), 4))
                next_gate_up(3, p)
                next_down(p)
            sp.wait_ge(gu_done, GU * last + 2)
            sp.dma_start(prow, a["p"][0, 0].rearrange("(t p) n -> p t n", p=P)).then_inc(ld_tail["p"], 16)
            sp.dma_start(gain_ple, a["ple_norm"].to_broadcast([P, D])).then_inc(ld_tail["gain_ple"], 16)
            sp.dma_start(wpp, a["w_ple_proj"][0].rearrange("(k p) n -> p k n", p=P)).then_inc(ld_tail["ple_proj"], 16)
            sp.wait_ge(gu_done, GU * last + 3)
            load_down(1, E - 2, gu_slot[2], ld_last_dn)
            for n in range(2):
                c = slice(512 * n, 512 * (n + 1))
                sp.dma_start(W[0][:, :, c], rows(a["w_ple_gate"][0])[:, :, c]).then_inc(ld_tail[f"ple_gate{n}"], 16)
            sp.dma_start(gain_fin, a["final_norm"].rearrange("(a n) -> a n", a=1).to_broadcast([P, D])).then_inc(ld_tail["gain_fin"], 16)
            sp.wait_ge(gu_done, GU * PAIRS)
            sp.wait_ge(dn_done, DN * PAIRS)
            sp.wait_ge(jobs_made, 1)
            n_jobs = sp.value_load(jobs_i[0:1, MAX_JOBS:MAX_JOBS + 1], min_val=0, max_val=MAX_JOBS)
            with sp.If(n_jobs > 0):
                with sp.Fori(0, MAX_JOBS) as j:
                    with sp.If(j < n_jobs):
                        q = sp.value_load(jobs_i[0:1, bass.ds(j, 1)], min_val=0, max_val=E * ROUNDS - 1)
                        e = sp.snap(q // 2)
                        sp.wait_ge(job_pe, j * PE_JOB_STEPS + 1)
                        for n in range(GU):
                            sp.dma_start(gu_slot[2 + n // 2][n % 2], gu_w[e][:, :, CHUNK * n:CHUNK * (n + 1)]).then_inc(ld_job, 16)
                        for n in range(DN):
                            sp.dma_start(dn_slot[n], dn_w[e][:, :, CHUNK * n:CHUNK * (n + 1)]).then_inc(ld_job, 16)
            for t in range(TT):
                sp.wait_ge(y_dve, t + 1)
                sp.wait_ge(y_act, t + 1)
                sp.dma_start(out_rows[:, t], hn3[:, t]).then_inc(stored, 16)
            sp.wait_ge(stored, 16 * TT)

        @block.gpsimd
        def _(pool):
            nc.gpsimd.memset(bmrows, 0.0).then_inc(s_zero, 1)
            pool.wait_ge(s_zero, 1)
            pool.dma_start(bmrows[0:16, :], a["b_merge_gate"].rearrange("a (r n) -> (a r) n", r=16)).then_inc(s_bias, 16)
            nc.gpsimd.memset(kz, 0.0).then_inc(s_zero, 1)
            nc.gpsimd.memset(small[:, 0:2 * P], 0.0).then_inc(s_zero, 1)
            unit_saved(pool, "bm")
            nc.gpsimd.memset(rkz, 0.0).then_inc(s_zero, 1)
            unit_ready(pool, "pr7")
            nc.gpsimd.memset(bdown, 0.0).then_inc(s_zero, 1)

        @block.scalar
        def _(actE):
            chain = Chain(actE, act_step)
            link = chain.link

            def copy(o, i, scale=1.0):
                return nc.scalar.activation(o, i, ACT.Copy, scale=scale)

            actE.dma_start(gain_mix, a["mix_norm"].to_broadcast([P, D])).then_inc(s_gain, 16)

            def squares(t, junk, done):
                nc.scalar.activation(junk, h[:, t], ACT.Square, accum_out=ssq[:, t:t + 1]).then_inc(done, 1)

            for t in range(TT):
                actE.wait_ge(s_x[t], 16)
                squares(t, junk[:, t], ssq_made)
            for n in range(2):
                unit_ready(actE, f"q{n}")
                copy(qT[:, 2 * n:2 * n + 2], ubank(f"q{n}")[:, :].rearrange("p (k n) -> p k n", k=2),
                     FOX_D ** -0.5).then_inc(act_freed, 1)
            actE.wait_ge(zff_made, 1)
            link(nc.scalar.activation(aff, aff, ACT.Exp))
            nc.scalar.activation(aff, aff, ACT.Ln, bias=1.0).then_inc(log1p_made, 1)
            for n, name in enumerate(("rq", "rk")):
                unit_ready(actE, name)
                copy(rraw[:, n], ubank(name)[:, :].rearrange("p (k n) -> p k n", k=2),
                     (1.0, RET_DK ** -0.5)[n]).then_inc(act_freed, 1)
            for t in range(TT):
                unit_ready(actE, f"rv{t}")
                copy(rv[:, t], ubank(f"rv{t}")[:, :]).then_inc(act_freed, 1)
            for n in range(2):
                unit_ready(actE, f"rg{n}")
                if n:
                    unit_saved(actE, "rg0")
                nc.scalar.activation(rgsig, ubank(f"rg{n}")[:, :].rearrange("p (k n) -> p k n", k=2),
                                     ACT.Sigmoid).then_inc(rgsig_made, 1)

            for b, pr in enumerate((probs0, probs1)):
                actE.wait_ge(max_made, b + 1)
                for hd in range(FOX_HEADS):
                    c = 8 * b + hd
                    last = nc.scalar.activation(pr[:, hd], pr[:, hd], ACT.Exp, bias=mx[:, c:c + 1],
                                                accum_out=sums[:, c:c + 1])
                last.then_inc(probs_exp, 1)
            for n in range(2):
                unit_ready(actE, f"ro{n}")
                v = ubank(f"ro{n}")[:, :].rearrange("p (k n) -> p k n", k=2)
                copy(rr[:, 2 * n:2 * n + 2], v)
                nc.scalar.activation(rsq[:, 2 * n:2 * n + 2], v, ACT.Square).then_inc(act_freed, 1)

            def gate(name, first):
                unit_ready(actE, name)
                for k in range(2):
                    last = nc.scalar.activation(gates[:, first + k], ubank(name)[:, k * T:(k + 1) * T],
                                                ACT.Sigmoid, bias=bmgT[:, first + k:first + k + 1])
                last.then_inc(act_freed, 1)

            actE.wait_ge(rot_made, 2)
            unit_saved(actE, "rg1")
            for n in range(4):
                gate(f"ga{n}", 2 * n)
            for hd in range(0, FOX_HEADS, 2):
                unit_ready(actE, f"pt{hd}")
                copy(probsT[:, hd], ubank(f"pt{hd}")[:, 0:3 * P]).then_inc(act_freed, 1)
            for n in range(2):
                unit_saved(actE, f"ms{n}")
                y = rseed[:, 2 * n:2 * n + 2]
                link(nc.scalar.activation(y, rsq[:, 2 * n:2 * n + 2], ACT.Ln))
                nc.scalar.activation(y, y, ACT.Exp, scale=-0.5).then_inc(rseed_made, 1)
            for n in range(4):
                gate(f"gb{n}", 8 + 2 * n)
            for n in range(2):
                unit_ready(actE, f"fo{n}")
                copy(foxT[:, 2 * n:2 * n + 2], ubank(f"fo{n}")[:, :].rearrange("p (k n) -> p k n", k=2)).then_inc(act_freed, 1)

            def save_hT(n):
                unit_ready(actE, f"ht{n}")
                k = 4 * (n % 2)
                copy(xnT[:, k:k + 4, tok(n // 2)], ubank(f"ht{n}")[:, :].rearrange("p (k n) -> p k n", k=4)).then_inc(act_freed, 1)

            unit_saved(actE, "out1")
            squares(0, hn[:, 1], ssq_made)
            save_hT(0)
            save_hT(2)
            unit_saved(actE, "out3")
            squares(1, gates_t[:, 0:D], ssq_made)
            save_hT(3)
            actE.wait_ge(top_made, 1)
            for t in range(TT):
                nc.scalar.activation(ew[:, t], lg[:, t], ACT.Exp, bias=nmax[:, t:t + 1]).then_inc(rexp_made, 1)

            def save_gathered(p):
                for n, b in enumerate((7, 4)):
                    actE.wait_ge(gather_done, 2 * p + (n + 1))
                    copy(xg[:, 4 * n:4 * n + 4], bank[b][:, :].rearrange("p (k s) -> p k s", k=4)).then_inc(xg_saved, 1)

            def pair(p, last):
                def sigmoid(n):
                    actE.wait_ge(clipped, GU * p + (n + 1))
                    nc.scalar.activation(ex, gl[:, 0:256], ACT.Sigmoid, scale=ALPHA).then_inc(sig_done, 1)

                def save_activations(n):
                    actE.wait_ge(at_done, 2 * p + (n + 1))
                    copy(actT[:, 4 * n:4 * n + 4], bank[6][:, :].rearrange("p (k s) -> p k s", k=4)).then_inc(at_saved, 1)

                sigmoid(0)
                sigmoid(1)
                sigmoid(2)
                save_activations(0)
                sigmoid(3)
                save_activations(1)
                if not last:
                    save_gathered(p + 1)
                else:
                    actE.wait_ge(p_transposed, 1)
                    copy(pT, bank[4][:, :].rearrange("p (k n) -> p k n", k=2)).then_inc(pT_saved, 1)

            save_gathered(0)
            pair(0, False)
            with actE.Fori(1, PAIRS - 1) as p:
                pair(p, False)
            pair(PAIRS - 1, True)

            n_jobs = actE.value_load(jobs_i[0:1, MAX_JOBS:MAX_JOBS + 1], min_val=0, max_val=MAX_JOBS)
            with actE.If(n_jobs > 0):
                with actE.Fori(0, MAX_JOBS) as j:
                    with actE.If(j < n_jobs):
                        pe0, dve0 = j * PE_JOB_STEPS + 1, j * DVE_JOB_STEPS
                        for n, b in enumerate((7, 4)):
                            actE.wait_ge(job_pe, pe0 + PE_AT["gather"] + (n + 1))
                            copy(xg[:, 4 * n:4 * n + 4], bank[b][:, :].rearrange("p (k s) -> p k s", k=4)).then_inc(job_act, 1)
                        for n in range(GU):
                            actE.wait_ge(job_dve, dve0 + DVE_AT["gu"] + (2 * n + 1))
                            nc.scalar.activation(ex, gl[:, 0:256], ACT.Sigmoid, scale=ALPHA).then_inc(job_act, 1)
                        for n in range(2):
                            actE.wait_ge(job_pe, pe0 + PE_AT["actT"] + (n + 1))
                            copy(actT[:, 4 * n:4 * n + 4], bank[6 + n][:, :].rearrange("p (k s) -> p k s", k=4)).then_inc(job_act, 1)

            for t in range(TT):
                actE.wait_ge(h2_made, 2 * (t + 1))
                squares(t, hn[:, t], ssq_tail)
                actE.wait_ge(hT_done, 2 * t + 1)
                copy(hn3T[:, 0:4, tok(t)], bank[2 * t][:, :].rearrange("p (k n) -> p k n", k=4)).then_inc(ht_act, 1)
            for n in range(4):
                t, c = n // 2, n % 2
                actE.wait_ge(gate_done, n + 1)
                if n == 0:
                    actE.wait_ge(rstd_made, 1)
                nc.scalar.activation(sig[:, c], bank[n][:, :], ACT.Sigmoid, scale=rstd[:, t:t + 1]).then_inc(ple_sig, 1)
                actE.wait_ge(sig_made, n + 1)
                nc.scalar.activation(hn[:, t, 512 * c:512 * (c + 1)], h[:, t, 512 * c:512 * (c + 1)], ACT.Square,
                                     accum_out=ssq_half[:, n:n + 1]).then_inc(ssq_tail, 1)
                if c:
                    actE.wait_ge(rstd_fin, t + 1)
                    nc.scalar.activation(hn3[:, t, 512:1024], hn3[:, t, 512:1024], ACT.Copy,
                                         scale=rstd[:, t:t + 1]).then_inc(y_act, 1)

        @block.vector
        def _(dve):
            chain = Chain(dve, dve_step)
            link = chain.link
            v = nc.vector

            def inverse_rms(c, done=None, count=0):
                x, y, w = ssq[:, c], rstd[:, c], newton[:, c]
                link(v.tensor_scalar(x, x, 1.0 / D, EPS, ALU.mult, ALU.add))
                link(v.tensor_scalar(y.bitcast(I32), x.bitcast(I32), -0.5, ROOT_MAGIC, ALU.mult, ALU.add))
                for step in range(3):
                    link(v.tensor_tensor(w, y, y, ALU.mult))
                    link(v.scalar_tensor_tensor(out=w, in0=w, scalar=-0.5, in1=x, op0=ALU.mult, op1=ALU.mult))
                    last = v.scalar_tensor_tensor(out=y, in0=w, scalar=1.5, in1=y, op0=ALU.add, op1=ALU.mult)
                    if step == 2 and done is not None:
                        last.then_inc(done, 1)
                        dve.wait_ge(done, count)
                    else:
                        link(last)

            def two(b):
                return b[:, :].rearrange("p (k n) -> p k n", k=2)

            dve.wait_ge(s_gain, 16)
            for t in range(TT):
                dve.wait_ge(s_x[t], 16)
                v.tensor_tensor(xgain[:, t], h[:, t], gain_mix, ALU.mult).then_inc(xgain_made, 1)
            dve.wait_ge(ssq_made, TT)
            inverse_rms(slice(0, TT))
            dve.wait_ge(s_cmain, 16)
            for t in range(TT):
                v.tensor_scalar(diag[:, t], ident, rstd[:, t:t + 1], None, ALU.mult).then_inc(diag_made, 1)
            unit_ready(dve, "bm")
            link(v.tensor_copy(rT, ubank("bm")[:, P:P + T]))
            for n in range(4):
                v.tensor_tensor(xnT[:, 2 * n:2 * n + 2], two(ubank(f"xt{n}")), rT.unsqueeze(1).to_broadcast([P, 2, T]),
                                ALU.mult).then_inc(dve_freed, 1)
            v.tensor_copy(bmgT, ubank("bm")[:, 0:16]).then_inc(dve_freed, 1)
            dve.wait_ge(s_zero, 3)
            kz_p = kz.rearrange("p (t s) n -> p t s n", s=2)
            for n in range(2):
                unit_ready(dve, f"k{n}")
                for s in range(2):
                    last = v.tensor_copy(kz_p[64 * s:64 * s + 64, 2 * n:2 * n + 2, s],
                                         two(ubank(f"k{n}"))[64 * s:64 * s + 64])
                last.then_inc(dve_freed, 1)
            unit_ready(dve, "ff")
            dve.wait_ge(s_bf, 16)
            v.tensor_tensor(zff, ubank("ff")[:, 0:16].rearrange("p (t n) -> p t n", t=TT),
                            bfb.unsqueeze(1).to_broadcast([P, TT, FOX_HEADS]), ALU.add).then_inc(dve_freed, 1)
            unit_saved(dve, "ff")
            v.scalar_tensor_tensor(out=aff, in0=zff, scalar=-1.0, in1=zff,
                                   op0=ALU.mult, op1=ALU.min).then_inc(zff_made, 1)
            unit_saved(dve, "bm")
            for t in range(TT):
                unit_ready(dve, f"v{t}")
                v.tensor_copy(fv[:, t], ubank(f"v{t}")[:, :]).then_inc(dve_freed, 1)
            dve.wait_ge(log1p_made, 1)
            link(v.scalar_tensor_tensor(out=lf[:, :, 0:FOX_HEADS], in0=zff, scalar=0.0, in1=aff,
                                        op0=ALU.min, op1=ALU.subtract))
            v.tensor_copy(lf[:, :, 32:32 + FOX_HEADS], lf[:, :, 0:FOX_HEADS]).then_inc(lf_made, 1)
            dve.wait_ge(s_cmix, 16)
            sin2 = mix("sin").unsqueeze(1).to_broadcast([P, 2, T])
            cos2 = mix("cos").unsqueeze(1).to_broadcast([P, 2, T])
            rkz_p = rkz.rearrange("p (t s) n -> p t s n", s=2)
            dve.wait_ge(s_zero, 4)
            for n, name in enumerate(("rotq", "rotk")):
                unit_ready(dve, name)
                v.tensor_tensor(rtmp, two(ubank(name)), sin2, ALU.mult).then_inc(dve_freed, 1)
                link(v.tensor_tensor(rraw[:, n], rraw[:, n], cos2, ALU.mult))
                if n == 0:
                    v.tensor_tensor(rqT, rraw[:, n], rtmp, ALU.add).then_inc(rot_made, 1)
                    dve.wait_ge(rot_made, 1)
                else:
                    for s in range(2):
                        hp = slice(64 * s, 64 * s + 64)
                        last = v.tensor_tensor(rkz_p[hp, :, s], rraw[hp, n], rtmp[hp], ALU.add)
                    last.then_inc(rot_made, 1)
            unit_ready(dve, "cs")
            cs = ubank("cs")[:, 0:T]
            v.tensor_scalar(L, cs, mix("la"), mix("lb"), ALU.mult, ALU.add)
            for hd in range(FOX_HEADS):
                last = v.tensor_scalar(R[:, hd], cs, mix("ra")[:, hd:hd + 1], mix("rb")[:, hd:hd + 1], ALU.mult, ALU.add)
            last.then_inc(dve_freed, 1)
            for n in range(2):
                dve.wait_ge(rgsig_made, n + 1)
                v.tensor_tensor(roT[:, 2 * n:2 * n + 2], rgsig, two(ubank(f"rg{n}")), ALU.mult).then_inc(dve_freed, 1)
            for hd in range(RET_HEADS):
                unit_ready(dve, f"rs{hd}")
                dec = mix("decay")[:, hd * 3 * P:(hd + 1) * 3 * P]
                v.tensor_tensor(scT[:, hd], ubank(f"rs{hd}")[:, 0:3 * P], dec, ALU.mult).then_inc(dve_freed, 1)
            m = mix("mask")
            for n in range(2):
                unit_ready(dve, f"fs{n}")
                v.tensor_tensor(probs0[:, 4 * n:4 * n + 4], ubank(f"fs{n}")[:, :].rearrange("p (k n) -> p k n", k=4),
                                m[:, P:2 * P].unsqueeze(1).to_broadcast([P, 4, P]), ALU.add).then_inc(dve_freed, 1)
            unit_saved(dve, "fs1")
            link(v.reduce_max(mx[:, 0:8], probs0, AX.X))
            v.tensor_scalar(mx[:, 0:8], mx[:, 0:8], -1.0, None, ALU.mult).then_inc(max_made, 1)
            unit_ready(dve, "ro1")
            for n in range(4):
                unit_ready(dve, f"fs{2 + n}")
                v.tensor_tensor(probs1[:, 2 * n:2 * n + 2], two(ubank(f"fs{2 + n}")),
                                m.unsqueeze(1).to_broadcast([P, 2, T]), ALU.add).then_inc(dve_freed, 1)
            unit_saved(dve, "fs5")
            link(v.reduce_max(mx[:, 8:16], probs1, AX.X))
            v.tensor_scalar(mx[:, 8:16], mx[:, 8:16], -1.0, None, ALU.mult).then_inc(max_made, 1)
            for b, pr in enumerate((probs0, probs1)):
                dve.wait_ge(probs_exp, b + 1)
                c = slice(8 * b, 8 * b + 8)
                link(v.reciprocal(sums[:, c], sums[:, c]))
                v.tensor_tensor(pr, pr, sums[:, c].unsqueeze(2).to_broadcast([P, FOX_HEADS, P * (b + 1)]),
                                ALU.mult).then_inc(probs_made, 1)
            for hd in range(1, FOX_HEADS, 2):
                unit_ready(dve, f"pt{hd}")
                v.tensor_copy(probsT[:, hd], ubank(f"pt{hd}")[:, 0:3 * P]).then_inc(dve_freed, 1)
            for n in range(2):
                unit_ready(dve, f"ms{n}")
                s2 = rsq[:, 2 * n:2 * n + 2]
                v.tensor_scalar(s2, two(ubank(f"ms{n}")), EPS, None, ALU.add).then_inc(dve_freed, 1)
                dve.wait_ge(rseed_made, n + 1)
                y = rseed[:, 2 * n:2 * n + 2]
                link(v.tensor_tensor(s2, s2, y, ALU.mult))
                link(v.tensor_tensor(s2, s2, y, ALU.mult))
                link(v.tensor_scalar(s2, s2, -0.5, 1.5, ALU.mult, ALU.add))
                link(v.tensor_tensor(s2, s2, y, ALU.mult))
                link(v.tensor_tensor(s2, s2, rr[:, 2 * n:2 * n + 2], ALU.mult))
                v.tensor_tensor(roT[:, 2 * n:2 * n + 2], roT[:, 2 * n:2 * n + 2], s2, ALU.mult).then_inc(ro_made, 1)
            unit_saved(dve, "gb3")
            for n in range(4):
                unit_ready(dve, f"pr{n}")
                g1 = gates[:, 8 + 2 * n:10 + 2 * n]
                v.tensor_tensor(g1, g1, two(ubank(f"pr{n}")), ALU.mult).then_inc(dve_freed, 1)
            for n in range(4):
                unit_ready(dve, f"pr{4 + n}")
                g, g1 = gates[:, 2 * n:2 * n + 2], gates[:, 8 + 2 * n:10 + 2 * n]
                link(v.tensor_tensor(g, g, two(ubank(f"pr{4 + n}")), ALU.mult))
                v.tensor_tensor(g, g, g1, ALU.add).then_inc(dve_freed, 1)

            def add_out(n):
                unit_ready(dve, f"out{n}")
                t, c = n // 2, slice(512 * (n % 2), 512 * (n % 2 + 1))
                v.tensor_tensor(h[:, t, c], h[:, t, c], ubank(f"out{n}")[:, :], ALU.add).then_inc(dve_freed, 1)
                unit_saved(dve, f"out{n}")
                if n == 0:
                    dve.wait_ge(ld["gain_ffn"], 16)
                if n == 2:
                    dve.wait_ge(ssq_made, TT + 1)
                v.tensor_tensor(hn[:, t, c], h[:, t, c], gain_ffn[:, c], ALU.mult).then_inc(hn_made, 1)

            add_out(0)
            add_out(1)
            add_out(2)
            unit_ready(dve, "ht1")
            v.tensor_copy(xnT[:, 4:8, tok(0)], ubank("ht1")[:, :].rearrange("p (k n) -> p k n", k=4)).then_inc(dve_freed, 1)
            inverse_rms(slice(0, 1))
            add_out(3)
            dve.wait_ge(ssq_made, 2 * TT)
            inverse_rms(slice(1, 2))
            unit_ready(dve, "rl")
            dve.wait_ge(s_br, 16)
            for t in range(TT):
                last = v.scalar_tensor_tensor(out=lg[:, t], in0=ubank("rl")[:, E * t:E * (t + 1)], scalar=rstd[:, t:t + 1],
                                              in1=brb, op0=ALU.mult, op1=ALU.add)
            last.then_inc(dve_freed, 1)
            unit_saved(dve, "rl")
            for t in range(TT):
                link(v.max(m8[:, t], lg[:, t]))
            v.tensor_scalar(nmax.unsqueeze(2), m8[:, :, 0:1], -1.0, None, ALU.mult).then_inc(top_made, 1)
            thr = m8[:, :, TOP_K - 1:TOP_K].to_broadcast([P, TT, E])
            v.tensor_tensor(gt, lg, thr, ALU.is_gt)
            link(v.tensor_tensor(eq, lg, thr, ALU.is_equal))
            for t in range(TT):
                v.tensor_tensor_scan(cum[:, t], ones[:, 0:E], eq[:, t], 0.0, ALU.mult, ALU.add)
            link(v.reduce_sum(ngt, gt, AX.X))
            link(v.tensor_scalar(ngt, ngt, -1.0, float(TOP_K), ALU.mult, ALU.add))
            link(v.tensor_tensor(cum, cum, ngt.unsqueeze(2).to_broadcast([P, TT, E]), ALU.is_le))
            link(v.tensor_tensor(eq, eq, cum, ALU.mult))
            v.tensor_tensor(sel, gt, eq, ALU.add).then_inc(sel_made, 1)

            def one_hot(o, position, weight):
                for t in range(TT):
                    last = v.tensor_scalar(o[t], iota[:, 0:o[t].shape[-1]], position(t), weight(t),
                                           ALU.is_equal, ALU.mult)
                return last

            def col(table, t, e):
                return table[:, t, bass.ds(e, 1)] if not isinstance(e, int) else table[:, t, e:e + 1]

            def pair_hot(p):
                for half in range(2):
                    s = slice(SLOTS * half, SLOTS * (half + 1))
                    last = one_hot([hot[:, t, s] for t in range(TT)], lambda t: col(posm, t, 2 * p + half),
                                   lambda t: rstd[:, t:t + 1])
                last.then_inc(hot_made, 1)

            def swiglu(psum, dst, clip_sem, done_sem, wait_sigmoid):
                glu, lin = gl[:, 0:256], gl[:, 256:512]
                v.tensor_scalar(glu, psum[:, 0:CHUNK:2], LIMIT, None, ALU.min).then_inc(clip_sem, 1)
                link(v.tensor_scalar(lin, psum[:, 1:CHUNK:2], LIMIT, -LIMIT, ALU.min, ALU.max))
                link(v.scalar_tensor_tensor(out=lin, in0=lin, scalar=1.0, in1=glu, op0=ALU.add, op1=ALU.mult))
                wait_sigmoid()
                v.tensor_tensor(dst, lin, ex, ALU.mult).then_inc(done_sem, 1)

            ident_n = ident.rearrange("p (n e) -> p n e", n=GU)

            def pair_picker(p):
                src = ident_n[:, :, bass.ds(2 * p, 2)] if not isinstance(p, int) else ident_n[:, :, 2 * p:2 * p + 2]
                v.tensor_copy(ind.rearrange("p n (w s) -> p n w s", w=2),
                              src.unsqueeze(3).to_broadcast([P, GU, 2, SLOTS])).then_inc(ind_made, 1)

            def pair(p, first, last):
                if not first:
                    dve.wait_ge(ct_done, p)
                for half in range(2):
                    s = slice(SLOTS * half, SLOTS * (half + 1))
                    ins = one_hot([comb[:, t, s] for t in range(TT)], lambda t: col(posm, t, 2 * p + half),
                                  lambda t: col(wr, t, 2 * p + half))
                ins.then_inc(comb_made, 1)
                if not last:
                    dve.wait_ge(gather_done, 2 * p + 2)
                    pair_hot(p + 1)
                for n in range(GU):
                    dve.wait_ge(gu_done, GU * p + (n + 1))
                    if not (first and n == 0):
                        dve.wait_ge(act_made, GU * p + n)
                    swiglu(bank[4 + n % 2], act[:, 256 * n:256 * (n + 1)], clipped, act_made,
                           lambda: dve.wait_ge(sig_done, GU * p + (n + 1)))
                if not last:
                    pair_picker(p + 1)
                if first:
                    dve.wait_ge(acc_begun, 1)
                save_down(p, 0)
                dve.wait_ge(ct_done, p + 1)
                v.tensor_copy(combT, bank[7][:, 0:T]).then_inc(ct_saved, 1)
                if first:
                    make_jobs()
                save_down(p, 1)

            def save_down(p, n):
                dve.wait_ge(dn_done, DN * p + (n + 1))
                v.tensor_copy(Y[:, CHUNK * n:CHUNK * (n + 1)], bank[5 + n][:, :]).then_inc(y_saved, 1)

            def make_jobs():
                link(v.tensor_tensor_scan(jscan, ones[:, 0:64], jf, 0.0, ALU.mult, ALU.add))
                link(v.tensor_copy(jobf[:, MAX_JOBS:MAX_JOBS + 1], jscan[:, 63:64]))
                link(v.tensor_tensor(jscan, jscan, jf, ALU.mult))
                for j in range(MAX_JOBS):
                    link(v.tensor_scalar(jtmp, jscan, float(j + 1), None, ALU.is_equal))
                    link(v.tensor_tensor(jtmp, jtmp, iota[:, 0:64], ALU.mult))
                    link(v.reduce_sum(jobf[:, j:j + 1], jtmp, AX.X))
                v.tensor_copy(jobs_i[:, :], jobf).then_inc(jobs_made, 1)

            unit_ready(dve, "pos")
            pos = ubank("pos")
            link(v.tensor_tensor(posm, pos[:, 0:2 * E].rearrange("p (t e) -> p t e", t=TT), sel, ALU.mult))
            link(v.tensor_scalar(posm, posm, -1.0, None, ALU.add))
            pair_hot(0)
            for r in range(ROUNDS):
                last = v.tensor_scalar(posq[:, :, :, r], posm, -float(SLOTS + 2 * SLOTS * r), None, ALU.add)
            last.then_inc(dve_freed, 1)
            dve.wait_ge(rexp_made, 2)
            link(v.tensor_tensor(ew, ew, sel, ALU.mult))
            link(v.reduce_sum(ngt, ew, AX.X))
            link(v.reciprocal(ngt, ngt))
            link(v.memset(small[:, 0:2 * P], 0.0))
            link(v.tensor_tensor(wr, ew, ngt.unsqueeze(2).to_broadcast([P, TT, E]), ALU.mult))
            v.tensor_copy(wp[:, :, 0:E], wr).then_inc(w_made, 1)
            pair_picker(0)
            unit_ready(dve, "wt")
            v.tensor_copy(combT, ubank("wt")[:, 0:T])
            for r in range(ROUNDS):
                last = v.tensor_scalar(jf.rearrange("p (e r) -> p e r", r=ROUNDS)[:, :, r], ubank("wt")[:, T:T + E],
                                       float(SLOTS + 2 * SLOTS * r), None, ALU.is_gt)
            last.then_inc(dve_freed, 1)

            pair(0, True, False)
            with dve.Fori(1, PAIRS - 1) as p:
                chain.enter(p, 1, 2 * GU)
                pair(p, False, False)
                chain.leave(PAIRS - 2)
            pair(PAIRS - 1, False, True)

            dve.wait_ge(jobs_made, 1)
            n_jobs = dve.value_load(jobs_i[0:1, MAX_JOBS:MAX_JOBS + 1], min_val=0, max_val=MAX_JOBS)
            with dve.If(n_jobs > 0):
                with dve.Fori(0, MAX_JOBS) as j:
                    with dve.If(j < n_jobs):
                        chain.enter(j, 0, 2 * GU)
                        q = dve.value_load(jobs_i[0:1, bass.ds(j, 1)], min_val=0, max_val=E * ROUNDS - 1)
                        e = dve.snap(q // 2)
                        pe0, act0, dve0 = j * PE_JOB_STEPS + 1, j * ACT_JOB_STEPS, j * DVE_JOB_STEPS
                        dve.wait_ge(job_pe, pe0)
                        posf = posq.rearrange("p t e r -> p t (e r)")
                        one_hot([hot[:, t] for t in range(TT)], lambda t: col(posf, t, q), lambda t: rstd[:, t:t + 1])
                        one_hot([comb[:, t] for t in range(TT)], lambda t: col(posf, t, q),
                                lambda t: col(wr, t, e))
                        v.tensor_copy(ind, ident_n[:, :, bass.ds(e, 1)].to_broadcast([P, GU, P])).then_inc(job_dve, 1)
                        dve.wait_ge(job_pe, pe0 + PE_AT["comb"] + 1)
                        v.tensor_copy(combT, bank[5][:, 0:T]).then_inc(job_dve, 1)
                        for n in range(GU):
                            dve.wait_ge(job_pe, pe0 + PE_AT["gu"] + (n + 1))
                            dve.wait_ge(job_dve, dve0 + DVE_AT["gu"] + 2 * n)
                            swiglu(bank[4 + n % 2], act[:, 256 * n:256 * (n + 1)], job_dve, job_dve,
                                   lambda: dve.wait_ge(job_act, act0 + ACT_AT["sigmoid"] + (n + 1)))
                        for n in range(DN):
                            dve.wait_ge(job_pe, pe0 + PE_AT["down"] + (n + 1))
                            v.tensor_copy(Y[:, CHUNK * n:CHUNK * (n + 1)], bank[4 + n][:, :]).then_inc(job_dve, 1)
                        dve.wait_ge(job_pe, pe0 + PE_JOB_STEPS)
                        v.memset(newton, 0.0)
                        chain.leave(MAX_JOBS)
            chain = Chain(dve, tail_step)
            link = chain.link

            dve.wait_ge(job_pe, 1)
            dve.wait_ge(ld_tail["gain_ple"], 16)

            def add_moe(n):
                t, c = n // 2, slice(512 * (n % 2), 512 * (n % 2 + 1))
                v.tensor_tensor(h[:, t, c], h[:, t, c], bank[n][:, :], ALU.add).then_inc(h2_made, 1)
                dve.wait_ge(h2_made, n + 1)
                v.tensor_tensor(hn3[:, t, c], h[:, t, c], gain_ple[:, c], ALU.mult).then_inc(hn3_made, 1)

            def save_hn3T(t):
                dve.wait_ge(hT_done, 2 * t + 2)
                v.tensor_copy(hn3T[:, 4:8, tok(t)], bank[2 * t + 1][:, :].rearrange("p (k n) -> p k n", k=4)).then_inc(ht_dve, 1)

            add_moe(0)
            add_moe(1)
            add_moe(2)
            save_hn3T(0)
            add_moe(3)
            save_hn3T(1)
            dve.wait_ge(ssq_tail, TT)
            inverse_rms(slice(0, TT), rstd_made, 1)
            for n in range(4):
                t, c = n // 2, slice(512 * (n % 2), 512 * (n % 2 + 1))
                s, o = sig[:, n % 2], h[:, n // 2, c]
                dve.wait_ge(ple_sig, n + 1)
                link(v.tensor_tensor(s, s, bank[PROJ_BANK[n]][:, :], ALU.mult))
                v.tensor_tensor(o, o, s, ALU.add).then_inc(sig_made, 1)
                if n == 0:
                    dve.wait_ge(ld_tail["gain_fin"], 16)
                dve.wait_ge(sig_made, n + 1)
                v.tensor_tensor(hn3[:, t, c], o, gain_fin[:, c], ALU.mult)
                if n % 2:
                    dve.wait_ge(ssq_tail, TT + n + 1)
                    link(v.tensor_tensor(ssq[:, t:t + 1], ssq_half[:, n - 1:n], ssq_half[:, n:n + 1], ALU.add))
                    inverse_rms(slice(t, t + 1), rstd_fin, t + 1)
                    v.tensor_scalar(hn3[:, t, 0:512], hn3[:, t, 0:512], rstd[:, t:t + 1], None, ALU.mult).then_inc(y_dve, 1)

        @block.tensor
        def _(pe):
            mm = nc.tensor.matmul

            def begin(name):
                n = NUMBER[name]
                if n >= 8:
                    unit_saved(pe, UNITS[n - 8][0])
                return ubank(name)

            def transposes(name, pieces):
                b = begin(name)
                for n, piece in enumerate(pieces):
                    last = nc.tensor.transpose(b[:, n * P:(n + 1) * P], piece, ident)
                last.then_inc(unit_done, 1)

            def to_T(name, w, cols, src=None, tiles=KT):
                b = begin(name)
                src = xnT if src is None else src
                for n, c in enumerate(cols):
                    for k in range(tiles):
                        if name == "q0" and n == 0 and k % 2 == 0:
                            unit_saved(pe, f"xt{k // 2}")
                        last = mm(b[:, n * T:(n + 1) * T], w[:, k, c:c + P], src[:, k], start=(k == 0), stop=(k == tiles - 1))
                last.then_inc(unit_done, 1)

            def to_tokens(name, w, t, c, src=None):
                b = begin(name)
                src = xnT if src is None else src
                for k in range(KT):
                    last = mm(b[:, :], src[:, k, tok(t)], w[:, k, c:c + 512], start=(k == 0), stop=(k == KT - 1))
                last.then_inc(unit_done, 1)

            pe.wait_ge(s_cmain, 16)
            pe.wait_ge(xgain_made, TT)
            for n in range(4):
                transposes(f"xt{n}", [xgain[:, t, k * P:(k + 1) * P] for k in (2 * n, 2 * n + 1) for t in range(TT)])
            b = begin("bm")
            pe.wait_ge(s_bias, 16)
            nc.tensor.transpose(b[:, 0:P], bmrows, ident)
            pe.wait_ge(diag_made, TT)
            for t in range(TT):
                last = mm(b[:, P + t * P:P + (t + 1) * P], ones, diag[:, t], start=True, stop=True)
            last.then_inc(unit_done, 1)
            for n in range(2):
                pe.wait_ge(ld[f"q{n}"], 16)
                to_T(f"q{n}", W[0], (2 * P * n, 2 * P * n + P))
            pe.wait_ge(ld["k"], 16)
            for n in range(2):
                to_T(f"k{n}", W[0], (512 + 2 * P * n, 512 + 2 * P * n + P))
            b = begin("ff")
            pe.wait_ge(s_ffw, 16)
            for t in range(TT):
                for k in range(KT):
                    last = mm(b[:, 8 * t:8 * t + 8], xnT[:, k, tok(t)], ffw[:, k], start=(k == 0), stop=(k == KT - 1))
            last.then_inc(unit_done, 1)
            pe.wait_ge(ld["v"], 16)
            for t in range(TT):
                to_tokens(f"v{t}", W[1], t, 0)
            pe.wait_ge(ld["rqk"], 16)
            to_T("rq", W[1], (512, 512 + P))
            to_T("rk", W[1], (512 + 2 * P, 512 + 3 * P))
            pe.wait_ge(ld["rvg"], 16)
            to_tokens("rv0", W[2], 0, 0)
            pe.wait_ge(s_cmix, 16)
            for n, name in enumerate(("rotq", "rotk")):
                b = begin(name)
                unit_saved(pe, ("rq", "rk")[n])
                mm(b[:, :], mix("rot"), rraw[:, n].rearrange("p k n -> p (k n)"), start=True, stop=True).then_inc(unit_done, 1)
            to_tokens("rv1", W[2], 1, 0)
            b = begin("cs")
            pe.wait_ge(lf_made, 1)
            mm(b[:, 0:T], lf[:, 0], tri, start=True, stop=False)
            mm(b[:, P:T], lf[:, 1], tri[:, 0:P], start=False, stop=True).then_inc(unit_done, 1)
            for n in range(2):
                to_T(f"rg{n}", W[2], (512 + 2 * P * n, 512 + 2 * P * n + P))
            pe.wait_ge(rot_made, 2)
            for hd in range(RET_HEADS):
                b = begin(f"rs{hd}")
                mm(b[:, 0:T], rkz[:, hd, 0:P], rqT[:, hd // 2], start=True, stop=True)
                mm(b[:, T:3 * P], rkz[:, hd, P:T], rqT[:, hd // 2, P:T], start=True, stop=True).then_inc(unit_done, 1)
            unit_saved(pe, "cs")
            unit_saved(pe, "q1")
            for n in range(6):
                b = begin(f"fs{n}")
                t, heads, width = (0, range(4 * n, 4 * n + 4), P) if n < 2 else (1, range(2 * n - 4, 2 * n - 2), T)
                for i, hd in enumerate(heads):
                    o = b[:, i * width:(i + 1) * width]
                    mm(o, qT[:, hd // 2, tok(t)], kz[:, hd, 0:width], start=True, stop=False)
                    last = mm(o, L[:, tok(t)], R[:, hd, 0:width], start=False, stop=True)
                last.then_inc(unit_done, 1)
            unit_saved(pe, "rs3")
            unit_saved(pe, "rv1")
            for n in range(2):
                b = begin(f"ro{n}")
                for i in range(2):
                    hd = 2 * n + i
                    c = slice(hd * RET_DV, (hd + 1) * RET_DV)
                    mm(b[:, i * T:(i + 1) * T], rv[:, 0, c], scT[:, hd, 0:T], start=True, stop=False)
                    last = mm(b[:, i * T + P:(i + 1) * T], rv[:, 1, c], scT[:, hd, T:3 * P], start=False, stop=True)
                last.then_inc(unit_done, 1)
            pe.wait_ge(ld["gate0"], 16)
            for n in range(4):
                to_T(f"ga{n}", W[0], (2 * P * n, 2 * P * n + P))
            pe.wait_ge(probs_made, 2)
            for hd in range(FOX_HEADS):
                transposes(f"pt{hd}", [probs0[:, hd], probs1[:, hd, 0:P], probs1[:, hd, P:T]])
            for n in range(2):
                b = begin(f"ms{n}")
                unit_saved(pe, f"ro{n}")
                mm(b[:, :], mix("mean"), rsq[:, 2 * n:2 * n + 2].rearrange("p k n -> p (k n)"), start=True, stop=True).then_inc(unit_done, 1)
            pe.wait_ge(ld["gate1"], 16)
            for n in range(4):
                to_T(f"gb{n}", W[1], (2 * P * n, 2 * P * n + P))
            unit_saved(pe, "pt6")
            unit_saved(pe, "pt7")
            for n in range(2):
                b = begin(f"fo{n}")
                for i in range(2):
                    for t in range(TT):
                        for s in range(2):
                            hd = 2 * (2 * n + i) + s
                            last = mm(b[64 * s:64 * s + 64, i * T + t * P:(i + 1) * T], fv[:, t, FOX_D * hd:FOX_D * (hd + 1)],
                                      probsT[:, hd, t * T:(t + 2) * P], start=(t == 0), stop=(t == 1), skip_group_check=True)
                last.then_inc(unit_done, 1)
            pe.wait_ge(ld["branch"], 16)
            pe.wait_ge(ro_made, 2)
            for n in range(4):
                to_T(f"pr{n}", W[2][:, 4:8], (2 * P * n, 2 * P * n + P), roT, 4)
            unit_saved(pe, "fo1")
            for n in range(4):
                to_T(f"pr{4 + n}", W[2], (2 * P * n, 2 * P * n + P), foxT, 4)
            pe.wait_ge(ld["out"], 16)

            def out_piece(b, n, ks):
                for k in ks:
                    if n == 0 and k % 2 == 0:
                        unit_saved(pe, f"pr{4 + k // 2}")
                    last = mm(b[:, :], gates[:, k, tok(n // 2)], W[3][:, k, 512 * (n % 2):512 * (n % 2 + 1)],
                              start=(k == 0), stop=(k == KT - 1))
                return last

            def h_transposes(n):
                pe.wait_ge(hn_made, n + 1)
                k = 4 * (n % 2)
                transposes(f"ht{n}", [hn[:, n // 2, (k + i) * P:(k + i + 1) * P] for i in range(4)])

            def router_logits(b, t):
                for k in range(KT):
                    last = mm(b[:, E * t:E * (t + 1)], xnT[:, k, tok(t)], wrout[:, k], start=(k == 0), stop=(k == KT - 1))
                return last

            for n in range(3):
                out_piece(begin(f"out{n}"), n, range(KT)).then_inc(unit_done, 1)
            h_transposes(0)
            b = ubank("out3")
            unit_saved(pe, UNITS[NUMBER["out3"] - 8][0])
            out_piece(b, 3, range(4))
            h_transposes(1)
            h_transposes(2)
            out_piece(b, 3, range(4, KT)).then_inc(unit_done, 1)
            unit_saved(pe, "ht0")
            unit_saved(pe, "ht1")
            b = begin("rl")
            pe.wait_ge(s_wrouter, 16)
            router_logits(b, 0)
            h_transposes(3)
            unit_saved(pe, "ht3")
            last = router_logits(b, 1)
            last.then_inc(unit_done, 1)
            b = begin("pos")
            pe.wait_ge(sel_made, 1)
            mm(b[:, 0:E], tri[:, 0:P], sel[:, 0], start=True, stop=True)
            mm(b[:, E:2 * E], ones, sel[:, 0], start=True, stop=False)
            mm(b[:, E:2 * E], tri[:, 0:P], sel[:, 1], start=False, stop=True).then_inc(unit_done, 1)

            def gather(done, banks):
                for n in range(2):
                    for i in range(4):
                        k = 4 * n + i
                        for t in range(TT):
                            last = mm(bank[banks[n]][:, i * P:(i + 1) * P], hn[:, t, k * P:(k + 1) * P], hot[:, t],
                                      start=(t == 0), stop=(t == TT - 1))
                    last.then_inc(done, 1)

            def gate_up(b, n, w, stationary, cols, done):
                for k in range(KT):
                    for half, c in enumerate(cols):
                        mm(b[c, :], stationary[:, k, c], w[half][:, k], start=(k == 0), stop=False, skip_group_check=True)
                for c in cols:
                    last = mm(b[c, :], ind[:, n, c], bgu[:, :], start=False, stop=True, skip_group_check=True)
                last.then_inc(done, 1)

            def down(b, w, cols, done):
                for k in range(FT):
                    for half, c in enumerate(cols):
                        last = mm(b[c, :], actT[:, k, c], w[half][:, k], start=(k == 0), stop=(k == FT - 1), skip_group_check=True)
                last.then_inc(done, 1)

            def comb_transpose(b, done):
                for t in range(TT):
                    last = nc.tensor.transpose(b[:, tok(t)], comb[:, t], ident)
                last.then_inc(done, 1)

            def act_transpose(b, n, done):
                for i in range(4):
                    k = 4 * n + i
                    last = nc.tensor.transpose(b[:, i * P:(i + 1) * P], act[:, k * P:(k + 1) * P], ident)
                last.then_inc(done, 1)

            def scatter(halves=range(DN)):
                for c in halves:
                    for t in range(TT):
                        last = mm(bank[2 * t + c][:, :], combT[:, tok(t)], Y[:, 512 * c:512 * (c + 1)],
                                  start=False, stop=False, skip_group_check=True)
                return last

            def scatter_first(p):
                pe.wait_ge(ct_saved, p + 1)
                pe.wait_ge(y_saved, 2 * p + 1)
                scatter([0])

            def finish_pair(p):
                pe.wait_ge(y_saved, 2 * p + 2)
                return scatter([1])

            AB = [slice(SLOTS * half, SLOTS * (half + 1)) for half in range(2)]

            def pair(p, first, last):
                def gate_up_chunk(n):
                    loads = 4 if n == SPLIT else 2
                    pe.wait_ge(ld_gu[n], 16 * loads * p + 16 * loads)
                    gate_up(bank[4 + n % 2], n, gu_slot[n], xg, AB, gu_done)

                def down_chunk(n):
                    if last and n:
                        pe.wait_ge(ld_last_dn, 32)
                    else:
                        pe.wait_ge(ld_dn, 64 * p + 32 * (n + 1))
                    down(bank[5 + n], gu_slot[2] if last and n else dn_slot, AB, dn_done)

                pe.wait_ge(xg_saved, 2 * p + 2)
                pe.wait_ge(ind_made, p + 1)
                gate_up_chunk(0)
                if not first:
                    pe.wait_ge(y_saved, 2 * p)
                gate_up_chunk(1)
                pe.wait_ge(act_made, GU * p + 1)
                gate_up_chunk(2)
                pe.wait_ge(act_made, GU * p + 2)
                act_transpose(bank[6], 0, at_done)
                gate_up_chunk(3)
                if not first:
                    finish_pair(p - 1)
                pe.wait_ge(at_saved, 2 * p + 1)
                pe.wait_ge(act_made, GU * p + 4)
                act_transpose(bank[6], 1, at_done)
                pe.wait_ge(at_saved, 2 * p + 2)
                down_chunk(0)
                if first:
                    begin_output()
                if not last:
                    pe.wait_ge(hot_made, p + 2)
                    gather(gather_done, (7, 4))
                    pe.wait_ge(xg_saved, 2 * p + 3)
                pe.wait_ge(comb_made, p + 1)
                comb_transpose(bank[7], ct_done)
                if last:
                    pe.wait_ge(ld_tail["p"], 16)
                    for k in range(2):
                        for t in range(TT):
                            ins = nc.tensor.transpose(bank[4][:, k * T + t * P:k * T + (t + 1) * P], prow[:, t, k * P:(k + 1) * P], ident)
                    ins.then_inc(p_transposed, 1)
                scatter_first(p)
                down_chunk(1)

            def begin_output():
                for n in range(len(UNITS) - 8, len(UNITS)):
                    unit_saved(pe, UNITS[n][0])
                pe.wait_ge(ld["b_down"], 16)
                for n in range(4):
                    last = mm(bank[n][:, :], combT[:, tok(n // 2)], bdown[:, 512 * (n % 2):512 * (n % 2 + 1)],
                              start=True, stop=False, skip_group_check=True)
                last.then_inc(acc_begun, 1)

            pe.wait_ge(s_bgu, 16 * GU)
            pe.wait_ge(hot_made, 1)
            unit_saved(pe, "out3")
            unit_saved(pe, "ht0")
            gather(gather_done, (7, 4))
            pe.wait_ge(w_made, 1)
            b = begin("wt")
            for t in range(TT):
                mm(b[:, 2 * P:2 * P + E], ones, sel[:, t], start=(t == 0), stop=(t == TT - 1))
            for t in range(TT):
                last = nc.tensor.transpose(b[:, tok(t)], wp[:, t], ident)
            last.then_inc(unit_done, 1)
            pair(0, True, False)
            with pe.Fori(1, PAIRS - 1) as p:
                pair(p, False, False)
            pair(PAIRS - 1, False, True)
            pe.wait_ge(pT_saved, 1)
            finish_pair(PAIRS - 1).then_inc(job_pe, 1)

            pe.wait_ge(jobs_made, 1)
            n_jobs = pe.value_load(jobs_i[0:1, MAX_JOBS:MAX_JOBS + 1], min_val=0, max_val=MAX_JOBS)
            with pe.If(n_jobs > 0):
                with pe.Fori(0, MAX_JOBS) as j:
                    with pe.If(j < n_jobs):
                        act0, dve0 = j * ACT_JOB_STEPS, j * DVE_JOB_STEPS
                        pe.wait_ge(job_dve, dve0 + 1)
                        gather(job_pe, (7, 4))
                        comb_transpose(bank[5], job_pe)
                        pe.wait_ge(ld_job, j * (16 * (GU + DN)) + 16 * (GU + DN))
                        pe.wait_ge(job_act, act0 + ACT_AT["xg"] + 2)
                        pe.wait_ge(job_dve, dve0 + DVE_AT["comb"] + 1)
                        for n in range(GU):
                            if n >= 2:
                                pe.wait_ge(job_dve, dve0 + DVE_AT["gu"] + 2 * (n - 1))
                            gate_up(bank[4 + n % 2], n, [gu_slot[2 + n // 2][n % 2]], xg, [slice(0, P)], job_pe)
                        pe.wait_ge(job_dve, dve0 + DVE_AT["gu"] + 2 * GU)
                        for n in range(2):
                            act_transpose(bank[6 + n], n, job_pe)
                        pe.wait_ge(job_act, act0 + ACT_JOB_STEPS)
                        for n in range(DN):
                            down(bank[4 + n], [dn_slot[n]], [slice(0, P)], job_pe)
                        pe.wait_ge(job_dve, dve0 + DVE_JOB_STEPS)
                        scatter().then_inc(job_pe, 1)

            def projection(n):
                for k in range(2):
                    last = mm(bank[PROJ_BANK[n]][:, :], pT[:, k, tok(n // 2)], wpp[:, k, 512 * (n % 2):512 * (n % 2 + 1)],
                              start=(k == 0), stop=(k == 1))
                last.then_inc(proj_done, 1)

            def hn3_transposes(n):
                pe.wait_ge(hn3_made, n + 1)
                for i in range(4):
                    k = 4 * (n % 2) + i
                    last = nc.tensor.transpose(bank[n][:, i * P:(i + 1) * P], hn3[:, n // 2, k * P:(k + 1) * P], ident)
                last.then_inc(hT_done, 1)

            pe.wait_ge(ld_tail["ple_proj"], 16)
            for t in range(TT):
                projection(2 * t)
                projection(2 * t + 1)
                hn3_transposes(2 * t)
                hn3_transposes(2 * t + 1)
            for n in range(4):
                pe.wait_ge(ht_act, n // 2 + 1)
                pe.wait_ge(ht_dve, n // 2 + 1)
                pe.wait_ge(ld_tail[f"ple_gate{n % 2}"], 16)
                for k in range(KT):
                    last = mm(bank[n][:, :], hn3T[:, k, tok(n // 2)], W[0][:, k, 512 * (n % 2):512 * (n % 2 + 1)],
                              start=(k == 0), stop=(k == KT - 1))
                last.then_inc(gate_done, 1)


_INS = ["x", "p", "mix_norm", "w_in", "b_forget", "w_branch", "w_merge_gate", "b_merge_gate", "w_out",
        "ffn_norm", "w_router", "b_router", "w_gate_up", "b_gate_up", "w_down", "b_down",
        "ple_norm", "w_ple_gate", "w_ple_proj", "final_norm"]


def kernel(**inputs):
    import concourse.bacc as _bacc
    from concourse.bass_utils import run_bass_kernel_spmd as _run

    nc = _bacc.Bacc("TRN2", target_bir_lowering=False, num_devices=1)
    data = {name: np.ascontiguousarray(inputs[name]) for name in _INS}
    data["t_main"], data["t_mix"] = tables()
    arrays, args = {}, {}
    for name, x in data.items():
        arrays[f"in_{name}"] = x
        args[name] = nc.dram_tensor(f"in_{name}", x.shape, mybir.dt.from_np(x.dtype), kind="ExternalInput").ap()
    out = nc.dram_tensor("out_0", (1, T, D), F32, kind="ExternalOutput").ap()
    build(nc, args, out)
    r = _run(nc, [arrays], core_ids=[0])
    return r.results[0]["out_0"]
```
